# Optimizing a Trainium2 kernel written in Bass

```python
import jax, jax.numpy as jnp
from jax import lax
import numpy as np
import math

D_MODEL = 1024
BATCH = 1
SEQ = 1024
DEPTH = 1

D_MIX = D_MODEL
D_A = D_MIX // 2
D_B = D_MIX - D_A
HEAD_DIM = 64
N_GROUPS_A = D_A // HEAD_DIM
N_GROUPS_B = D_B // HEAD_DIM
K_SHORT = 3
K_CONFORMER = 31
K_FFN = 3
D_FF = 2816
D_IN = 3 * D_A + 2 * D_B
RMS_EPS = 1e-6
LN_EPS = 1e-5


def rmsnorm(x, g):
    xf = x.astype(jnp.float32)
    y = xf * lax.rsqrt(jnp.mean(xf * xf, axis=-1, keepdims=True) + RMS_EPS)
    return (y * g.astype(jnp.float32)).astype(x.dtype)

def layernorm(x, g, b):
    xf = x.astype(jnp.float32)
    mu = jnp.mean(xf, axis=-1, keepdims=True)
    var = jnp.mean(jnp.square(xf - mu), axis=-1, keepdims=True)
    y = (xf - mu) * lax.rsqrt(var + LN_EPS)
    return (y * g.astype(jnp.float32) + b.astype(jnp.float32)).astype(x.dtype)

def dwconv(x, w):
    k, c = w.shape
    rhs = w[:, None, :].astype(x.dtype)
    return lax.conv_general_dilated(
        x, rhs, window_strides=(1,), padding=[(k // 2, k // 2)],
        dimension_numbers=("NWC", "WIO", "NWC"), feature_group_count=c)

def first_inputs(seed: int = 0) -> dict:
    key = jax.random.key(seed)
    ks = jax.random.split(key, 16)
    f32 = jnp.float32

    def nrm(k, shape, scale):
        return jax.random.normal(k, shape, f32) * scale

    return {
        "x": jax.random.normal(ks[0], (BATCH, SEQ, D_MODEL), f32),
        "norm_mix_g": 1.0 + nrm(ks[1], (DEPTH, D_MODEL), 0.05),
        "w_in": nrm(ks[2], (DEPTH, D_MODEL, D_IN), D_MODEL ** -0.5),
        "conv_a_w": nrm(ks[3], (DEPTH, K_SHORT, D_A), K_SHORT ** -0.5),
        "conv_b_w": nrm(ks[4], (DEPTH, K_CONFORMER, D_B), K_CONFORMER ** -0.5),
        "conv_b_b": nrm(ks[5], (DEPTH, D_B), 0.02),
        "ln_b_g": 1.0 + nrm(ks[6], (DEPTH, D_B), 0.05),
        "ln_b_b": nrm(ks[7], (DEPTH, D_B), 0.02),
        "w_out": nrm(ks[8], (DEPTH, D_MIX, D_MODEL), D_MIX ** -0.5),
        "norm_ffn_g": 1.0 + nrm(ks[9], (DEPTH, D_MODEL), 0.05),
        "w_gate": nrm(ks[10], (DEPTH, D_MODEL, D_FF), D_MODEL ** -0.5),
        "w_up": nrm(ks[11], (DEPTH, D_MODEL, D_FF), D_MODEL ** -0.5),
        "conv_ffn_w": nrm(ks[12], (DEPTH, K_FFN, D_FF), K_FFN ** -0.5),
        "w_down": nrm(ks[13], (DEPTH, D_FF, D_MODEL), D_FF ** -0.5),
        "norm_final_g": 1.0 + nrm(ks[14], (D_MODEL,), 0.05),
    }

def first_block(x, norm_mix_g, w_in, conv_a_w, conv_b_w, conv_b_b, ln_b_g, ln_b_b,
              w_out, norm_ffn_g, w_gate, w_up, conv_ffn_w, w_down, norm_final_g):
    for l in range(DEPTH):
        h = rmsnorm(x, norm_mix_g[l])
        z = jnp.einsum("bsd,de->bse", h, w_in[l])
        a_h, a_bg, a_cg, b_val, b_gate = jnp.split(
            z, [D_A, 2 * D_A, 3 * D_A, 3 * D_A + D_B], axis=-1)
        y_a = a_bg * dwconv(a_cg * a_h, conv_a_w[l])
        u = b_val * jax.nn.sigmoid(b_gate)
        u = dwconv(u, conv_b_w[l]) + conv_b_b[l].astype(u.dtype)
        y_b = jax.nn.silu(layernorm(u, ln_b_g[l], ln_b_b[l]))
        y = jnp.concatenate([y_a, y_b], axis=-1)
        x = x + jnp.einsum("bse,ed->bsd", y, w_out[l])

        h = rmsnorm(x, norm_ffn_g[l])
        g = dwconv(jnp.einsum("bsd,df->bsf", h, w_gate[l]), conv_ffn_w[l])
        v = jnp.einsum("bsd,df->bsf", h, w_up[l])
        x = x + jnp.einsum("bsf,fd->bsd", jax.nn.silu(g) * v, w_down[l])

    return rmsnorm(x, norm_final_g)


DEPTH_2 = 2

N_A = DEPTH_2 // 2
N_B = DEPTH_2 - N_A
EXPAND = 2
A_WIDTH = EXPAND * D_MODEL
POOL_WINDOWS = (2, 4, 8, 16)
N_POOL_GROUPS = len(POOL_WINDOWS)
GROUP_WIDTH = A_WIDTH // N_POOL_GROUPS
N_HEADS = D_MODEL // HEAD_DIM
N_KV_HEADS = max(1, N_HEADS // 8)
GQA_GROUPS = N_HEADS // N_KV_HEADS
B_WIDTH = N_HEADS * HEAD_DIM
WINDOW = 128
BLOCK = 128
N_BUCKETS = 32
MAX_DISTANCE = 128
EPS = 1e-6
NEG_INF = -1e30


def rmsnorm_2(x, g):
    xf = x.astype(jnp.float32)
    y = xf * lax.rsqrt(jnp.mean(xf * xf, axis=-1, keepdims=True) + EPS)
    return y.astype(x.dtype) * g

def modulate(h, shift, scale):
    return h * (1 + scale[:, None, :]) + shift[:, None, :]

def t5_causal_buckets():
    i = np.arange(BLOCK)[:, None]
    j = np.arange(2 * BLOCK)[None, :]
    n = np.maximum(i + BLOCK - j, 0)
    max_exact = N_BUCKETS // 2
    large = max_exact + (np.log(np.maximum(n, 1) / max_exact) / math.log(MAX_DISTANCE / max_exact)
                         * (N_BUCKETS - max_exact)).astype(np.int32)
    large = np.minimum(large, N_BUCKETS - 1)
    return np.where(n < max_exact, n, large).astype(np.int32)

def band_mask(n_blocks):
    i = jnp.arange(BLOCK)[:, None]
    j = jnp.arange(2 * BLOCK)[None, :]
    rel = i + BLOCK - j
    band = (rel >= 0) & (rel < WINDOW)
    blk = jnp.arange(n_blocks)[:, None, None]
    return band[None] & ((blk > 0) | (j[None] >= BLOCK))

def causal_multiscale_pool(u):
    S = u.shape[1]
    uf = u.astype(jnp.float32)
    csp = jnp.pad(jnp.cumsum(uf, axis=1), ((0, 0), (1, 0), (0, 0)))
    t = jnp.arange(S)
    outs = []
    for g, w in enumerate(POOL_WINDOWS):
        c_g = csp[..., g * GROUP_WIDTH:(g + 1) * GROUP_WIDTH]
        upper = c_g[:, 1:]
        lower = jnp.pad(c_g, ((0, 0), (w, 0), (0, 0)))[:, 1:S + 1]
        count = jnp.minimum(t + 1, w).astype(jnp.float32)[None, :, None]
        outs.append((upper - lower) / count)
    return (jnp.concatenate(outs, axis=-1) - uf).astype(u.dtype)

def pool_mixer(h, w_in, w_group, scale, w_out):
    B, S, _ = h.shape
    u, z = jnp.split(h @ w_in, 2, axis=-1)
    p = causal_multiscale_pool(u).reshape(B, S, N_POOL_GROUPS, GROUP_WIDTH)
    y = jnp.einsum('bsgc,gcd->bsgd', p, w_group).reshape(B, S, A_WIDTH) * scale
    return (y * jax.nn.silu(z)) @ w_out

def shared_kv_blocks(x, c_act, kv_norm_g, kv_ada_w, kv_ada_b, w_kv):
    B, S, _ = x.shape
    nb = S // BLOCK
    shift, scale = jnp.split(c_act @ kv_ada_w + kv_ada_b, 2, axis=-1)
    hk = modulate(rmsnorm_2(x, kv_norm_g), shift, scale)
    kv = (hk @ w_kv).reshape(B, S, 2, N_KV_HEADS, HEAD_DIM)
    k, v = kv[:, :, 0], kv[:, :, 1]

    def to_band(t):
        prev = jnp.pad(t, ((0, 0), (BLOCK, 0), (0, 0), (0, 0)))[:, :S]
        prev = prev.reshape(B, nb, BLOCK, N_KV_HEADS, HEAD_DIM)
        cur = t.reshape(B, nb, BLOCK, N_KV_HEADS, HEAD_DIM)
        return jnp.concatenate([prev, cur], axis=2).transpose(1, 0, 2, 3, 4)

    return to_band(k), to_band(v)

def swa_sink_mixer(h, kb, vb, pos_bias, mask, w_in, sinks, w_out):
    B, S, _ = h.shape
    nb = S // BLOCK
    q, z = jnp.split(h @ w_in, 2, axis=-1)
    q = q * (HEAD_DIM ** -0.5)
    qb = q.reshape(B, nb, BLOCK, N_KV_HEADS, GQA_GROUPS, HEAD_DIM).transpose(1, 0, 2, 3, 4, 5)
    sink = sinks.astype(jnp.float32).reshape(N_KV_HEADS, GQA_GROUPS)[None, :, :, None, None]

    def block_fn(args):
        qn, kn, vn, mn = args
        s = jnp.einsum('bqhgd,bkhd->bhgqk', qn, kn).astype(jnp.float32) + pos_bias
        s = jnp.where(mn[None, None, None], s, NEG_INF)
        m = jnp.maximum(jnp.max(s, axis=-1, keepdims=True), sink)
        p = jnp.exp(s - m)
        p = p / (jnp.sum(p, axis=-1, keepdims=True) + jnp.exp(sink - m))
        return jnp.einsum('bhgqk,bkhd->bqhgd', p.astype(vn.dtype), vn)

    o = lax.map(block_fn, (qb, kb, vb, mask))
    o = o.transpose(1, 0, 2, 3, 4, 5).reshape(B, S, B_WIDTH)
    return (o * jax.nn.silu(z)) @ w_out

def second_inputs(seed: int = 0) -> dict:
    key = jax.random.key(seed)
    ks = jax.random.split(key, 18)
    D, E, GW = D_MODEL, A_WIDTH, GROUP_WIDTH
    nrm = jax.random.normal
    f32 = jnp.float32
    return {
        "x": nrm(ks[0], (BATCH, SEQ, D), f32),
        "c": nrm(ks[1], (BATCH, D), f32),
        "norm_g": 1.0 + 0.05 * nrm(ks[2], (DEPTH_2, D), f32),
        "ada_w": 0.5 * D ** -0.5 * nrm(ks[3], (DEPTH_2, D, 3 * D), f32),
        "ada_b": 0.02 * nrm(ks[4], (DEPTH_2, 3 * D), f32),
        "a_w_in": D ** -0.5 * nrm(ks[5], (N_A, D, 2 * E), f32),
        "a_w_group": GW ** -0.5 * nrm(ks[6], (N_A, N_POOL_GROUPS, GW, GW), f32),
        "a_scale": 1.0 + 0.1 * nrm(ks[7], (N_A, E), f32),
        "a_w_out": E ** -0.5 * nrm(ks[8], (N_A, E, D), f32),
        "kv_norm_g": 1.0 + 0.05 * nrm(ks[9], (D,), f32),
        "kv_ada_w": 0.5 * D ** -0.5 * nrm(ks[10], (D, 2 * D), f32),
        "kv_ada_b": 0.02 * nrm(ks[11], (2 * D,), f32),
        "w_kv": D ** -0.5 * nrm(ks[12], (D, 2 * N_KV_HEADS * HEAD_DIM), f32),
        "b_w_in": D ** -0.5 * nrm(ks[13], (N_B, D, 2 * B_WIDTH), f32),
        "b_sinks": 0.5 * nrm(ks[14], (N_B, N_HEADS), f32),
        "b_w_out": B_WIDTH ** -0.5 * nrm(ks[15], (N_B, B_WIDTH, D), f32),
        "rel_bias": 0.5 * nrm(ks[16], (N_BUCKETS, N_HEADS), f32),
        "final_g": 1.0 + 0.05 * nrm(ks[17], (D,), f32),
    }

def second_block(x, c, norm_g, ada_w, ada_b, a_w_in, a_w_group, a_scale, a_w_out,
              kv_norm_g, kv_ada_w, kv_ada_b, w_kv, b_w_in, b_sinks, b_w_out,
              rel_bias, final_g):
    S = x.shape[1]
    nb = S // BLOCK
    c_act = jax.nn.silu(c)
    buckets = t5_causal_buckets()
    pos_bias = rel_bias[buckets].astype(jnp.float32).transpose(2, 0, 1)
    pos_bias = pos_bias.reshape(N_KV_HEADS, GQA_GROUPS, BLOCK, 2 * BLOCK)[None]
    mask = band_mask(nb)

    kb = vb = None
    for l in range(DEPTH_2):
        shift, scale, gate = jnp.split(c_act @ ada_w[l] + ada_b[l], 3, axis=-1)
        if l < N_A:
            h = modulate(rmsnorm_2(x, norm_g[l]), shift, scale)
            y = pool_mixer(h, a_w_in[l], a_w_group[l], a_scale[l], a_w_out[l])
        else:
            if l == N_A:
                kb, vb = shared_kv_blocks(x, c_act, kv_norm_g, kv_ada_w, kv_ada_b, w_kv)
            j = l - N_A
            h = modulate(rmsnorm_2(x, norm_g[l]), shift, scale)
            y = swa_sink_mixer(h, kb, vb, pos_bias, mask, b_w_in[j], b_sinks[j], b_w_out[j])
        x = x + gate[:, None, :] * y
    return rmsnorm_2(x, final_g)


def setup_inputs(seed=0):
    out = dict(first_inputs(seed))
    for name, value in second_inputs(seed + 1).items():
        if name != "x":
            out[name + "_2"] = value
    return out


def reference(
    x, norm_mix_g, w_in, conv_a_w, conv_b_w, conv_b_b, ln_b_g, ln_b_b, w_out, norm_ffn_g,
    w_gate, w_up, conv_ffn_w, w_down, norm_final_g, c_2, norm_g_2, ada_w_2, ada_b_2, a_w_in_2,
    a_w_group_2, a_scale_2, a_w_out_2, kv_norm_g_2, kv_ada_w_2, kv_ada_b_2, w_kv_2, b_w_in_2,
    b_sinks_2, b_w_out_2, rel_bias_2, final_g_2,
):
    x = first_block(
        x, norm_mix_g, w_in, conv_a_w, conv_b_w, conv_b_b, ln_b_g, ln_b_b, w_out, norm_ffn_g,
        w_gate, w_up, conv_ffn_w, w_down, norm_final_g,
    )
    return second_block(
        x, c_2, norm_g_2, ada_w_2, ada_b_2, a_w_in_2, a_w_group_2, a_scale_2, a_w_out_2,
        kv_norm_g_2, kv_ada_w_2, kv_ada_b_2, w_kv_2, b_w_in_2, b_sinks_2, b_w_out_2, rel_bias_2,
        final_g_2,
    )


_drawn_inputs = setup_inputs


def setup_inputs(seed=0):
    import zlib

    import numpy as np

    out = dict(_drawn_inputs(seed))
    spreads = {}
    factors = {'conv_b_b': 4.085,
     'ln_b_b': 7.492,
     'norm_g_2': 4.152,
     'ada_b_2': 3.799,
     'a_scale_2': 3.038,
     'kv_norm_g_2': 8.0,
     'kv_ada_b_2': 8.0,
     'b_sinks_2': 64.0,
     'rel_bias_2': 3.25}
    for name, (base, spread) in spreads.items():
        noise = np.random.default_rng([zlib.crc32(name.encode()), seed]).standard_normal(out[name].shape)
        drawn = base * np.exp(spread * noise) if base else spread * noise
        out[name] = __import__('jax').numpy.asarray(drawn.astype(out[name].dtype))
    for name, factor in factors.items():
        out[name] = (out[name] * factor).astype(out[name].dtype)
    return out
```

```python
import math
from contextlib import ExitStack

import concourse.bass as bass
from concourse import mybir

P = 128
D = 1024
S = 1024
HALF = S // 2
KT = D // P
DM = 512
MT = DM // P
DFF = 2816
FT = DFF // P
TAPS = 31
POOL_WINDOWS = (2, 4, 8, 16)
GROUPS = len(POOL_WINDOWS)
HEADS, HD = 16, 64
BLOCK = 128
NB = S // BLOCK
BUCKETS, MAX_DISTANCE = 32, 128
NEG = -1e30
RLEN = 384

VEC = {}
_at = 0
for _name, _n in (("mix_g", KT), ("conv_a", 3 * MT), ("conv_b", TAPS * MT), ("conv_b_b", MT), ("ln_g", MT),
                  ("ln_b", MT), ("ffn_g", KT), ("conv_ffn", 3 * FT), ("fin1_g", KT), ("norm2_g", 2 * KT),
                  ("ada_b", 64), ("a_scale", 16), ("kv_g", KT), ("fin2_g", KT)):
    VEC[_name] = _at
    _at += _n
NVEC = _at
NADA = 64
SHIFT0, SCALE0, GATE0, SHIFT1, SCALE1, GATE1, SHIFTKV, SCALEKV = 0, 8, 16, 24, 32, 40, 48, 56

HEAD_ORDER = [4 * q + o for q in range(HEADS // 4) for o in (0, 2, 1, 3)]

PAIR_PLACES = ([n % 3 for n in range(14)]
               + [2] + [0, 1, 2] * 10 + [0, 1]
               + [0, 1, 2, 0, 1, 2, 1] * GROUPS)
SLAB_PLACE = [2 * p + h for p in PAIR_PLACES for h in (0, 1)]
SLAB_PLACE += [0, 1] + [4]
SLAB_PLACE += [2 * p + h for p in (1, 0, 2, 1, 0, 2, 1, 0, 2, 1, 0, 2) for h in (0, 1)]
NSLAB = len(SLAB_PLACE)
FFN_SLAB, POOL_SLAB, ATT_SLAB = 28, 94, 150
FFN_LOOPS = 10

OUT_TILE = 16 + 24
FFN_TILE = OUT_TILE + 4 * 16
POOL_TILE = FFN_TILE + 4 + 24 * FFN_LOOPS + 20
ATT_TILE = POOL_TILE + 56 * GROUPS
Q_TILE = ATT_TILE + 6
Z_TILE = Q_TILE + 16


def slab_ends():
    ends, t = [], 0

    def products(slabs, crossed=True):
        nonlocal t
        for n in range(slabs):
            ends.append(t + ((3 + n) if crossed else 2 * (n + 1)))
        t += 2 * slabs

    def down():
        nonlocal t
        t += 16
        ends.extend([t, t])

    for _ in range(4):
        products(2)
    products(12, False)
    for _ in range(4):
        down()
    products(2)
    for _ in range(FFN_LOOPS):
        products(2), products(2), down()
    products(2), down()
    for _ in range(GROUPS):
        products(2, False), products(2, False), products(2, False)
        ends.extend([t + 4, t + 4 + 4 + 16 + 4])
        t += 4
        products(2, False)
        t += 16
        downs = [t, t]
        t += 4
        t += 16
        ends.extend(downs + [t, t])
    products(2), products(1, False), products(2)
    products(6, False)
    for n in (0, 0, 1, 0, 1, 0, 1, 1):
        down() if n else products(2, False)
    return ends


SLAB_END = slab_ends()


def refill_after(g, per=0, times=1):
    need = []
    for i in range(times):
        at = g + (per[0] * i if per else 0)
        older = [o for o in range(at) if SLAB_PLACE[o] == SLAB_PLACE[at]]
        need.append((SLAB_END[older[-1]] if older else 0) - (per[1] * i if per else 0))
    return max(need)


def bucket_of(n):
    exact = BUCKETS // 2
    if n < exact:
        return n
    return min(exact + int(math.log(n / exact) / math.log(MAX_DISTANCE / exact) * (BUCKETS - exact)), BUCKETS - 1)


def build(nc, x_in, vec_in, slab_in, ada_in, c_in, rel_in, sink_in, row_scratch, skew_scratch, out):
    f32, f32r = mybir.dt.float32, mybir.dt.float32r
    ACT, ALU, AX = mybir.ActivationFunctionType, mybir.AluOpType, mybir.AxisListType
    root = ExitStack()
    with root:
        def sb(scope, name, shape, dt=f32):
            return scope.enter_context(nc.sbuf_tensor(name, shape, dt))

        def sem(name):
            return root.enter_context(nc.semaphore(name))

        X = sb(root, "stream", [P, KT, S])
        HH = sb(root, "norm_hi", [P, KT, S], f32r)
        HL = sb(root, "norm_lo", [P, KT, S], f32r)
        WH = [sb(root, f"w_hi{n}", [P, 1024], f32r) for n in range(6)]
        WL = [sb(root, f"w_lo{n}", [P, 1024], f32r) for n in range(6)]
        RAW = [sb(root, f"w_raw{n}", [P, 1024]) for n in range(2)]
        vec = sb(root, "vec", [P, NVEC])
        ones = sb(root, "ones", [P, P])
        mods = sb(root, "mods", [P, NADA])
        gains = sb(root, "gains", [P, 3 * KT])
        ada_sum = sb(root, "ada_sum", [P, 6])
        inv_count = sb(root, "inv_count", [P, 16])
        eps = sb(root, "eps", [P, 2])
        zero = sb(root, "zero", [P, 1])
        sinks = sb(root, "sinks", [P, HEADS])
        top = sb(root, "top", [P, 4, 4])
        neg_top = sb(root, "neg_top", [P, 4, 4])
        sink_gap = sb(root, "sink_gap", [P, 4, 4])
        sink_exp = sb(root, "sink_exp", [P, 4, 4])
        total = sb(root, "total", [P, 4, 4])

        with ExitStack() as s:
            MYH = [sb(s, f"mix_y_hi{n}", [P, 2, S], f32r) for n in range(2)]
            MYL = [sb(s, f"mix_y_lo{n}", [P, 2, S], f32r) for n in range(2)]
            UB = [sb(s, f"glu{n}", [P, 1056]) for n in range(5)]
            rel = sb(s, "rel", [HEADS, BUCKETS])
            by_distance = sb(s, "by_distance", [HEADS, RLEN])
        with ExitStack() as s:
            FYH = sb(s, "ffn_y_hi", [P, 2, S], f32r)
            FYL = sb(s, "ffn_y_lo", [P, 2, S], f32r)
            ADA = sb(s, "ada_raw", [P, 6, 1024])
            c_act = sb(s, "c_act", [P, D])
        with ExitStack() as s:
            PH = sb(s, "pooled_hi", [P, 4, S], f32r)
            PL = sb(s, "pooled_lo", [P, 4, S], f32r)
            SZ = sb(s, "pool_gate", [P, 2, S])
            GYH = sb(s, "pool_y_hi", [P, 2, S], f32r)
            GYL = sb(s, "pool_y_lo", [P, 2, S], f32r)
            T = [sb(s, f"temp{n}", [P, 1044]) for n in range(3)]
        with ExitStack() as s:
            Q = sb(s, "q_then_o", [P, KT, S])
            KD = [sb(s, f"keys{n}", [P, S]) for n in range(2)]
            with ExitStack() as s2:
                BIAS = sb(s2, "bias", [P, 8, 2 * BLOCK])
                PB = [sb(s2, f"probs{n}", [P, 4, 2 * BLOCK]) for n in range(4)]
                ident = sb(s2, "ident", [P, P])
            AYH = sb(s, "att_y_hi", [P, 2, S], f32r)
            AYL = sb(s, "att_y_lo", [P, 2, S], f32r)
            AZ = sb(s, "att_gate", [P, 2, S])
        V = [w[:, :].rearrange("p (b c) -> p b c", b=NB) for w in (WH[2], WL[2])]
        PT = [w[:, :].rearrange("p (k h q) -> p k (h q)", k=2, h=4) for w in (WH[3], WL[3])]
        VT = PB[0][:, :, :].rearrange("p a b -> p (a b)")

        psum = root.enter_context(nc.psum_tensor("psum", [P, 8, 512], f32))
        bank = [psum[:, n, :] for n in range(8)]

        vec_ready = sem("vec_ready")
        x_ready = [sem(f"x_ready{n}") for n in range(2)]
        rel_ready, sink_ready = sem("rel_ready"), sem("sink_ready")
        setup_done = sem("setup_done")
        distance_done, rows_out, skew_out, bias_ready = (sem(n) for n in ("distance_done", "rows_out", "skew_out", "bias_ready"))
        raw_ready = [sem(f"raw_ready{n}") for n in range(2)]
        w_hi_done, slab_ready = sem("w_hi_done"), sem("slab_ready")
        tiles = sem("tiles")
        act_read, dve_read = sem("act_read"), sem("dve_read")
        dve_step = sem("dve_step")
        square_done, sum_done, stat_done, root_done, rstd_done = (
            sem(n) for n in ("square_done", "sum_done", "stat_done", "root_done", "rstd_done"))
        norm_done, hi_done, lo_done = sem("norm_done"), sem("hi_done"), sem("lo_done")
        stream_normed = sem("stream_normed")
        glu_done, conv_done = sem("glu_done"), sem("conv_done")
        prod_done, my_done, my_hi, my_lo = sem("prod_done"), sem("my_done"), sem("my_hi"), sem("my_lo")
        ln_sum, ln_centred, ln_square, ln_added, ln_var, ln_root, ln_rstd, ln_scaled, ln_silu = (
            sem(n) for n in ("ln_sum", "ln_centred", "ln_square", "ln_added", "ln_var", "ln_root", "ln_rstd",
                             "ln_scaled", "ln_silu"))
        f_conv, f_silu, f_mul, f_hi, f_lo = (sem(n) for n in ("f_conv", "f_silu", "f_mul", "f_hi", "f_lo"))
        c_loaded, c_ready, ada_loaded, ada_summed, ada_read = (
            sem(n) for n in ("c_loaded", "c_ready", "ada_loaded", "ada_summed", "ada_read"))
        gains_done = sem("gains_done")
        p_done, p_hi, p_lo, gy_hi, gy_lo = (sem(n) for n in ("p_done", "p_hi", "p_lo", "gy_hi", "gy_lo"))
        v_turned, v_hi, v_split, ident_zero, ident_done = (
            sem(n) for n in ("v_turned", "v_hi", "v_split", "ident_zero", "ident_done"))
        scored, biased, gap_done, exp_done, inv_done, normed, turned, turned_hi, turned_split, mixed, o_read = (
            sem(n) for n in ("scored", "biased", "gap_done", "exp_done", "inv_done", "normed", "turned",
                             "turned_hi", "turned_split", "mixed", "o_read"))
        az_done, ay_hi, ay_lo, out_done = sem("az_done"), sem("ay_hi"), sem("ay_lo"), sem("out_done")

        def hs(half):
            return slice(HALF * half, HALF * half + HALF)

        def body(t, half=None):
            return t[:, 16:16 + S] if half is None else t[:, 16 + HALF * half:16 + HALF * half + HALF]

        def slot(n):
            return body(T[(n % 4) // 2], n % 2)

        def v(name, n=0):
            return vec[:, VEC[name] + n:VEC[name] + n + 1]

        MIX, FFN, FIN1, POOL, KV, ATT, FIN2 = range(7)
        STATS_BEFORE = {MIX: 0, FFN: 1, FIN1: 2, POOL: 3, KV: 4, FIN2: 5}
        APPLIED_BEFORE = {MIX: 0, FFN: 16, FIN1: 32, POOL: 32, KV: 48, ATT: 64, FIN2: 80}

        def gain(n, k):
            if n == MIX:
                return v("mix_g", k)
            if n == FFN:
                return v("ffn_g", k)
            if n == FIN1:
                return v("fin1_g", k)
            if n == FIN2:
                return v("fin2_g", k)
            at = KT * {POOL: 0, KV: 1, ATT: 2}[n] + k
            return gains[:, at:at + 1]

        def shift(n, k):
            if n not in (POOL, KV, ATT):
                return None
            at = {POOL: SHIFT0, KV: SHIFTKV, ATT: SHIFT1}[n] + k
            return mods[:, at:at + 1]

        block = root.enter_context(nc.Block())

        @block.sync
        def _(sp):
            sp.dma_start(vec[:, :], vec_in).then_inc(vec_ready, 16)
            for half in range(2):
                sp.dma_start(X[:, :, hs(half)], x_in[:, :, hs(half)]).then_inc(x_ready[half], 16)
            for n in range(2):
                sp.dma_start(RAW[n][:, :], slab_in[n, :, :]).then_inc(raw_ready[n], 16)
            with sp.Fori(1, NSLAB // 2) as i:
                for n in range(2):
                    sp.wait_ge(slab_ready, 2 * i + n - 1)
                    sp.dma_start(RAW[n][:, :], slab_in[2 * i + n, :, :]).then_inc(raw_ready[n], 16)
            if NSLAB % 2:
                sp.wait_ge(slab_ready, NSLAB - 2)
                sp.dma_start(RAW[0][:, :], slab_in[NSLAB - 1, :, :]).then_inc(raw_ready[0], 16)
            for half in range(2):
                for k in range(0, KT, 4):
                    sp.wait_ge(stream_normed, 16 + 8 * half + k + 4)
                    sp.dma_start(out[:, k:k + 4, hs(half)], X[:, k:k + 4, hs(half)]).then_inc(out_done, 16)
            sp.wait_ge(out_done, 64)

        @block.gpsimd
        def _(gp):
            gp.wait_ge(setup_done, 1)

            def split(g, at, place, refill):
                if at >= 6:
                    gp.wait_ge(tiles, refill)
                gp.wait_ge(raw_ready[at % 2], 8 * (g - at % 2) + 16)
                nc.gpsimd.tensor_tensor(WH[place][:, :], RAW[at % 2][:, :], zero[:, :].to_broadcast([P, 1024]),
                                        ALU.add).then_inc(w_hi_done, 1)
                gp.wait_ge(w_hi_done, g + 1)
                nc.gpsimd.tensor_tensor(WL[place][:, :], RAW[at % 2][:, :], WH[place][:, :].bitcast(f32),
                                        ALU.subtract).then_inc(slab_ready, 1)

            def straight(first, last):
                for g in range(first, last):
                    split(g, g, SLAB_PLACE[g], refill_after(g))

            straight(0, FFN_SLAB + 2)
            with gp.Fori(0, FFN_LOOPS) as i:
                for n in range(FFN_SLAB + 2, FFN_SLAB + 8):
                    split(n + 6 * i, n, SLAB_PLACE[n], refill_after(n, (6, 24), FFN_LOOPS) + 24 * i)
            straight(POOL_SLAB - 4, POOL_SLAB)
            with gp.Fori(0, GROUPS) as i:
                for n in range(POOL_SLAB, POOL_SLAB + 14):
                    split(n + 14 * i, n, SLAB_PLACE[n], refill_after(n, (14, 56), GROUPS) + 56 * i)
            straight(ATT_SLAB, ATT_SLAB + 11)
            gp.wait_ge(lo_done, APPLIED_BEFORE[ATT] + 16)
            nc.gpsimd.memset(ident[:, :], 1.0).then_inc(ident_zero, 1)
            gp.wait_ge(ident_zero, 1)
            nc.gpsimd.affine_select(out=ident[:, :], in_=ident[:, :], compare_op=ALU.is_equal, fill=0.0, base=0,
                                    pattern=[[-1, P]], channel_multiplier=1).then_inc(ident_done, 1)
            straight(ATT_SLAB + 11, ATT_SLAB + 15)
            for u in range(32):
                lo = BLOCK if (u % 16) // 2 == 0 else 0
                gp.wait_ge(inv_done, u + 1)
                nc.gpsimd.tensor_tensor(PB[u % 4][:, :, lo:], PB[u % 4][:, :, lo:],
                                        total[:, u % 4, :].unsqueeze(2).to_broadcast([P, 4, 2 * BLOCK - lo]),
                                        ALU.mult).then_inc(normed, 1)
            gp.wait_ge(mixed, 32)
            straight(ATT_SLAB + 15, NSLAB)

        @block.tensor
        def _(pe):
            def products(dst, terms):
                for n, (wh, wl, xh, xl) in enumerate(terms):
                    nc.tensor.matmul(dst, wh, xh, start=n == 0, stop=False)
                    nc.tensor.matmul(dst, wh, xl, start=False, stop=False)
                    last = nc.tensor.matmul(dst, wl, xh, start=False, stop=n == len(terms) - 1)
                return last

            def slab_tile(t, place, half, gate=None):
                terms = []
                for k in range(KT):
                    cols = slice(P * k, P * k + P)
                    terms.append((WH[place][:, cols], WL[place][:, cols], HH[:, k, hs(half)], HL[:, k, hs(half)]))
                if gate is None:
                    products(bank[t % 4], terms).then_inc(tiles, 1)
                    return
                for n, (wh, wl, xh, xl) in enumerate(terms):
                    pe.wait_ge(lo_done, gate + 8 * half + n + 1)
                    nc.tensor.matmul(bank[t % 4], wh, xh, start=n == 0, stop=False)
                    nc.tensor.matmul(bank[t % 4], wh, xl, start=False, stop=False)
                    last = nc.tensor.matmul(bank[t % 4], wl, xh, start=False, stop=n == KT - 1)
                last.then_inc(tiles, 1)

            def freed(j, own, own_base, before):
                if j >= 4:
                    pe.wait_ge(own, own_base + j - 3)
                else:
                    for reader, count in before:
                        pe.wait_ge(reader, count - 3 + j)

            def pair_job(t, g, place, own_base, before, gate=None, crossed=True):
                order = [(0, 0), (1, 0), (0, 1), (1, 1)] if crossed else [(0, 0), (0, 1), (1, 0), (1, 1)]
                for j, (n, half) in enumerate(order):
                    if j == 0:
                        pe.wait_ge(slab_ready, g + 1)
                    if n == 1 and order[j - 1][0] == 0 and j < 3:
                        pe.wait_ge(slab_ready, g + 2)
                    freed(j, act_read, own_base, before)
                    slab_tile(t + j, place + n, half, gate if n == 0 else None)

            def down_job(t, g, place, own_base, before, yh, yl):
                pe.wait_ge(slab_ready, g + 2)
                for j in range(16):
                    half, e = divmod(j, 8)
                    freed(j, dve_read, own_base, before)
                    cols = slice(P * e, P * e + P)
                    products(bank[(t + j) % 4], [(WH[place + r][:, cols], WL[place + r][:, cols],
                                                  yh[:, r, hs(half)], yl[:, r, hs(half)]) for r in range(2)]
                             ).then_inc(tiles, 1)

            def stats(n):
                base = STATS_BEFORE[n]
                for half in range(2):
                    pe.wait_ge(sum_done, 14 * base + 7 * half + 7)
                    nc.tensor.matmul(bank[4 + half], ones[:, :], body(T[2], half), start=True, stop=True
                                     ).then_inc(stat_done, 1)

            pe.wait_ge(setup_done, 1)

            stats(MIX)
            for n in range(4):
                pair_job(4 * n, 2 * n, SLAB_PLACE[2 * n], 4 * n, [(act_read, 4 * n)] if n else [],
                         gate=0 if n == 0 else None)
            for n in range(6):
                pair_job(16 + 4 * n, 8 + 2 * n, SLAB_PLACE[8 + 2 * n], 16 + 4 * n, [(act_read, 16 + 4 * n)],
                         crossed=False)
            for n in range(4):
                pe.wait_ge(my_lo, 4 * n + 4)
                down_job(OUT_TILE + 16 * n, 20 + 2 * n, SLAB_PLACE[20 + 2 * n], 16 * n,
                         [(dve_read, 16 * n)] if n else [(act_read, 40)], MYH[n % 2], MYL[n % 2])
                if n == 0:
                    pe.wait_ge(conv_done, MT)
                    for half in range(2):
                        for j in range(MT):
                            last = nc.tensor.matmul(bank[4 + half], ones[:, :], body(UB[(j + 4) % 5], half),
                                                    start=j == 0, stop=j == MT - 1)
                        last.then_inc(ln_sum, 1)
                if n == 1:
                    for half in range(2):
                        pe.wait_ge(ln_added, 3 * half + 3)
                        nc.tensor.matmul(bank[4 + half], ones[:, :], body(T[2], half), start=True, stop=True
                                         ).then_inc(ln_var, 1)

            stats(FFN)
            pair_job(FFN_TILE, FFN_SLAB, SLAB_PLACE[FFN_SLAB], 40, [(dve_read, 64)], gate=APPLIED_BEFORE[FFN])

            with pe.Fori(0, FFN_LOOPS) as i:
                t, g, a, d = FFN_TILE + 4 + 24 * i, FFN_SLAB + 2 + 6 * i, 44 + 8 * i, 64 + 16 * i
                at = FFN_SLAB + 2
                pair_job_t = FFN_TILE + 4
                for m in range(2):
                    before = [(act_read, 44), (dve_read, d)] if m == 0 else [(act_read, a + 4)]
                    order = [(0, 0), (1, 0), (0, 1), (1, 1)]
                    for j, (n, half) in enumerate(order):
                        if half == 0:
                            pe.wait_ge(slab_ready, g + 2 * m + n + 1)
                        freed(j, act_read, a + 4 * m, before)
                        slab_tile(pair_job_t + 4 * m + j, SLAB_PLACE[at + 2 * m] + n, half)
                pe.wait_ge(f_lo, 2 * i + 2)
                pe.wait_ge(slab_ready, g + 6)
                for j in range(16):
                    half, e = divmod(j, 8)
                    freed(j, dve_read, d, [(act_read, a + 8)])
                    cols = slice(P * e, P * e + P)
                    place = SLAB_PLACE[at + 4]
                    products(bank[(pair_job_t + j) % 4], [(WH[place + r][:, cols], WL[place + r][:, cols],
                                                           FYH[:, r, hs(half)], FYL[:, r, hs(half)])
                                                          for r in range(2)]).then_inc(tiles, 1)
            t, g = POOL_TILE - 20, POOL_SLAB - 4
            pair_job(t, g, SLAB_PLACE[g], 124, [(dve_read, 224)])
            pe.wait_ge(f_lo, FT)
            down_job(t + 4, g + 2, SLAB_PLACE[g + 2], 224, [(act_read, 128)], FYH, FYL)

            stats(FIN1)
            stats(POOL)
            with pe.Fori(0, GROUPS) as i:
                g, a, d = POOL_SLAB + 14 * i, 128 + 16 * i, 240 + 40 * i

                def input_slab(n, j, a0, before):
                    pe.wait_ge(slab_ready, g + n + 1)
                    for half in range(2):
                        if n == 0:
                            pe.wait_ge(lo_done, APPLIED_BEFORE[POOL] + 8 * half + 8)
                        for reader, count in before(half):
                            pe.wait_ge(reader, count)
                        slab_tile(j + half, SLAB_PLACE[POOL_SLAB + n], half)

                for n in range(4):
                    input_slab(n, 2 * n, a, lambda half, n=n: [(dve_read, d - 3 + 2 * n + half)] if n < 2
                               else [(act_read, a + 2 * n + half - 3)])
                for n in range(2):
                    input_slab(4 + n, 8 + 2 * n, a, lambda half, n=n: [(act_read, a + 8 + 2 * n + half - 3)])

                def group_product(j, first, before):
                    place = SLAB_PLACE[POOL_SLAB + 6 + first // 2]
                    for m, (e, half) in enumerate([(0, 0), (1, 0), (0, 1), (1, 1)]):
                        pe.wait_ge(before[0], before[1] - 3 + m)
                        terms = []
                        for k in range(4):
                            cols = slice(256 * k + P * e, 256 * k + P * e + P)
                            terms.append((WH[place][:, cols], WL[place][:, cols], PH[:, k, hs(half)], PL[:, k, hs(half)]))
                        products(bank[(j + m) % 4], terms).then_inc(tiles, 1)

                pe.wait_ge(slab_ready, g + 8)
                pe.wait_ge(p_lo, 4 * i + 4)
                group_product(12, 0, (act_read, a + 12))
                for n in range(2):
                    input_slab(8 + n, 16 + 2 * n, a, lambda half, n=n: [(dve_read, d + 4 - 3 + 2 * n + half)])

                def down(n, j, first):
                    pe.wait_ge(slab_ready, g + n + 2)
                    place = SLAB_PLACE[POOL_SLAB + n]
                    for m in range(16):
                        half, e = divmod(m, 8)
                        if first and m < 4:
                            pe.wait_ge(act_read, a + 16 - 3 + m)
                        else:
                            pe.wait_ge(dve_read, d + (4 if first else 24) + m - 3)
                        cols = slice(P * e, P * e + P)
                        products(bank[(j + m) % 4], [(WH[place + r][:, cols], WL[place + r][:, cols],
                                                      GYH[:, r, hs(half)], GYL[:, r, hs(half)])
                                                     for r in range(2)]).then_inc(tiles, 1)

                pe.wait_ge(gy_lo, 8 * i + 4)
                down(10, 20, True)
                group_product(36, 2, (dve_read, d + 20))
                pe.wait_ge(gy_lo, 8 * i + 8)
                down(12, 40, False)

            stats(KV)
            t, g = ATT_TILE, ATT_SLAB
            pair_job(t, g, SLAB_PLACE[g], 192, [(dve_read, 400)], gate=APPLIED_BEFORE[KV])
            pe.wait_ge(slab_ready, g + 3)
            for half in range(2):
                pe.wait_ge(act_read, 192 + 4 + half - 3)
                slab_tile(t + 4 + half, SLAB_PLACE[g + 2], half)
            t, g = Q_TILE, ATT_SLAB + 3
            for n in range(4):
                pair_job(t + 4 * n, g + 2 * n, SLAB_PLACE[g + 2 * n], 198 + 4 * n, [(act_read, 198 + 4 * n)],
                         gate=APPLIED_BEFORE[ATT] if n == 0 else None, crossed=n == 0)
            pe.wait_ge(ident_done, 1)
            for b in range(NB):
                last = nc.tensor.transpose(bank[4 + b // 4][:, P * (b % 4):P * (b % 4) + P],
                                           VT[:, P * b:P * b + P], ident[:, :])
                if b % 4 == 3:
                    last.then_inc(v_turned, 1)
            pe.wait_ge(v_split, 2)
            pe.wait_ge(act_read, 214)

            def quad(u):
                group, rest = divmod(u, 16)
                blk, quarter = divmod(rest, 2)
                return group, blk, 4 * group + 2 * quarter

            def scores(u):
                group, blk, q_tile = quad(u)
                if u >= 2:
                    pe.wait_ge(biased, u - 1)
                lo = BLOCK if blk == 0 else 0
                keys = slice(BLOCK * blk - BLOCK + lo, BLOCK * blk + BLOCK)
                for pos in range(4):
                    rows = slice(HD * (pos // 2), HD * (pos // 2) + HD)
                    dst = bank[4 + 2 * (u % 2) + pos // 2]
                    last = nc.tensor.matmul(dst[:, 256 * (pos % 2) + lo:256 * (pos % 2) + 256],
                                            Q[rows, q_tile + pos % 2, BLOCK * blk:BLOCK * blk + BLOCK],
                                            KD[group][rows, keys], start=True, stop=True)
                last.then_inc(scored, 1)

            def turn(u):
                _, blk, _ = quad(u)
                pe.wait_ge(normed, u + 1)
                if u:
                    pe.wait_ge(turned_split, u)
                for chunk in range(1 if blk == 0 else 0, 2):
                    for pos in range(4):
                        last = nc.tensor.transpose(bank[chunk][:, P * pos:P * pos + P],
                                                   PB[u % 4][:, pos, BLOCK * chunk:BLOCK * chunk + BLOCK], ident[:, :])
                last.then_inc(turned, 1)

            def mix_values(u):
                _, blk, _ = quad(u)
                pe.wait_ge(turned_split, u + 1)
                if u >= 2:
                    pe.wait_ge(o_read, u - 1)
                terms = []
                for chunk in range(1 if blk == 0 else 0, 2):
                    b = blk - 1 + chunk
                    terms.append((V[0][:, b, :], V[1][:, b, :], PT[0][:, chunk, :], PT[1][:, chunk, :]))
                products(bank[2 + u % 2], terms).then_inc(mixed, 1)

            for u in range(32 + 4):
                if u < 32:
                    scores(u)
                if u >= 4:
                    mix_values(u - 4)
                if 3 <= u < 35:
                    turn(u - 3)

            pe.wait_ge(o_read, 32)
            pe.wait_ge(turned_split, 32)
            t, g, a, d, done = Z_TILE, ATT_SLAB + 11, 214, 400, 0
            before = []
            for is_down in (0, 0, 1, 0, 1, 0, 1, 1):
                if is_down:
                    pe.wait_ge(ay_lo, 2 * done + 2)
                    down_job(t, g, SLAB_PLACE[g], d, before, AYH, AYL)
                    t, d, done, before = t + 16, d + 16, done + 1, [(dve_read, d + 16)]
                else:
                    pair_job(t, g, SLAB_PLACE[g], a, before, crossed=False)
                    t, a, before = t + 4, a + 4, [(act_read, a + 4)]
                g += 2
            stats(FIN2)

        @block.scalar
        def _(act):
            def stats(n, ready):
                base = STATS_BEFORE[n]
                for half in range(2):
                    for k in range(KT):
                        for where, count in ready(half, k):
                            act.wait_ge(where, count)
                        if k >= 4:
                            act.wait_ge(sum_done, 14 * base + 7 * half + k - 4 + (1 if k == 4 else 0))
                        elif half == 1:
                            act.wait_ge(sum_done, 14 * base + k + 4)
                        nc.scalar.activation(slot(k), X[:, k, hs(half)], ACT.Square).then_inc(square_done, 1)

            def roots(n):
                base = STATS_BEFORE[n]
                for half in range(2):
                    act.wait_ge(stat_done, 2 * base + half + 1)
                    nc.scalar.activation(body(T[2], half), bank[4 + half], ACT.Sqrt, bias=eps[:, 0:1], scale=1.0 / D
                                         ).then_inc(root_done, 1)

            def his(n, h_free=None):
                base = APPLIED_BEFORE[n]
                for m in range(16):
                    half, k = divmod(m, 8)
                    if h_free and k == 0:
                        act.wait_ge(tiles, h_free[half])
                    act.wait_ge(norm_done, base + m + 1)
                    if shift(n, k) is None:
                        nc.scalar.copy(HH[:, k, hs(half)], slot(m)).then_inc(hi_done, 1)
                    else:
                        nc.scalar.activation(HH[:, k, hs(half)], slot(m), ACT.Identity, bias=shift(n, k)
                                             ).then_inc(hi_done, 1)

            def read_tile(t, dst, func=ACT.Copy, scale=1.0):
                count, b = t if isinstance(t, tuple) else (t, t % 4)
                act.wait_ge(tiles, count + 1)
                nc.scalar.activation(dst, bank[b], func, scale=scale).then_inc(act_read, 1)

            act.dma_start(rel[:, :], rel_in).then_inc(rel_ready, 16)
            act.dma_start(sinks[:, :], sink_in).then_inc(sink_ready, 16)

            stats(MIX, lambda half, k: [(x_ready[half], 16)] if k == 0 else [])
            act.wait_ge(setup_done, 1)
            roots(MIX)
            his(MIX)
            act.wait_ge(distance_done, 1)
            act.dma_start(row_scratch, by_distance[:, :]).then_inc(rows_out, 16)
            act.wait_ge(lo_done, 16)
            for j in range(MT):
                for half in range(2):
                    if j:
                        act.wait_ge(glu_done, 2 * (j - 1) + half + 1)
                    read_tile(4 * j + 2 * half, body(T[1], half))
                    read_tile(4 * j + 2 * half + 1, body(T[0], half), ACT.Sigmoid)
            act.wait_ge(rows_out, 16)
            act.dma_start(skew_scratch, row_scratch.unsqueeze(1).to_broadcast([HEADS, P, RLEN])).then_inc(skew_out, 16)
            act.wait_ge(glu_done, 2 * MT)
            for j in range(MT):
                t = 16 + 6 * j
                for half in range(2):
                    if j:
                        act.wait_ge(my_lo, 2 * j)
                    read_tile(t + half, body(T[0], half))
                for half in range(2):
                    if j:
                        act.wait_ge(my_done, 2 * j)
                    read_tile(t + 2 + half, body(T[1], half))
                for half in range(2):
                    act.wait_ge(prod_done, 2 * j + half + 1)
                    read_tile(t + 4 + half, body(T[1], half))
                for half in range(2):
                    act.wait_ge(my_done, 2 * j + half + 1)
                    nc.scalar.copy(MYH[j // 2][:, j % 2, hs(half)], body(T[0], half)).then_inc(my_hi, 1)
            for half in range(2):
                for j in range(MT):
                    act.wait_ge(ln_centred, MT * half + j + 1)
                    if half == 0:
                        act.wait_ge(my_lo, 8)
                    else:
                        act.wait_ge(ln_added, 3)
                    nc.scalar.activation(slot(j), body(UB[(j + 4) % 5], half), ACT.Square).then_inc(ln_square, 1)
            for half in range(2):
                act.wait_ge(ln_var, half + 1)
                nc.scalar.activation(body(T[2], half), bank[4 + half], ACT.Sqrt, bias=eps[:, 1:2], scale=1.0 / DM
                                     ).then_inc(ln_root, 1)
            m = 0
            for j in range(MT):
                act.wait_ge(tiles, OUT_TILE + 16 * (1 + j // 2))
                for half in range(2):
                    c = body(UB[(j + 4) % 5], half)
                    act.wait_ge(ln_scaled, m + 1)
                    nc.scalar.activation(c, c, ACT.Silu, bias=v("ln_b", j), scale=v("ln_g", j)).then_inc(ln_silu, 1)
                    act.wait_ge(ln_silu, m + 1)
                    nc.scalar.copy(MYH[j // 2][:, j % 2, hs(half)], c).then_inc(my_hi, 1)
                    m += 1

            stats(FFN, lambda half, k: [(dve_read, 48 + 8 * half + k + 1)])
            roots(FFN)
            his(FFN)
            act.wait_ge(tiles, FFN_TILE)
            act.dma_start(ADA[:, :, :], ada_in[0:6, :, :].rearrange("s p n -> p s n")).then_inc(ada_loaded, 16)
            act.dma_start(c_act[:, :], c_in).then_inc(c_loaded, 16)

            def ffn_tile(f, t, b0, free_slot, place, y_free):
                for n, (T_n, half) in enumerate(((0, 0), (1, 0), (0, 1), (1, 1))):
                    if free_slot:
                        act.wait_ge(f_conv if T_n == 0 else f_mul, f)
                    read_tile((t + n, (b0 + n) % 4), body(T[T_n], half))
                act.wait_ge(f_conv, f + 1)
                nc.scalar.activation(body(T[2]), body(T[2]), ACT.Silu).then_inc(f_silu, 1)
                act.wait_ge(tiles, y_free)
                act.wait_ge(f_mul, f + 1)
                nc.scalar.copy(FYH[:, place, :], body(T[2])).then_inc(f_hi, 1)

            act.wait_ge(lo_done, APPLIED_BEFORE[FFN] + 16)
            ffn_tile(0, FFN_TILE, FFN_TILE, False, 0, FFN_TILE)
            act.wait_ge(c_loaded, 16)
            nc.scalar.activation(c_act[:, :], c_act[:, :], ACT.Silu).then_inc(c_ready, 1)
            with act.Fori(0, FFN_LOOPS) as i:
                t = FFN_TILE + 4 + 24 * i
                ffn_tile(2 * i + 1, t, FFN_TILE + 4, True, 1, t)
                ffn_tile(2 * i + 2, t + 4, FFN_TILE + 8, True, 0, t + 24)
                act.wait_ge(ada_summed, i + 1)
                act.dma_start(ADA[:, :, :], ada_in[bass.ds(6 * i + 6, 6), :, :].rearrange("s p n -> p s n")
                              ).then_inc(ada_loaded, 16)
            ffn_tile(FT - 1, POOL_TILE - 20, POOL_TILE - 20, True, 1, POOL_TILE - 20)

            stats(FIN1, lambda half, k: [(dve_read, 224 + 8 * half + k + 1)])
            roots(FIN1)
            stats(POOL, lambda half, k: [(stream_normed, 8 * half + k + 1)])
            roots(POOL)
            his(POOL)
            act.wait_ge(lo_done, APPLIED_BEFORE[POOL] + 16)
            with act.Fori(0, GROUPS) as g:
                t, d = POOL_TILE + 56 * g, 240 + 40 * g
                for n in range(4):
                    for half in range(2):
                        act.wait_ge(p_done, 4 * g + n + 1)
                        read_tile((t + 2 * n + half, (2 * n + half) % 4), body(T[0], half))
                    act.wait_ge(tiles, t - 16)
                    act.wait_ge(p_done, 4 * g + n + 2)
                    src = T[1]
                    nc.scalar.copy(PH[:, n, :], body(src)).then_inc(p_hi, 1)
                for n in range(2):
                    act.wait_ge(dve_read, d - 16)
                    for half in range(2):
                        read_tile((t + 8 + 2 * n + half, (2 * n + half) % 4), SZ[:, n, hs(half)], ACT.Silu)

                def y_his(first, base, free):
                    act.wait_ge(tiles, free)
                    for m, (e, half) in enumerate(((0, 0), (1, 0), (0, 1), (1, 1))):
                        act.wait_ge(dve_read, base + m + 1)
                        nc.scalar.copy(GYH[:, e, hs(half)], body(T[1 + e], half)).then_inc(gy_hi, 1)

                y_his(0, d, t)
                for n in range(2):
                    act.wait_ge(dve_read, d + 4)
                    for half in range(2):
                        read_tile((t + 16 + 2 * n + half, (2 * n + half) % 4), SZ[:, n, hs(half)], ACT.Silu)
                y_his(2, d + 20, t + 36)

            stats(KV, lambda half, k: [(dve_read, 384 + 8 * half + k + 1)])
            roots(KV)
            his(KV)
            act.wait_ge(tiles, ATT_TILE)
            act.wait_ge(skew_out, 16)
            act.dma_start(BIAS[:, :, :], bass.AP(skew_scratch.tensor, skew_scratch.offset + BLOCK - 1,
                                                 [[RLEN - 1, P], [RLEN * P, 8], [1, 2 * BLOCK]])
                          ).then_inc(bias_ready, 16)
            t = ATT_TILE
            for half in range(2):
                for n in range(2):
                    read_tile(t + 2 * half + n, KD[n][:, hs(half)])
            for half in range(2):
                read_tile(t + 4 + half, VT[:, hs(half)])
            his(ATT, (ATT_TILE + 5, ATT_TILE + 6))
            t = Q_TILE
            for n in range(4):
                for j, (e, half) in enumerate([(0, 0), (1, 0), (0, 1), (1, 1)] if n == 0 else
                                              [(0, 0), (0, 1), (1, 0), (1, 1)]):
                    read_tile(t + 4 * n + j, Q[:, 2 * n + e, hs(half)], scale=HD ** -0.5)
            for n in range(2):
                act.wait_ge(v_turned, n + 1)
                nc.scalar.copy(WH[2][:, 512 * n:512 * n + 512], bank[4 + n]).then_inc(v_hi, 1)

            for u in range(32 + 4):
                if u >= 4:
                    w = u - 4
                    group, rest = divmod(w, 16)
                    blk, quarter = divmod(rest, 2)
                    tile = 4 * group + 2 * quarter
                    act.wait_ge(mixed, w + 1)
                    for side in range(2):
                        rows = slice(HD * side, HD * side + HD)
                        src = bank[2 + w % 2][HD * group:HD * group + HD, 2 * BLOCK * side:2 * BLOCK * side + 2 * BLOCK]
                        ins = nc.scalar.copy(Q[rows, tile:tile + 2, BLOCK * blk:BLOCK * blk + BLOCK],
                                             src.rearrange("p (a b) -> p a b", a=2))
                    ins.then_inc(o_read, 1)
                if 3 <= u < 35:
                    w = u - 3
                    lo = 1 if (w % 16) // 2 == 0 else 0
                    act.wait_ge(turned, w + 1)
                    if w:
                        act.wait_ge(mixed, w)
                    nc.scalar.copy(PT[0][:, lo:2, :], psum[:, lo:2, :]).then_inc(turned_hi, 1)
                if u < 32:
                    lo = BLOCK if (u % 16) // 2 == 0 else 0
                    act.wait_ge(gap_done, u + 1)
                    for pos in range(4):
                        nc.scalar.activation(PB[u % 4][:, pos, lo:], PB[u % 4][:, pos, lo:], ACT.Exp,
                                             bias=neg_top[:, u % 4, pos:pos + 1],
                                             accum_out=total[:, u % 4, pos:pos + 1])
                    nc.scalar.activation(sink_exp[:, u % 4, :], sink_gap[:, u % 4, :], ACT.Exp).then_inc(exp_done, 1)
                if u == 15:
                    act.wait_ge(biased, 16)
                    act.dma_start(BIAS[:, :, :], bass.AP(skew_scratch.tensor,
                                                         skew_scratch.offset + 8 * RLEN * P + BLOCK - 1,
                                                         [[RLEN - 1, P], [RLEN * P, 8], [1, 2 * BLOCK]])
                                  ).then_inc(bias_ready, 16)

            act.wait_ge(o_read, 32)
            t, ends = Z_TILE, []
            for n in range(4):
                for e in range(2):
                    if n:
                        act.wait_ge(az_done, 2 * n - 1 + e)
                    for half in range(2):
                        read_tile(t + 2 * e + half, AZ[:, e, hs(half)], ACT.Silu)
                if n:
                    act.wait_ge(tiles, Z_TILE + 8 + 16 + 20 * (n - 1))
                for e in range(2):
                    act.wait_ge(az_done, 2 * n + e + 1)
                    nc.scalar.copy(AYH[:, e, :], Q[:, 2 * n + e, :]).then_inc(ay_hi, 1)
                t += 4 if n == 0 else 20
            act.wait_ge(tiles, Z_TILE + 80)
            stats(FIN2, lambda half, k: [(dve_read, 448 + 8 * half + k + 1)])
            roots(FIN2)

        @block.vector
        def _(dve):
            steps = [0]

            def step(ins):
                steps[0] += 1
                ins.then_inc(dve_step, 1)
                dve.wait_ge(dve_step, steps[0])

            def sums(n):
                base = STATS_BEFORE[n]
                for half in range(2):
                    dst = body(T[2], half)
                    if n == POOL:
                        dve.wait_ge(stream_normed, 8 * half + 8)
                    for k in range(1, KT):
                        dve.wait_ge(square_done, 16 * base + 8 * half + k + 1)
                        if k > 1:
                            dve.wait_ge(sum_done, 14 * base + 7 * half + k - 1)
                        nc.vector.tensor_tensor(dst, slot(0) if k == 1 else dst, slot(k), ALU.add).then_inc(sum_done, 1)

            def rstds(n):
                base = STATS_BEFORE[n]
                for half in range(2):
                    dve.wait_ge(root_done, 2 * base + half + 1)
                    dst = body(T[2], half)
                    nc.vector.reciprocal(dst, dst).then_inc(rstd_done, 1)

            def apply(n):
                base = APPLIED_BEFORE[n]
                stat = 2 * STATS_BEFORE[KV if n == ATT else n]

                def lo(m):
                    half, k = divmod(m, 8)
                    dve.wait_ge(hi_done, base + m + 1)
                    src = slot(m)
                    if shift(n, k) is None:
                        ins = nc.vector.tensor_tensor(HL[:, k, hs(half)], src, HH[:, k, hs(half)].bitcast(f32), ALU.subtract)
                    else:
                        ins = nc.vector.scalar_tensor_tensor(HL[:, k, hs(half)], src, shift(n, k),
                                                             HH[:, k, hs(half)].bitcast(f32), ALU.add, ALU.subtract)
                    ins.then_inc(lo_done, 1)

                for m in range(16):
                    half, k = divmod(m, 8)
                    if k == 0:
                        dve.wait_ge(rstd_done, stat + half + 1)
                    if m >= 4 or n == ATT:
                        dve.wait_ge(lo_done, base + m - 3)
                    nc.vector.scalar_tensor_tensor(slot(m), X[:, k, hs(half)], gain(n, k), body(T[2], half),
                                                   ALU.mult, ALU.mult).then_inc(norm_done, 1)
                    if m:
                        lo(m - 1)
                lo(15)

            def norm_stream(n, count):
                for m in range(16):
                    half, k = divmod(m, 8)
                    if k == 0:
                        dve.wait_ge(rstd_done, 2 * STATS_BEFORE[n] + half + 1)
                    piece = X[:, k, hs(half)]
                    nc.vector.scalar_tensor_tensor(piece, piece, gain(n, k), body(T[2], half), ALU.mult, ALU.mult
                                                   ).then_inc(stream_normed, 1)

            def add_down(t, b0, d, gate=None):
                dve.wait_ge(dve_read, d)
                for j in range(16):
                    half, e = divmod(j, 8)
                    dve.wait_ge(tiles, t + j + 1)
                    piece = X[:, e, hs(half)]
                    src = bank[(b0 + j) % 4]
                    if gate is None:
                        ins = nc.vector.tensor_tensor(piece, src, piece, ALU.add)
                    else:
                        ins = nc.vector.scalar_tensor_tensor(piece, src, mods[:, gate + e:gate + e + 1], piece,
                                                             ALU.mult, ALU.add)
                    ins.then_inc(dve_read, 1)

            dve.sem_inc(ada_read, 1)
            dve.sem_inc(p_done, 1)
            step(nc.vector.memset(zero[:, :], 0.0))
            nc.vector.memset(ones[:, :], 1.0)
            nc.vector.memset(eps[:, 0:1], 1e-6)
            nc.vector.memset(eps[:, 1:2], 1e-5).then_inc(setup_done, 1)
            for n in range(15):
                nc.vector.memset(inv_count[:, n:n + 1], 1.0 / (n + 1))
            for buf in T:
                nc.vector.memset(buf[:, 0:16], 0.0)
                nc.vector.memset(buf[:, 16 + S:], 0.0)
            for buf in UB:
                nc.vector.memset(buf[:, 0:16], 0.0)
                nc.vector.memset(buf[:, 16 + S:], 0.0)
            step(nc.vector.memset(by_distance[:, :], NEG))
            dve.wait_ge(rel_ready, 16)
            first = 0
            for n in range(1, BLOCK + 1):
                if n == BLOCK or bucket_of(n) != bucket_of(first):
                    b = bucket_of(first)
                    last = nc.vector.tensor_copy(by_distance[:, 2 * BLOCK - n:2 * BLOCK - first],
                                                 rel[:, b:b + 1].to_broadcast([HEADS, n - first]))
                    first = n
            last.then_inc(distance_done, 1)

            sums(MIX)
            rstds(MIX)
            dve.wait_ge(vec_ready, 16)
            apply(MIX)

            def conv_taps(j, first, last):
                u, c = UB[j], body(UB[(j + 4) % 5])
                for tap in range(first, last):
                    w = v("conv_b", TAPS * j + tap)
                    window = u[:, 1 + tap:1 + tap + S]
                    if tap == 0:
                        dve.wait_ge(glu_done, 2 * j + 2)
                        if j:
                            dve.wait_ge(conv_done, j)
                        step(nc.vector.tensor_scalar(c, window, w, v("conv_b_b", j), ALU.mult, ALU.add))
                    else:
                        ins = nc.vector.scalar_tensor_tensor(c, window, w, c, ALU.mult, ALU.add)
                        if tap == TAPS - 1:
                            ins.then_inc(conv_done, 1)
                        else:
                            step(ins)

            for j in range(MT):
                for half in range(2):
                    dve.wait_ge(act_read, 4 * j + 2 * half + 2)
                    nc.vector.tensor_tensor(body(UB[j], half), body(T[1], half), body(T[0], half), ALU.mult
                                            ).then_inc(glu_done, 1)
                for piece in {1: [(0, 0, 14)], 2: [(0, 14, 28)], 3: [(0, 28, 31), (1, 0, 8)]}.get(j, []):
                    conv_taps(*piece)
            conv_turns = [(1, 8, 14), (1, 14, 20), (1, 20, 26), (1, 26, 31), (2, 0, 7), (2, 7, 14), (2, 14, 21),
                          (2, 21, 28), (2, 28, 31), (3, 0, 6), (3, 6, 12), (3, 12, 18)]
            for j in range(MT):
                conv_taps(*conv_turns[3 * j])
                for half in range(2):
                    dve.wait_ge(act_read, 16 + 6 * j + 3 + half)
                    nc.vector.tensor_tensor(body(T[2], half), body(T[0], half), body(T[1], half), ALU.mult
                                            ).then_inc(prod_done, 1)
                conv_taps(*conv_turns[3 * j + 1])
                dve.wait_ge(prod_done, 2 * j + 2)
                step(nc.vector.tensor_scalar(body(T[0]), T[2][:, 15:15 + S], v("conv_a", 3 * j), None, ALU.mult))
                step(nc.vector.scalar_tensor_tensor(body(T[0]), T[2][:, 16:16 + S], v("conv_a", 3 * j + 1), body(T[0]),
                                                    ALU.mult, ALU.add))
                step(nc.vector.scalar_tensor_tensor(body(T[0]), T[2][:, 17:17 + S], v("conv_a", 3 * j + 2), body(T[0]),
                                                    ALU.mult, ALU.add))
                for half in range(2):
                    dve.wait_ge(act_read, 16 + 6 * j + 5 + half)
                    piece = body(T[0], half)
                    nc.vector.tensor_tensor(piece, piece, body(T[1], half), ALU.mult).then_inc(my_done, 1)
                for half in range(2):
                    dve.wait_ge(my_hi, 2 * j + half + 1)
                    nc.vector.tensor_tensor(MYL[j // 2][:, j % 2, hs(half)], body(T[0], half),
                                            MYH[j // 2][:, j % 2, hs(half)].bitcast(f32), ALU.subtract).then_inc(my_lo, 1)
                conv_taps(*conv_turns[3 * j + 2])
            conv_taps(3, 18, TAPS)
            dve.wait_ge(x_ready[0], 16)
            dve.wait_ge(x_ready[1], 16)

            def add_out(n):
                if n:
                    dve.wait_ge(dve_read, 16 * n)
                for m in range(16):
                    half, e = divmod(m, 8)
                    dve.wait_ge(tiles, OUT_TILE + 16 * n + m + 1)
                    piece = X[:, e, hs(half)]
                    nc.vector.tensor_tensor(piece, bank[(OUT_TILE + m) % 4], piece, ALU.add).then_inc(dve_read, 1)

            add_out(0)
            dve.wait_ge(conv_done, MT)
            for half in range(2):
                dve.wait_ge(ln_sum, half + 1)
                for j in range(MT):
                    c = body(UB[(j + 4) % 5], half)
                    nc.vector.scalar_tensor_tensor(c, bank[4 + half], -1.0 / DM, c, ALU.mult, ALU.add).then_inc(ln_centred, 1)
            for half in range(2):
                dst = body(T[2], half)
                for j in range(1, MT):
                    dve.wait_ge(ln_square, MT * half + j + 1)
                    if j > 1:
                        dve.wait_ge(ln_added, 3 * half + j - 1)
                    nc.vector.tensor_tensor(dst, slot(0) if j == 1 else dst, slot(j), ALU.add).then_inc(ln_added, 1)
            add_out(1)
            for half in range(2):
                dve.wait_ge(ln_root, half + 1)
                nc.vector.reciprocal(body(T[2], half), body(T[2], half)).then_inc(ln_rstd, 1)
            for m in range(2 * MT):
                j, half = divmod(m, 2)
                dve.wait_ge(ln_rstd, half + 1)
                c = body(UB[(j + 4) % 5], half)
                nc.vector.tensor_tensor(c, c, body(T[2], half), ALU.mult).then_inc(ln_scaled, 1)
            for m in range(2 * MT):
                j, half = divmod(m, 2)
                dve.wait_ge(my_hi, 8 + m + 1)
                nc.vector.tensor_tensor(MYL[j // 2][:, j % 2, hs(half)], body(UB[(j + 4) % 5], half),
                                        MYH[j // 2][:, j % 2, hs(half)].bitcast(f32), ALU.subtract).then_inc(my_lo, 1)
            add_out(2)
            add_out(3)

            sums(FFN)
            rstds(FFN)
            apply(FFN)

            def ffn_conv(f, a, first_step, taps, free=True):
                if free:
                    dve.wait_ge(f_lo, f)
                dve.wait_ge(act_read, a + 3)
                ins = nc.vector.tensor_scalar(body(T[2]), T[0][:, 15:15 + S], taps(0), None, ALU.mult)
                ins.then_inc(dve_step, 1)
                dve.wait_ge(dve_step, first_step + 1)
                ins = nc.vector.scalar_tensor_tensor(body(T[2]), T[0][:, 16:16 + S], taps(1), body(T[2]), ALU.mult, ALU.add)
                ins.then_inc(dve_step, 1)
                dve.wait_ge(dve_step, first_step + 2)
                nc.vector.scalar_tensor_tensor(body(T[2]), T[0][:, 17:17 + S], taps(2), body(T[2]), ALU.mult, ALU.add
                                               ).then_inc(f_conv, 1)
                dve.wait_ge(f_silu, f + 1)
                dve.wait_ge(act_read, a + 4)
                nc.vector.tensor_tensor(body(T[2]), body(T[2]), body(T[1]), ALU.mult).then_inc(f_mul, 1)

            def ffn_lo(f, place):
                dve.wait_ge(f_hi, f + 1)
                nc.vector.tensor_tensor(FYL[:, place, :], body(T[2]), FYH[:, place, :].bitcast(f32), ALU.subtract
                                        ).then_inc(f_lo, 1)

            def ffn_w(f):
                return lambda n: v("conv_ffn", 3 * f + n)

            def ada_products(turn, first, last, final):
                if first == 0:
                    dve.wait_ge(ada_loaded, 16 * turn + 16)
                    dve.wait_ge(ada_read, turn + 1)
                for n in range(first, last):
                    ins = nc.vector.tensor_tensor_reduce(out=ADA[:, n, :], in0=ADA[:, n, :], in1=c_act[:, :], scale=1.0,
                                                         scalar=0.0, op0=ALU.mult, op1=ALU.add,
                                                         accum_out=ada_sum[:, n:n + 1])
                if final:
                    ins.then_inc(ada_summed, 1)

            ffn_conv(0, 40, steps[0], ffn_w(0), False)
            ffn_lo(0, 0)
            dve.wait_ge(c_ready, 1)
            base = steps[0] + 2
            with dve.Fori(0, FFN_LOOPS) as i:
                a = 44 + 8 * i

                def loop_w(odd):
                    return lambda n: vec[:, bass.ds(VEC["conv_ffn"] + 3 + 3 * odd + n + 6 * i, 1)]

                ffn_conv(2 * i + 1, a, base + 4 * i, loop_w(0))
                ffn_lo(2 * i + 1, 1)
                ada_products(i, 0, 3, False)
                ffn_conv(2 * i + 2, a + 4, base + 4 * i + 2, loop_w(1))
                add_down(FFN_TILE + 12 + 24 * i, FFN_TILE, 64 + 16 * i)
                ffn_lo(2 * i + 2, 0)
                ada_products(i, 3, 6, True)
                dve.wait_ge(ada_summed, i + 1)
                nc.vector.tensor_tensor(mods[:, bass.ds(6 * i, 6)], ada_sum[:, :],
                                        vec[:, bass.ds(VEC["ada_b"] + 6 * i, 6)], ALU.add).then_inc(ada_read, 1)
            steps[0] = base + 4 * FFN_LOOPS
            ffn_conv(FT - 1, 124, steps[0], ffn_w(FT - 1))
            steps[0] += 2
            ffn_lo(FT - 1, 1)
            n = 6 * FFN_LOOPS
            ada_products(FFN_LOOPS, 0, NADA - n, True)
            dve.wait_ge(ada_summed, FFN_LOOPS + 1)
            nc.vector.tensor_tensor(mods[:, n:], ada_sum[:, 0:NADA - n], vec[:, VEC["ada_b"] + n:VEC["ada_b"] + NADA],
                                    ALU.add).then_inc(ada_read, 1)
            dve.wait_ge(ada_read, FFN_LOOPS + 2)
            for at, scale, base_col in ((0, SCALE0, VEC["norm2_g"]), (KT, SCALEKV, VEC["kv_g"]),
                                        (2 * KT, SCALE1, VEC["norm2_g"] + KT)):
                nc.vector.scalar_tensor_tensor(gains[:, at:at + KT], mods[:, scale:scale + KT], 1.0,
                                               vec[:, base_col:base_col + KT], ALU.add, ALU.mult).then_inc(gains_done, 1)
            add_down(POOL_TILE - 16, POOL_TILE, 224)

            sums(FIN1)
            rstds(FIN1)
            norm_stream(FIN1, 16)
            sums(POOL)
            rstds(POOL)
            dve.wait_ge(gains_done, 3)
            apply(POOL)
            dve.wait_ge(stream_normed, 16)
            for g in range(GROUPS):
                w = POOL_WINDOWS[g]
                t, a, d = POOL_TILE + 56 * g, 128 + 16 * g, 240 + 40 * g
                for n in range(4):
                    dve.wait_ge(act_read, a + 2 * n + 2)
                    if n:
                        dve.wait_ge(p_lo, 4 * g + n)
                    elif g:
                        dve.wait_ge(gy_lo, 8 * g)
                    order = [1, 2, 1, 2] if g % 2 else [2, 1, 2]
                    src, width = 0, 1
                    for m in range(g + 1):
                        dst = order[m]
                        step(nc.vector.tensor_tensor(body(T[dst]), body(T[src]), T[src][:, 16 - width:16 - width + S],
                                                     ALU.add))
                        src, width = dst, 2 * width
                    edge = w - 1
                    step(nc.vector.scalar_tensor_tensor(T[1][:, 16:16 + S], T[src][:, 16:16 + S], 1.0 / w,
                                                        T[0][:, 16:16 + S], ALU.mult, ALU.subtract))
                    step(nc.vector.tensor_tensor(T[1][:, 16:16 + edge], T[src][:, 16:16 + edge], inv_count[:, 0:edge],
                                                 ALU.mult))
                    nc.vector.tensor_tensor(T[1][:, 16:16 + edge], T[1][:, 16:16 + edge], T[0][:, 16:16 + edge],
                                            ALU.subtract).then_inc(p_done, 1)
                    dve.wait_ge(p_hi, 4 * g + n + 1)
                    nc.vector.tensor_tensor(PL[:, n, :], body(T[1]), PH[:, n, :].bitcast(f32), ALU.subtract
                                            ).then_inc(p_lo, 1)

                def group_y(first, t0, gates_read, d0):
                    for m, (e, half) in enumerate(((0, 0), (1, 0), (0, 1), (1, 1))):
                        dve.wait_ge(tiles, t0 + m + 1)
                        dve.wait_ge(act_read, gates_read)
                        nc.vector.scalar_tensor_tensor(body(T[1 + e], half), bank[m], v("a_scale", 4 * g + first + e),
                                                       SZ[:, e, hs(half)], ALU.mult, ALU.mult).then_inc(dve_read, 1)
                    for m, (e, half) in enumerate(((0, 0), (1, 0), (0, 1), (1, 1))):
                        dve.wait_ge(gy_hi, 8 * g + 2 * first + m + 1)
                        nc.vector.tensor_tensor(GYL[:, e, hs(half)], body(T[1 + e], half),
                                                GYH[:, e, hs(half)].bitcast(f32), ALU.subtract).then_inc(gy_lo, 1)

                group_y(0, t + 12, a + 12, d)
                add_down(t + 20, 0, d + 4, GATE0)
                group_y(2, t + 36, a + 16, d + 20)
                add_down(t + 40, 0, d + 24, GATE0)

            sums(KV)
            rstds(KV)
            apply(KV)
            apply(ATT)

            for n in range(2):
                dve.wait_ge(v_hi, n + 1)
                cols = slice(512 * n, 512 * n + 512)
                nc.vector.tensor_tensor(WL[2][:, cols], bank[4 + n], WH[2][:, cols].bitcast(f32), ALU.subtract
                                        ).then_inc(v_split, 1)
            dve.wait_ge(sink_ready, 16)

            def soften(u):
                group, rest = divmod(u, 16)
                blk, quarter = divmod(rest, 2)
                r, lo = u % 4, BLOCK if blk == 0 else 0
                if rest == 0:
                    dve.wait_ge(bias_ready, 16 * group + 16)
                dve.wait_ge(scored, u + 1)
                if u >= 4:
                    dve.wait_ge(turned, u - 3)
                scores = psum[:, 4 + 2 * (u % 2):6 + 2 * (u % 2), :].rearrange("p a (b c) -> p (a b) c", b=2)
                nc.vector.tensor_tensor(PB[r][:, :, lo:], scores[:, :, lo:], BIAS[:, 4 * quarter:4 * quarter + 4, lo:],
                                        ALU.add).then_inc(biased, 1)
                dve.wait_ge(biased, u + 1)
                step(nc.vector.tensor_reduce(top[:, r, :], PB[r][:, :, lo:], AX.X, ALU.max))
                sink = sinks[:, 8 * group + 4 * quarter:8 * group + 4 * quarter + 4]
                step(nc.vector.tensor_tensor(top[:, r, :], top[:, r, :], sink, ALU.max))
                nc.vector.tensor_scalar(neg_top[:, r, :], top[:, r, :], -1.0, None, ALU.mult)
                nc.vector.tensor_tensor(sink_gap[:, r, :], sink, top[:, r, :], ALU.subtract).then_inc(gap_done, 1)

            for u in range(32 + 3):
                if u < 32:
                    soften(u)
                if 1 <= u < 33:
                    r = (u - 1) % 4
                    dve.wait_ge(exp_done, u)
                    step(nc.vector.tensor_tensor(total[:, r, :], total[:, r, :], sink_exp[:, r, :], ALU.add))
                    nc.vector.reciprocal(total[:, r, :], total[:, r, :]).then_inc(inv_done, 1)
                if u >= 3:
                    w = u - 3
                    lo = 1 if (w % 16) // 2 == 0 else 0
                    dve.wait_ge(turned_hi, w + 1)
                    nc.vector.tensor_tensor(PT[1][:, lo:2, :], psum[:, lo:2, :], PT[0][:, lo:2, :].bitcast(f32),
                                            ALU.subtract).then_inc(turned_split, 1)

            dve.wait_ge(o_read, 32)
            t, d = Z_TILE, 400

            def gated(n):
                for e in range(2):
                    dve.wait_ge(act_read, 214 + 4 * n + 2 * e + 2)
                    nc.vector.tensor_tensor(Q[:, 2 * n + e, :], Q[:, 2 * n + e, :], AZ[:, e, :], ALU.mult).then_inc(az_done, 1)

            def gated_lo(n):
                for e in range(2):
                    dve.wait_ge(ay_hi, 2 * n + e + 1)
                    nc.vector.tensor_tensor(AYL[:, e, :], Q[:, 2 * n + e, :], AYH[:, e, :].bitcast(f32), ALU.subtract
                                            ).then_inc(ay_lo, 1)

            gated(0)
            gated_lo(0)
            for n in range(1, 4):
                gated(n)
                first = Z_TILE + 8 + 20 * (n - 1)
                add_down(first, first, 400 + 16 * (n - 1), GATE1)
                gated_lo(n)
            add_down(Z_TILE + 64, Z_TILE + 64, 448, GATE1)
            sums(FIN2)
            rstds(FIN2)
            norm_stream(FIN2, 32)


def kernel(x, norm_mix_g, w_in, conv_a_w, conv_b_w, conv_b_b, ln_b_g, ln_b_b, w_out, norm_ffn_g, w_gate, w_up,
           conv_ffn_w, w_down, norm_final_g, c_2, norm_g_2, ada_w_2, ada_b_2, a_w_in_2, a_w_group_2, a_scale_2,
           a_w_out_2, kv_norm_g_2, kv_ada_w_2, kv_ada_b_2, w_kv_2, b_w_in_2, b_sinks_2, b_w_out_2, rel_bias_2,
           final_g_2):
    import numpy as np
    import concourse.bacc as bacc
    from concourse.bass_utils import run_bass_kernel_spmd as run

    def columns(a):
        return np.asarray(a).reshape(-1, P).T

    def taps(w):
        w = np.asarray(w)
        return w.reshape(w.shape[0], -1, P).transpose(2, 1, 0).reshape(P, -1)

    def column_slab(w, e):
        return w[:, P * e:P * e + P].reshape(KT, P, P).transpose(1, 0, 2).reshape(P, 1024)

    def row_slab(w, r):
        return w[P * r:P * r + P, :]

    x = np.asarray(x)
    w_in, w_out, w_gate, w_up, w_down = (np.asarray(a)[0] for a in (w_in, w_out, w_gate, w_up, w_down))
    a_in, a_group, a_out = np.asarray(a_w_in_2)[0], np.asarray(a_w_group_2)[0], np.asarray(a_w_out_2)[0]
    w_kv, b_in, b_out = np.asarray(w_kv_2), np.asarray(b_w_in_2)[0], np.asarray(b_w_out_2)[0]
    slabs = []
    for j in range(MT):
        slabs += [column_slab(w_in, 12 + j), column_slab(w_in, 16 + j)]
    for j in range(MT):
        slabs += [column_slab(w_in, 8 + j), column_slab(w_in, j), column_slab(w_in, 4 + j)]
    slabs += [row_slab(w_out, r) for r in range(KT)]
    for f in range(FT):
        slabs += [column_slab(w_gate, f), column_slab(w_up, f)]
        if f and f % 2 == 0:
            slabs += [row_slab(w_down, f - 2), row_slab(w_down, f - 1)]
    slabs += [row_slab(w_down, FT - 2), row_slab(w_down, FT - 1)]
    for g in range(GROUPS):
        slabs += [column_slab(a_in, 4 * g + n) for n in range(4)]
        slabs += [column_slab(a_in, 16 + 4 * g + n) for n in range(2)]
        slabs += [a_group[g][:, 256 * n:256 * n + 256].reshape(4, P, 256).transpose(1, 0, 2).reshape(P, 1024)
                  for n in range(2)]
        slabs += [column_slab(a_in, 16 + 4 * g + n) for n in range(2, 4)]
        slabs += [row_slab(a_out, 4 * g + n) for n in range(4)]
    for g in range(2):
        k = w_kv[:, HD * g:HD * g + HD]
        slabs.append(column_slab(np.concatenate([k, k], axis=1), 0))
    slabs.append(column_slab(w_kv, 1))
    slabs += [column_slab(b_in, n) for n in range(KT)]
    z = [[column_slab(b_in, 8 + 2 * n), column_slab(b_in, 9 + 2 * n)] for n in range(4)]
    o = [[row_slab(b_out, 2 * n), row_slab(b_out, 2 * n + 1)] for n in range(4)]
    slabs += z[0] + z[1] + o[0] + z[2] + o[1] + z[3] + o[2] + o[3]
    slabs = np.stack(slabs)
    assert len(slabs) == NSLAB

    ada_w, kv_ada = np.asarray(ada_w_2), np.asarray(kv_ada_w_2)
    ada = np.stack([w[:, P * e:P * e + P].T for w in (ada_w[0], ada_w[1], kv_ada) for e in range(w.shape[1] // P)])
    ada = np.concatenate([ada, ada[:2]])
    vec = np.concatenate([columns(norm_mix_g), taps(np.asarray(conv_a_w)[0]), taps(np.asarray(conv_b_w)[0]),
                          columns(conv_b_b), columns(ln_b_g), columns(ln_b_b), columns(norm_ffn_g),
                          taps(np.asarray(conv_ffn_w)[0]), columns(norm_final_g), columns(norm_g_2),
                          columns(ada_b_2), columns(kv_ada_b_2), columns(a_scale_2), columns(kv_norm_g_2),
                          columns(final_g_2)], axis=1)
    assert vec.shape[1] == NVEC
    arrays = {
        "x": x[0].T.reshape(KT, P, S).transpose(1, 0, 2),
        "vec": vec,
        "slabs": slabs,
        "ada": ada,
        "c": np.broadcast_to(np.asarray(c_2)[0], (P, D)),
        "rel": np.asarray(rel_bias_2).T[HEAD_ORDER],
        "sinks": np.broadcast_to(np.asarray(b_sinks_2)[0][HEAD_ORDER], (P, HEADS)),
    }
    arrays = {n: np.ascontiguousarray(a) for n, a in arrays.items()}
    nc = bacc.Bacc("TRN2", target_bir_lowering=False, num_devices=1, dynamic_dma_scratch_size=16)
    f32 = mybir.dt.float32
    arrays = {f"in_{n}": a for n, a in arrays.items()}
    aps = [nc.dram_tensor(n, a.shape, f32, kind="ExternalInput").ap() for n, a in arrays.items()]
    row_scratch = nc.dram_tensor("row_scratch", (HEADS, RLEN), f32, kind="Internal").ap()
    skew_scratch = nc.dram_tensor("skew_scratch", (HEADS, P, RLEN), f32, kind="Internal").ap()
    out = nc.dram_tensor("out", (P, KT, S), f32, kind="ExternalOutput").ap()
    build(nc, *aps, row_scratch, skew_scratch, out)
    r = run(nc, [arrays], core_ids=[0])
    return r.results[0]["out"].transpose(1, 0, 2).reshape(D, S).T[None]
```

```python
import math
from contextlib import ExitStack

import concourse.bass as bass
from concourse import mybir

P = 128
D = 1024
S = 1024
HALF = S // 2
KT = D // P
DM = 512
MT = DM // P
DFF = 2816
FT = DFF // P
TAPS = 31
POOL_WINDOWS = (2, 4, 8, 16)
GROUPS = len(POOL_WINDOWS)
HEADS, HD = 16, 64
BLOCK = 128
NB = S // BLOCK
BUCKETS, MAX_DISTANCE = 32, 128
NEG = -1e30
RLEN = 384

VEC = {}
_at = 0
for _name, _n in (("mix_g", KT), ("conv_a", 3 * MT), ("conv_b", TAPS * MT), ("conv_b_b", MT), ("ln_g", MT),
                  ("ln_b", MT), ("ffn_g", KT), ("conv_ffn", 3 * FT), ("fin1_g", KT), ("norm2_g", 2 * KT),
                  ("ada_b", 64), ("a_scale", 16), ("kv_g", KT), ("fin2_g", KT)):
    VEC[_name] = _at
    _at += _n
NVEC = _at
NADA = 64
SHIFT0, SCALE0, GATE0, SHIFT1, SCALE1, GATE1, SHIFTKV, SCALEKV = 0, 8, 16, 24, 32, 40, 48, 56

HEAD_ORDER = [4 * q + o for q in range(HEADS // 4) for o in (0, 2, 1, 3)]

PAIR_PLACES = ([n % 3 for n in range(14)]
               + [2] + [0, 1, 2] * 10 + [0, 1]
               + [0, 1, 2, 0, 1, 2, 1] * GROUPS)
SLAB_PLACE = [2 * p + h for p in PAIR_PLACES for h in (0, 1)]
SLAB_PLACE += [0, 1] + [4]
SLAB_PLACE += [2 * p + h for p in (1, 0, 2, 1, 0, 2, 1, 0, 2, 1, 0, 2) for h in (0, 1)]
NSLAB = len(SLAB_PLACE)
FFN_SLAB, POOL_SLAB, ATT_SLAB = 28, 94, 150
FFN_LOOPS = 10
ADA_FIRST = NADA - 6 * FFN_LOOPS

OUT_TILE = 16 + 24
FFN_TILE = OUT_TILE + 4 * 16
POOL_TILE = FFN_TILE + 4 + 24 * FFN_LOOPS + 20
ATT_TILE = POOL_TILE + 56 * GROUPS
Q_TILE = ATT_TILE + 6
Z_TILE = Q_TILE + 16


def slab_ends():
    ends, t = [], 0

    def products(slabs, crossed=True):
        nonlocal t
        for n in range(slabs):
            ends.append(t + ((3 + n) if crossed else 2 * (n + 1)))
        t += 2 * slabs

    def down():
        nonlocal t
        t += 16
        ends.extend([t, t])

    for _ in range(4):
        products(2)
    products(12, False)
    for _ in range(4):
        down()
    products(2)
    for _ in range(FFN_LOOPS):
        products(2), products(2), down()
    products(2, False), down()
    for _ in range(GROUPS):
        products(2, False), products(2, False), products(2, False)
        ends.extend([t + 4, t + 4 + 4 + 16 + 4])
        t += 4
        products(2, False)
        t += 16
        downs = [t, t]
        t += 4
        t += 16
        ends.extend(downs + [t, t])
    products(2), products(1, False), products(2)
    products(6, False)
    for n in (0, 0, 1, 0, 1, 0, 1, 1):
        down() if n else products(2, False)
    return ends


SLAB_END = slab_ends()


def refill_after(g, per=0, times=1):
    need = []
    for i in range(times):
        at = g + (per[0] * i if per else 0)
        older = [o for o in range(at) if SLAB_PLACE[o] == SLAB_PLACE[at]]
        need.append((SLAB_END[older[-1]] if older else 0) - (per[1] * i if per else 0))
    return max(need)


def bucket_of(n):
    exact = BUCKETS // 2
    if n < exact:
        return n
    return min(exact + int(math.log(n / exact) / math.log(MAX_DISTANCE / exact) * (BUCKETS - exact)), BUCKETS - 1)


def build(nc, x_in, vec_in, slab_in, ada_in, c_in, rel_in, sink_in, row_scratch, skew_scratch, out):
    f32, f32r = mybir.dt.float32, mybir.dt.float32r
    ACT, ALU, AX = mybir.ActivationFunctionType, mybir.AluOpType, mybir.AxisListType
    root = ExitStack()
    with root:
        def sb(scope, name, shape, dt=f32):
            return scope.enter_context(nc.sbuf_tensor(name, shape, dt))

        def sem(name):
            return root.enter_context(nc.semaphore(name))

        X = sb(root, "stream", [P, KT, S])
        HH = sb(root, "norm_hi", [P, KT, S], f32r)
        HL = sb(root, "norm_lo", [P, KT, S], f32r)
        WH = [sb(root, f"w_hi{n}", [P, 1024], f32r) for n in range(6)]
        WL = [sb(root, f"w_lo{n}", [P, 1024], f32r) for n in range(6)]
        RAW = [sb(root, f"w_raw{n}", [P, 1024]) for n in range(2)]
        vec = sb(root, "vec", [P, NVEC])
        ones = sb(root, "ones", [P, P])
        mods = sb(root, "mods", [P, NADA])
        gains = sb(root, "gains", [P, 3 * KT])
        ada_sum = sb(root, "ada_sum", [P, 6])
        inv_count = sb(root, "inv_count", [P, 16])
        eps = sb(root, "eps", [P, 3])
        zero = sb(root, "zero", [P, 1])
        scrap = sb(root, "scrap", [P, 1])
        sinks = sb(root, "sinks", [P, HEADS])
        top = sb(root, "top", [P, 4, 4])
        neg_top = sb(root, "neg_top", [P, 4, 4])
        sink_gap = sb(root, "sink_gap", [P, 4, 4])
        sink_exp = sb(root, "sink_exp", [P, 4, 4])
        total = sb(root, "total", [P, 4, 4])

        with ExitStack() as s:
            MYH = [sb(s, f"mix_y_hi{n}", [P, 2, S], f32r) for n in range(2)]
            MYL = [sb(s, f"mix_y_lo{n}", [P, 2, S], f32r) for n in range(2)]
            UB = [sb(s, f"glu{n}", [P, 1056]) for n in range(5)]
            rel = sb(s, "rel", [HEADS, BUCKETS])
            by_distance = sb(s, "by_distance", [HEADS, RLEN])
        with ExitStack() as s:
            FYH = sb(s, "ffn_y_hi", [P, 2, S], f32r)
            FYL = sb(s, "ffn_y_lo", [P, 2, S], f32r)
            ADA = sb(s, "ada_raw", [P, 6, 1024])
            c_act = sb(s, "c_act", [P, D])
            SQ_GAINED = sb(s, "squares_gained", [P, S])
            SUM_PLAIN = sb(s, "sum_plain", [P, S])
        with ExitStack() as s:
            PH = sb(s, "pooled_hi", [P, 4, S], f32r)
            PL = sb(s, "pooled_lo", [P, 4, S], f32r)
            SZ = sb(s, "pool_gate", [P, 2, S])
            GYH = sb(s, "pool_y_hi", [P, 2, S], f32r)
            GYL = sb(s, "pool_y_lo", [P, 2, S], f32r)
            T = [sb(s, f"temp{n}", [P, 1044]) for n in range(3)]
        with ExitStack() as s:
            Q = sb(s, "q_then_o", [P, KT, S])
            KD = [sb(s, f"keys{n}", [P, S]) for n in range(2)]
            with ExitStack() as s2:
                BIAS = sb(s2, "bias", [P, 8, 2 * BLOCK])
                PB = [sb(s2, f"probs{n}", [P, 4, 2 * BLOCK]) for n in range(4)]
                ident = sb(s2, "ident", [P, P])
            AYH = sb(s, "att_y_hi", [P, 2, S], f32r)
            AYL = sb(s, "att_y_lo", [P, 2, S], f32r)
            AZ = sb(s, "att_gate", [P, 2, S])
        V = [w[:, :].rearrange("p (b c) -> p b c", b=NB) for w in (WH[2], WL[2])]
        PT = [w[:, :].rearrange("p (k h q) -> p k (h q)", k=2, h=4) for w in (WH[3], WL[3])]
        VT = PB[0][:, :, :].rearrange("p a b -> p (a b)")

        psum = root.enter_context(nc.psum_tensor("psum", [P, 8, 512], f32))
        bank = [psum[:, n, :] for n in range(8)]

        vec_ready = sem("vec_ready")
        x_ready = [sem(f"x_ready{n}") for n in range(8)]
        rel_ready, sink_ready = sem("rel_ready"), sem("sink_ready")
        setup_done = sem("setup_done")
        distance_done, rows_out, skew_out, bias_ready = (sem(n) for n in ("distance_done", "rows_out", "skew_out", "bias_ready"))
        raw_ready = [sem(f"raw_ready{n}") for n in range(2)]
        w_hi_done, slab_ready = sem("w_hi_done"), sem("slab_ready")
        tiles = sem("tiles")
        act_read, dve_read = sem("act_read"), sem("dve_read")
        dve_step = sem("dve_step")
        square_done, sum_done, stat_done, root_done, rstd_done = (
            sem(n) for n in ("square_done", "sum_done", "stat_done", "root_done", "rstd_done"))
        table_loaded = sem("table_loaded")
        gained_square, gained_sum, sums_joined = (sem(n) for n in ("gained_square", "gained_sum", "sums_joined"))
        norm_done, hi_done, lo_done = sem("norm_done"), sem("hi_done"), sem("lo_done")
        stream_normed = sem("stream_normed")
        glu_done, conv_done = sem("glu_done"), sem("conv_done")
        prod_done, my_done, my_hi, my_lo = sem("prod_done"), sem("my_done"), sem("my_hi"), sem("my_lo")
        ln_sum, ln_centred, ln_square, ln_added, ln_var, ln_root, ln_rstd, ln_scaled, ln_silu = (
            sem(n) for n in ("ln_sum", "ln_centred", "ln_square", "ln_added", "ln_var", "ln_root", "ln_rstd",
                             "ln_scaled", "ln_silu"))
        f_conv, f_silu, f_mul, f_hi, f_lo = (sem(n) for n in ("f_conv", "f_silu", "f_mul", "f_hi", "f_lo"))
        c_loaded, c_ready, ada_loaded, ada_summed, ada_read = (
            sem(n) for n in ("c_loaded", "c_ready", "ada_loaded", "ada_summed", "ada_read"))
        gains_done = sem("gains_done")
        p_done, p_hi, p_lo, gy_hi, gy_lo = (sem(n) for n in ("p_done", "p_hi", "p_lo", "gy_hi", "gy_lo"))
        v_turned, v_hi, v_split, ident_zero, ident_done = (
            sem(n) for n in ("v_turned", "v_hi", "v_split", "ident_zero", "ident_done"))
        scored, biased, gap_done, exp_done, inv_done, normed, turned, turned_hi, turned_split, mixed, o_read = (
            sem(n) for n in ("scored", "biased", "gap_done", "exp_done", "inv_done", "normed", "turned",
                             "turned_hi", "turned_split", "mixed", "o_read"))
        az_done, ay_hi, ay_lo, out_done = sem("az_done"), sem("ay_hi"), sem("ay_lo"), sem("out_done")

        def hs(half):
            return slice(HALF * half, HALF * half + HALF)

        def body(t, half=None):
            return t[:, 16:16 + S] if half is None else t[:, 16 + HALF * half:16 + HALF * half + HALF]

        def slot(n):
            return body(T[(n % 4) // 2], n % 2)

        def v(name, n=0):
            return vec[:, VEC[name] + n:VEC[name] + n + 1]

        MIX, FFN, FIN1, POOL, KV, ATT, FIN2 = range(7)
        SUMS_BEFORE = {MIX: 0, FFN: 1, FIN1: 2, KV: 3, FIN2: 4}
        STATS_BEFORE = {MIX: 0, FFN: 1, POOL: 2, FIN1: 3, KV: 4, FIN2: 5}
        APPLIED_BEFORE = {MIX: 0, FFN: 16, FIN1: 32, POOL: 32, KV: 48, ATT: 64, FIN2: 80}

        def squares(n, m):
            return body(T[0], m % 2)

        LN_ORDER = [(half, 2 * pair + e) for pair in range(MT // 2) for half in range(2) for e in range(2)]

        def sum_place(n, half):
            return SUM_PLAIN[:, hs(half)] if n == FIN1 else body(T[2], half)

        def piece(n, m):
            return body(T[1], m % 2) if n != ATT and m < 8 else slot(m)

        def gain(n, k):
            if n == MIX:
                return v("mix_g", k)
            if n == FFN:
                return v("ffn_g", k)
            if n == FIN1:
                return v("fin1_g", k)
            if n == FIN2:
                return v("fin2_g", k)
            at = KT * {POOL: 0, KV: 1, ATT: 2}[n] + k
            return gains[:, at:at + 1]

        def shift(n, k):
            if n not in (POOL, KV, ATT):
                return None
            at = {POOL: SHIFT0, KV: SHIFTKV, ATT: SHIFT1}[n] + k
            return mods[:, at:at + 1]

        block = root.enter_context(nc.Block())

        @block.sync
        def _(sp):
            sp.dma_start(vec[:, :], vec_in).then_inc(vec_ready, 16)
            for n in range(8):
                half, k = divmod(2 * n, 8)
                sp.dma_start(X[:, k:k + 2, hs(half)], x_in[:, k:k + 2, hs(half)]).then_inc(x_ready[n], 16)
                if n % 4 == 3:
                    sp.dma_start(RAW[half][:, :], slab_in[half, :, :]).then_inc(raw_ready[half], 16)
            with sp.Fori(1, NSLAB // 2) as i:
                for n in range(2):
                    sp.wait_ge(slab_ready, 2 * i + n - 1)
                    sp.dma_start(RAW[n][:, :], slab_in[2 * i + n, :, :]).then_inc(raw_ready[n], 16)
            if NSLAB % 2:
                sp.wait_ge(slab_ready, NSLAB - 2)
                sp.dma_start(RAW[0][:, :], slab_in[NSLAB - 1, :, :]).then_inc(raw_ready[0], 16)
            for half in range(2):
                for k in range(0, KT, 2):
                    sp.wait_ge(stream_normed, 16 + 8 * half + k + 2)
                    sp.dma_start(out[:, k:k + 2, hs(half)], X[:, k:k + 2, hs(half)]).then_inc(out_done, 16)
            sp.wait_ge(out_done, 128)

        @block.gpsimd
        def _(gp):
            gp.wait_ge(setup_done, 1)

            def split(g, at, place, refill):
                if at >= 6:
                    gp.wait_ge(tiles, refill)
                gp.wait_ge(raw_ready[at % 2], 8 * (g - at % 2) + 16)
                nc.gpsimd.tensor_tensor(WH[place][:, :], RAW[at % 2][:, :], zero[:, :].to_broadcast([P, 1024]),
                                        ALU.add).then_inc(w_hi_done, 1)
                gp.wait_ge(w_hi_done, g + 1)
                nc.gpsimd.tensor_tensor(WL[place][:, :], RAW[at % 2][:, :], WH[place][:, :].bitcast(f32),
                                        ALU.subtract).then_inc(slab_ready, 1)

            def straight(first, last):
                for g in range(first, last):
                    split(g, g, SLAB_PLACE[g], refill_after(g))

            def sums(n, free=None, first=0):
                if free:
                    gp.wait_ge(*free)
                base = SUMS_BEFORE[n]
                for m in range(first, 16):
                    half, k = divmod(m, 8)
                    dst = sum_place(n, half)
                    if k == 0:
                        continue
                    gp.wait_ge(square_done, 16 * base + m + 1)
                    if k > 1:
                        gp.wait_ge(sum_done, 14 * base + 7 * half + k - 1)
                    nc.gpsimd.tensor_tensor(dst, squares(n, m - 1) if k == 1 else dst, squares(n, m), ALU.add
                                            ).then_inc(sum_done, 1)

            straight(0, 1)
            sums(MIX, first=8)
            straight(1, 15)
            for j in range(MT):
                if j:
                    gp.wait_ge(my_done, 2 * j)
                else:
                    gp.wait_ge(norm_done, 16)
                for half in range(2):
                    gp.wait_ge(act_read, 16 + 6 * j + 3 + half)
                    nc.gpsimd.tensor_tensor(body(T[2], half), body(T[0], half), body(T[1], half), ALU.mult
                                            ).then_inc(prod_done, 1)
                split(15 + 3 * j, 15 + 3 * j, SLAB_PLACE[15 + 3 * j], refill_after(15 + 3 * j))
                for half in range(2):
                    gp.wait_ge(my_hi, 2 * j + half + 1)
                    nc.gpsimd.tensor_tensor(MYL[j // 2][:, j % 2, hs(half)], body(T[0], half),
                                            MYH[j // 2][:, j % 2, hs(half)].bitcast(f32), ALU.subtract).then_inc(my_lo, 1)
                straight(16 + 3 * j, (18 if j < MT - 1 else 17) + 3 * j)
            for half in range(2):
                dst = body(T[2], half)
                for j in range(1, MT):
                    gp.wait_ge(ln_square, MT * half + j + 1)
                    if j > 1:
                        gp.wait_ge(ln_added, 3 * half + j - 1)
                    nc.gpsimd.tensor_tensor(dst, slot(0) if j == 1 else dst, slot(j), ALU.add).then_inc(ln_added, 1)
            straight(26, FFN_SLAB + 2)
            sums(FFN, (ln_scaled, 8))
            with gp.Fori(0, FFN_LOOPS) as i:
                for n in range(FFN_SLAB + 2, FFN_SLAB + 8):
                    split(n + 6 * i, n, SLAB_PLACE[n], refill_after(n, (6, 24), FFN_LOOPS) + 24 * i)
            straight(POOL_SLAB - 4, POOL_SLAB + 1)
            sums(FIN1, (f_lo, FT + 1))
            with gp.Fori(0, GROUPS - 1) as i:
                for n in range(POOL_SLAB + 1, POOL_SLAB + 15):
                    split(n + 14 * i, n, SLAB_PLACE[n], refill_after(n, (14, 56), GROUPS - 1) + 56 * i)
            straight(ATT_SLAB - 13, ATT_SLAB + 1)
            sums(KV, (gy_lo, 8 * GROUPS))
            straight(ATT_SLAB + 1, ATT_SLAB + 11)
            gp.wait_ge(lo_done, APPLIED_BEFORE[ATT] + 16)
            nc.gpsimd.memset(ident[:, :], 1.0).then_inc(ident_zero, 1)
            gp.wait_ge(ident_zero, 1)
            nc.gpsimd.affine_select(out=ident[:, :], in_=ident[:, :], compare_op=ALU.is_equal, fill=0.0, base=0,
                                    pattern=[[-1, P]], channel_multiplier=1).then_inc(ident_done, 1)
            straight(ATT_SLAB + 11, ATT_SLAB + 15)
            for u in range(32):
                lo = BLOCK if (u % 16) // 2 == 0 else 0
                gp.wait_ge(inv_done, u + 1)
                nc.gpsimd.tensor_tensor(PB[u % 4][:, :, lo:], PB[u % 4][:, :, lo:],
                                        total[:, u % 4, :].unsqueeze(2).to_broadcast([P, 4, 2 * BLOCK - lo]),
                                        ALU.mult).then_inc(normed, 1)
            gp.wait_ge(mixed, 32)
            straight(ATT_SLAB + 15, NSLAB)
            sums(FIN2, (az_done, 8))

        @block.tensor
        def _(pe):
            def products(dst, terms):
                for n, (wh, wl, xh, xl) in enumerate(terms):
                    nc.tensor.matmul(dst, wh, xh, start=n == 0, stop=False)
                    nc.tensor.matmul(dst, wh, xl, start=False, stop=False)
                    last = nc.tensor.matmul(dst, wl, xh, start=False, stop=n == len(terms) - 1)
                return last

            def stat(n, half):
                if n == POOL:
                    pe.wait_ge(sums_joined, half + 1)
                else:
                    pe.wait_ge(sum_done, 14 * SUMS_BEFORE[n] + 7 * half + 7)
                nc.tensor.matmul(bank[(6 if n == FIN1 else 4) + half], ones[:, :], sum_place(n, half), start=True, stop=True
                                 ).then_inc(stat_done, 1)

            def slab_tile(t, place, half, gate=None, norm=None):
                terms = []
                for k in range(KT):
                    cols = slice(P * k, P * k + P)
                    terms.append((WH[place][:, cols], WL[place][:, cols], HH[:, k, hs(half)], HL[:, k, hs(half)]))
                if gate is None:
                    products(bank[t % 4], terms).then_inc(tiles, 1)
                    return
                for n, (wh, wl, xh, xl) in enumerate(terms):
                    if half == 0 and n == 3 and norm is not None:
                        stat(norm, 1)
                    if norm == POOL and half == 0 and n in (5, 6):
                        stat(FIN1, n - 5)
                    pe.wait_ge(lo_done, gate + 8 * half + n + 1)
                    nc.tensor.matmul(bank[t % 4], wh, xh, start=n == 0, stop=False)
                    nc.tensor.matmul(bank[t % 4], wh, xl, start=False, stop=False)
                    last = nc.tensor.matmul(bank[t % 4], wl, xh, start=False, stop=n == KT - 1)
                last.then_inc(tiles, 1)

            def freed(j, own, own_base, before):
                if j >= 4:
                    pe.wait_ge(own, own_base + j - 3)
                else:
                    for reader, count in before:
                        pe.wait_ge(reader, count - 3 + j)

            def pair_job(t, g, place, own_base, before, gate=None, crossed=True, norm=None):
                order = [(0, 0), (1, 0), (0, 1), (1, 1)] if crossed else [(0, 0), (0, 1), (1, 0), (1, 1)]
                for j, (n, half) in enumerate(order):
                    if j == 0:
                        pe.wait_ge(slab_ready, g + 1)
                    if n == 1 and order[j - 1][0] == 0 and j < 3:
                        pe.wait_ge(slab_ready, g + 2)
                    freed(j, act_read, own_base, before)
                    slab_tile(t + j, place + n, half, gate if n == 0 else None, norm if n == 0 else None)

            def down_job(t, g, place, own_base, before, yh, yl, norm=None, between=None):
                pe.wait_ge(slab_ready, g + 2)
                for j in range(16):
                    half, e = divmod(j, 8)
                    if between:
                        between(j)
                    if norm is not None and j == (14 if norm == POOL else 10):
                        stat(norm, 0)
                    freed(j, dve_read, own_base, before)
                    cols = slice(P * e, P * e + P)
                    products(bank[(t + j) % 4], [(WH[place + r][:, cols], WL[place + r][:, cols],
                                                  yh[:, r, hs(half)], yl[:, r, hs(half)]) for r in range(2)]
                             ).then_inc(tiles, 1)

            pe.wait_ge(setup_done, 1)

            stat(MIX, 0)
            for n in range(4):
                pair_job(4 * n, 2 * n, SLAB_PLACE[2 * n], 4 * n, [(act_read, 4 * n)] if n else [],
                         gate=0 if n == 0 else None, norm=MIX if n == 0 else None)
            for n in range(6):
                pair_job(16 + 4 * n, 8 + 2 * n, SLAB_PLACE[8 + 2 * n], 16 + 4 * n, [(act_read, 16 + 4 * n)],
                         crossed=False)
            def ln_sums(n, m):
                if (n, m) == (0, 4):
                    pe.wait_ge(conv_done, MT)
                    for half in range(2):
                        for j in range(MT):
                            last = nc.tensor.matmul(bank[4 + half], ones[:, :], body(UB[(j + 4) % 5], half),
                                                    start=j == 0, stop=j == MT - 1)
                        last.then_inc(ln_sum, 1)
                if (n, m) in ((0, 12), (1, 2)):
                    half = n
                    pe.wait_ge(ln_added, 3 * half + 3)
                    nc.tensor.matmul(bank[4 + half], ones[:, :], body(T[2], half), start=True, stop=True
                                     ).then_inc(ln_var, 1)

            def out_between(n, m):
                ln_sums(n, m)
                if m % 8 == 0:
                    pe.wait_ge(my_lo, 4 * n + (4 if n < 2 else 2 + 2 * (m // 8)))

            for n in range(4):
                down_job(OUT_TILE + 16 * n, 20 + 2 * n, SLAB_PLACE[20 + 2 * n], 16 * n,
                         [(dve_read, 16 * n)] if n else [(act_read, 40)], MYH[n % 2], MYL[n % 2],
                         norm=FFN if n == 3 else None, between=lambda m, n=n: out_between(n, m))

            pair_job(FFN_TILE, FFN_SLAB, SLAB_PLACE[FFN_SLAB], 40, [(dve_read, 64)], gate=APPLIED_BEFORE[FFN], norm=FFN)

            with pe.Fori(0, FFN_LOOPS) as i:
                t, g, a, d = FFN_TILE + 4 + 24 * i, FFN_SLAB + 2 + 6 * i, 44 + 8 * i, 64 + 16 * i
                at = FFN_SLAB + 2
                pair_job_t = FFN_TILE + 4
                for m in range(2):
                    before = [(act_read, 44), (dve_read, d)] if m == 0 else [(act_read, a + 4)]
                    order = [(0, 0), (1, 0), (0, 1), (1, 1)]
                    for j, (n, half) in enumerate(order):
                        if half == 0:
                            pe.wait_ge(slab_ready, g + 2 * m + n + 1)
                        freed(j, act_read, a + 4 * m, before)
                        slab_tile(pair_job_t + 4 * m + j, SLAB_PLACE[at + 2 * m] + n, half)
                pe.wait_ge(f_lo, 2 * i + 2)
                pe.wait_ge(slab_ready, g + 6)
                for j in range(16):
                    half, e = divmod(j, 8)
                    freed(j, dve_read, d, [(act_read, a + 8)])
                    cols = slice(P * e, P * e + P)
                    place = SLAB_PLACE[at + 4]
                    products(bank[(pair_job_t + j) % 4], [(WH[place + r][:, cols], WL[place + r][:, cols],
                                                           FYH[:, r, hs(half)], FYL[:, r, hs(half)])
                                                          for r in range(2)]).then_inc(tiles, 1)
            t, g = POOL_TILE - 20, POOL_SLAB - 4
            pair_job(t, g, SLAB_PLACE[g], 124, [(dve_read, 224)], crossed=False)

            def last_y(m):
                if m % 8 == 0:
                    pe.wait_ge(f_lo, FT + m // 8)

            down_job(t + 4, g + 2, SLAB_PLACE[g + 2], 224, [(act_read, 128)], FYH, FYL, norm=POOL, between=last_y)

            def pool_turn(i, first_turn=False, last_turn=False):
                g, a, d = POOL_SLAB + 14 * i, 128 + 16 * i, 240 + 40 * i

                def input_slab(n, j, a0, before):
                    pe.wait_ge(slab_ready, g + n + 1)
                    for half in range(2):
                        for reader, count in before(half):
                            pe.wait_ge(reader, count)
                        gated = first_turn and n == 0
                        slab_tile(j + half, SLAB_PLACE[POOL_SLAB + n], half, APPLIED_BEFORE[POOL] if gated else None,
                                  POOL if gated else None)

                for n in range(4):
                    input_slab(n, 2 * n, a, lambda half, n=n: [(dve_read, d - 3 + 2 * n + half)] if n < 2
                               else [(act_read, a + 2 * n + half - 3)])
                for n in range(2):
                    input_slab(4 + n, 8 + 2 * n, a, lambda half, n=n: [(act_read, a + 8 + 2 * n + half - 3)])

                def group_product(j, first, before):
                    place = SLAB_PLACE[POOL_SLAB + 6 + first // 2]
                    for m, (e, half) in enumerate([(0, 0), (1, 0), (0, 1), (1, 1)]):
                        pe.wait_ge(before[0], before[1] - 3 + m)
                        terms = []
                        for k in range(4):
                            cols = slice(256 * k + P * e, 256 * k + P * e + P)
                            terms.append((WH[place][:, cols], WL[place][:, cols], PH[:, k, hs(half)], PL[:, k, hs(half)]))
                        products(bank[(j + m) % 4], terms).then_inc(tiles, 1)

                pe.wait_ge(slab_ready, g + 8)
                pe.wait_ge(p_lo, 4 * i + 4)
                group_product(12, 0, (act_read, a + 12))
                for n in range(2):
                    input_slab(8 + n, 16 + 2 * n, a, lambda half, n=n: [(dve_read, d + 4 - 3 + 2 * n + half)])

                def down(n, j, first):
                    pe.wait_ge(slab_ready, g + n + 2)
                    place = SLAB_PLACE[POOL_SLAB + n]
                    for m in range(16):
                        half, e = divmod(m, 8)
                        if e == 0:
                            pe.wait_ge(gy_lo, 8 * i + (0 if first else 4) + 2 * half + 2)
                        if last_turn and not first and m == 10:
                            stat(KV, 0)
                        if first and m < 4:
                            pe.wait_ge(act_read, a + 16 - 3 + m)
                        else:
                            pe.wait_ge(dve_read, d + (4 if first else 24) + m - 3)
                        cols = slice(P * e, P * e + P)
                        products(bank[(j + m) % 4], [(WH[place + r][:, cols], WL[place + r][:, cols],
                                                      GYH[:, r, hs(half)], GYL[:, r, hs(half)])
                                                     for r in range(2)]).then_inc(tiles, 1)

                down(10, 20, True)
                group_product(36, 2, (dve_read, d + 20))
                down(12, 40, False)

            pool_turn(0, first_turn=True)
            with pe.Fori(1, GROUPS - 1) as i:
                pool_turn(i)
            pool_turn(GROUPS - 1, last_turn=True)

            t, g = ATT_TILE, ATT_SLAB
            pair_job(t, g, SLAB_PLACE[g], 192, [(dve_read, 400)], gate=APPLIED_BEFORE[KV], norm=KV)
            pe.wait_ge(slab_ready, g + 3)
            for half in range(2):
                pe.wait_ge(act_read, 192 + 4 + half - 3)
                slab_tile(t + 4 + half, SLAB_PLACE[g + 2], half)
            t, g = Q_TILE, ATT_SLAB + 3
            for n in range(4):
                pair_job(t + 4 * n, g + 2 * n, SLAB_PLACE[g + 2 * n], 198 + 4 * n, [(act_read, 198 + 4 * n)],
                         gate=APPLIED_BEFORE[ATT] if n == 0 else None, crossed=n == 0)
            pe.wait_ge(ident_done, 1)
            for b in range(NB):
                last = nc.tensor.transpose(bank[4 + b // 4][:, P * (b % 4):P * (b % 4) + P],
                                           VT[:, P * b:P * b + P], ident[:, :])
                if b % 4 == 3:
                    last.then_inc(v_turned, 1)
            pe.wait_ge(v_split, 2)
            pe.wait_ge(act_read, 214)

            def quad(u):
                group, rest = divmod(u, 16)
                blk, quarter = divmod(rest, 2)
                return group, blk, 4 * group + 2 * quarter

            def scores(u):
                group, blk, q_tile = quad(u)
                if u >= 2:
                    pe.wait_ge(biased, u - 1)
                lo = BLOCK if blk == 0 else 0
                keys = slice(BLOCK * blk - BLOCK + lo, BLOCK * blk + BLOCK)
                for pos in range(4):
                    rows = slice(HD * (pos // 2), HD * (pos // 2) + HD)
                    dst = bank[4 + 2 * (u % 2) + pos // 2]
                    last = nc.tensor.matmul(dst[:, 256 * (pos % 2) + lo:256 * (pos % 2) + 256],
                                            Q[rows, q_tile + pos % 2, BLOCK * blk:BLOCK * blk + BLOCK],
                                            KD[group][rows, keys], start=True, stop=True)
                last.then_inc(scored, 1)

            def turn(u):
                _, blk, _ = quad(u)
                pe.wait_ge(normed, u + 1)
                if u:
                    pe.wait_ge(turned_split, u)
                for chunk in range(1 if blk == 0 else 0, 2):
                    for pos in range(4):
                        last = nc.tensor.transpose(bank[chunk][:, P * pos:P * pos + P],
                                                   PB[u % 4][:, pos, BLOCK * chunk:BLOCK * chunk + BLOCK], ident[:, :])
                last.then_inc(turned, 1)

            def mix_values(u):
                _, blk, _ = quad(u)
                pe.wait_ge(turned_split, u + 1)
                if u >= 2:
                    pe.wait_ge(o_read, u - 1)
                terms = []
                for chunk in range(1 if blk == 0 else 0, 2):
                    b = blk - 1 + chunk
                    terms.append((V[0][:, b, :], V[1][:, b, :], PT[0][:, chunk, :], PT[1][:, chunk, :]))
                products(bank[2 + u % 2], terms).then_inc(mixed, 1)

            for u in range(32 + 4):
                if u < 32:
                    scores(u)
                if u >= 4:
                    mix_values(u - 4)
                if 3 <= u < 35:
                    turn(u - 3)

            pe.wait_ge(o_read, 32)
            pe.wait_ge(turned_split, 32)
            t, g, a, d, done = Z_TILE, ATT_SLAB + 11, 214, 400, 0
            before = []
            for is_down in (0, 0, 1, 0, 1, 0, 1, 1):
                if is_down:
                    pe.wait_ge(ay_lo, 2 * done + 2)
                    down_job(t, g, SLAB_PLACE[g], d, before, AYH, AYL, norm=FIN2 if done == 3 else None)
                    t, d, done, before = t + 16, d + 16, done + 1, [(dve_read, d + 16)]
                else:
                    pair_job(t, g, SLAB_PLACE[g], a, before, crossed=False)
                    t, a, before = t + 4, a + 4, [(act_read, a + 4)]
                g += 2
            stat(FIN2, 1)

        @block.scalar
        def _(act):
            loads = [0]

            def square(n, m):
                half, k = divmod(m, 8)
                at = 14 * SUMS_BEFORE[n] + 7 * half
                if k >= 2:
                    act.wait_ge(sum_done, at + k - 2 + (1 if k == 2 else 0))
                elif half == 1:
                    act.wait_ge(sum_done, at + k - 1)
                nc.scalar.activation(squares(n, m), X[:, k, hs(half)], ACT.Square).then_inc(square_done, 1)

            def square_gained(m):
                half, k = divmod(m, 8)
                if k >= 2:
                    act.wait_ge(gained_sum, 7 * half + k - 2 + (1 if k == 2 else 0))
                elif half == 1:
                    act.wait_ge(gained_sum, k + 6)
                nc.scalar.activation(SQ_GAINED[:, hs(m % 2)], X[:, k, hs(half)], ACT.Square, scale=gain(FIN1, k)
                                     ).then_inc(gained_square, 1)

            def load_roots():
                act.wait_ge(setup_done, 1)
                nc.scalar.activation(scrap[:, :], eps[:, 0:1], ACT.Sqrt).then_inc(table_loaded, 1)
                loads[0] += 1
                act.wait_ge(table_loaded, loads[0])

            def mean_root(n, half):
                act.wait_ge(stat_done, 2 * STATS_BEFORE[n] + half + 1)
                dst = sum_place(n, half)
                bias = eps[:, 2:3] if n == POOL else eps[:, 0:1]
                nc.scalar.activation(dst, bank[(6 if n == FIN1 else 4) + half], ACT.Sqrt, bias=bias, scale=1.0 / D
                                     ).then_inc(root_done, 1)

            def hi(n, m):
                half, k = divmod(m, 8)
                act.wait_ge(norm_done, APPLIED_BEFORE[n] + m + 1)
                if shift(n, k) is None:
                    nc.scalar.copy(HH[:, k, hs(half)], piece(n, m)).then_inc(hi_done, 1)
                else:
                    nc.scalar.activation(HH[:, k, hs(half)], piece(n, m), ACT.Identity, bias=shift(n, k)
                                         ).then_inc(hi_done, 1)

            def norm_after_down(n, reads):
                for m in range(16):
                    act.wait_ge(dve_read, reads + m + 1)
                    square(n, m)
                    if m == 2:
                        load_roots()
                    if m == 9:
                        mean_root(n, 0)
                    if m >= 11:
                        hi(n, m - 11)
                hi(n, 5)
                mean_root(n, 1)
                for m in range(6, 16):
                    hi(n, m)

            def read_tile(t, dst, func=ACT.Copy, scale=1.0):
                count, b = t if isinstance(t, tuple) else (t, t % 4)
                act.wait_ge(tiles, count + 1)
                nc.scalar.activation(dst, bank[b], func, scale=scale).then_inc(act_read, 1)

            act.dma_start(rel[:, :], rel_in).then_inc(rel_ready, 16)
            act.dma_start(sinks[:, :], sink_in).then_inc(sink_ready, 16)

            load_roots()
            for m in range(16):
                if m % 2 == 0:
                    act.wait_ge(x_ready[m // 2], 16)
                square(MIX, m)
                if m == 8:
                    mean_root(MIX, 0)
                if m >= 12:
                    hi(MIX, m - 12)
            for m in range(4, 16):
                hi(MIX, m)
                if m == 5:
                    mean_root(MIX, 1)
            act.wait_ge(distance_done, 1)
            act.dma_start(row_scratch, by_distance[:, :]).then_inc(rows_out, 16)
            act.wait_ge(lo_done, 16)
            for j in range(MT):
                for half in range(2):
                    if j:
                        act.wait_ge(glu_done, 2 * (j - 1) + half + 1)
                    read_tile(4 * j + 2 * half, body(T[1], half))
                    read_tile(4 * j + 2 * half + 1, body(T[0], half), ACT.Sigmoid)
            act.wait_ge(rows_out, 16)
            act.dma_start(skew_scratch, row_scratch.unsqueeze(1).to_broadcast([HEADS, P, RLEN])).then_inc(skew_out, 16)
            act.wait_ge(glu_done, 2 * MT)
            for j in range(MT):
                t = 16 + 6 * j
                for half in range(2):
                    if j:
                        act.wait_ge(my_lo, 2 * j)
                    read_tile(t + half, body(T[0], half))
                for half in range(2):
                    if j:
                        act.wait_ge(my_done, 2 * j)
                    read_tile(t + 2 + half, body(T[1], half))
                for half in range(2):
                    act.wait_ge(prod_done, 2 * j + half + 1)
                    read_tile(t + 4 + half, body(T[1], half))
                for half in range(2):
                    act.wait_ge(my_done, 2 * j + half + 1)
                    nc.scalar.copy(MYH[j // 2][:, j % 2, hs(half)], body(T[0], half)).then_inc(my_hi, 1)
            for half in range(2):
                for j in range(MT):
                    act.wait_ge(ln_centred, MT * half + j + 1)
                    if half == 0:
                        act.wait_ge(my_lo, 8)
                    else:
                        act.wait_ge(ln_added, max(j, 1))
                    nc.scalar.activation(slot(j), body(UB[(j + 4) % 5], half), ACT.Square).then_inc(ln_square, 1)
            for half in range(2):
                act.wait_ge(ln_var, half + 1)
                nc.scalar.activation(body(T[2], half), bank[4 + half], ACT.Sqrt, bias=eps[:, 1:2], scale=1.0 / DM
                                     ).then_inc(ln_root, 1)
            for m, (half, j) in enumerate(LN_ORDER):
                if m % 4 == 0:
                    act.wait_ge(tiles, OUT_TILE + 16 * (1 + j // 2))
                c = body(UB[(j + 4) % 5], half)
                act.wait_ge(ln_scaled, m + 1)
                nc.scalar.activation(c, c, ACT.Silu, bias=v("ln_b", j), scale=v("ln_g", j)).then_inc(ln_silu, 1)
                act.wait_ge(ln_silu, m + 1)
                nc.scalar.copy(MYH[j // 2][:, j % 2, hs(half)], c).then_inc(my_hi, 1)

            norm_after_down(FFN, 48)
            act.wait_ge(tiles, FFN_TILE)
            act.dma_start(ADA[:, 0:ADA_FIRST, :], ada_in[0:ADA_FIRST, :, :].rearrange("s p n -> p s n")
                          ).then_inc(ada_loaded, 16)
            act.dma_start(c_act[:, :], c_in).then_inc(c_loaded, 16)

            def ffn_tile(f, t, b0, free_slot, place, y_free):
                for n, (T_n, half) in enumerate(((0, 0), (1, 0), (0, 1), (1, 1))):
                    if free_slot:
                        act.wait_ge(f_conv if T_n == 0 else f_mul, f)
                    read_tile((t + n, (b0 + n) % 4), body(T[T_n], half))
                act.wait_ge(f_conv, f + 1)
                nc.scalar.activation(body(T[2]), body(T[2]), ACT.Silu).then_inc(f_silu, 1)
                act.wait_ge(tiles, y_free)
                act.wait_ge(f_mul, f + 1)
                nc.scalar.copy(FYH[:, place, :], body(T[2])).then_inc(f_hi, 1)

            act.wait_ge(lo_done, APPLIED_BEFORE[FFN] + 16)
            ffn_tile(0, FFN_TILE, FFN_TILE, False, 0, FFN_TILE)
            act.wait_ge(c_loaded, 16)
            nc.scalar.activation(c_act[:, :], c_act[:, :], ACT.Silu).then_inc(c_ready, 1)
            with act.Fori(0, FFN_LOOPS) as i:
                t = FFN_TILE + 4 + 24 * i
                ffn_tile(2 * i + 1, t, FFN_TILE + 4, True, 1, t)
                act.wait_ge(ada_summed, i + 1)
                act.dma_start(ADA[:, :, :], ada_in[bass.ds(6 * i + ADA_FIRST, 6), :, :].rearrange("s p n -> p s n")
                              ).then_inc(ada_loaded, 16)
                ffn_tile(2 * i + 2, t + 4, FFN_TILE + 8, True, 0, t + 24)
            t = POOL_TILE - 20
            for half in range(2):
                act.wait_ge(f_conv, FT - 1)
                read_tile(t + half, body(T[0], half))
            act.wait_ge(f_conv, FT)
            nc.scalar.activation(body(T[2]), body(T[2]), ACT.Silu).then_inc(f_silu, 1)
            for half in range(2):
                act.wait_ge(f_mul, FT - 1)
                read_tile(t + 2 + half, body(T[1], half))
                act.wait_ge(f_mul, FT + half)
                nc.scalar.copy(FYH[:, 1, hs(half)], body(T[2], half)).then_inc(f_hi, 1)

            for m in range(16):
                act.wait_ge(dve_read, 224 + m + 1)
                square(FIN1, m)
                square_gained(m)
                if m == 2:
                    load_roots()
                if m == 13:
                    mean_root(POOL, 0)
            for m in range(16):
                hi(POOL, m)
                if m == 5:
                    mean_root(POOL, 1)
            for half in range(2):
                mean_root(FIN1, half)
            act.wait_ge(lo_done, APPLIED_BEFORE[POOL] + 16)
            with act.Fori(0, GROUPS) as g:
                t, d = POOL_TILE + 56 * g, 240 + 40 * g
                for n in range(4):
                    for half in range(2):
                        act.wait_ge(p_done, 4 * g + n + 1)
                        read_tile((t + 2 * n + half, (2 * n + half) % 4), body(T[0], half))
                    act.wait_ge(tiles, t - 16)
                    act.wait_ge(p_done, 4 * g + n + 2)
                    src = T[1]
                    nc.scalar.copy(PH[:, n, :], body(src)).then_inc(p_hi, 1)
                for n in range(2):
                    act.wait_ge(dve_read, d - 16)
                    for half in range(2):
                        read_tile((t + 8 + 2 * n + half, (2 * n + half) % 4), SZ[:, n, hs(half)], ACT.Silu)

                def y_his(first, base, free):
                    act.wait_ge(tiles, free)
                    for m, (e, half) in enumerate(((0, 0), (1, 0), (0, 1), (1, 1))):
                        act.wait_ge(dve_read, base + m + 1)
                        nc.scalar.copy(GYH[:, e, hs(half)], body(T[1 + e], half)).then_inc(gy_hi, 1)

                y_his(0, d, t)
                for n in range(2):
                    act.wait_ge(dve_read, d + 4)
                    for half in range(2):
                        read_tile((t + 16 + 2 * n + half, (2 * n + half) % 4), SZ[:, n, hs(half)], ACT.Silu)
                y_his(2, d + 20, t + 36)

            norm_after_down(KV, 384)
            act.wait_ge(tiles, ATT_TILE)
            act.wait_ge(skew_out, 16)
            act.dma_start(BIAS[:, :, :], bass.AP(skew_scratch.tensor, skew_scratch.offset + BLOCK - 1,
                                                 [[RLEN - 1, P], [RLEN * P, 8], [1, 2 * BLOCK]])
                          ).then_inc(bias_ready, 16)
            t = ATT_TILE
            for half in range(2):
                for n in range(2):
                    read_tile(t + 2 * half + n, KD[n][:, hs(half)])
            for half in range(2):
                read_tile(t + 4 + half, VT[:, hs(half)])
            for m in range(16):
                if m % 8 == 0:
                    act.wait_ge(tiles, ATT_TILE + 5 + m // 8)
                hi(ATT, m)
            t = Q_TILE
            for n in range(4):
                for j, (e, half) in enumerate([(0, 0), (1, 0), (0, 1), (1, 1)] if n == 0 else
                                              [(0, 0), (0, 1), (1, 0), (1, 1)]):
                    read_tile(t + 4 * n + j, Q[:, 2 * n + e, hs(half)], scale=HD ** -0.5)
            for n in range(2):
                act.wait_ge(v_turned, n + 1)
                nc.scalar.copy(WH[2][:, 512 * n:512 * n + 512], bank[4 + n]).then_inc(v_hi, 1)

            for u in range(32 + 4):
                if u >= 4:
                    w = u - 4
                    group, rest = divmod(w, 16)
                    blk, quarter = divmod(rest, 2)
                    tile = 4 * group + 2 * quarter
                    act.wait_ge(mixed, w + 1)
                    for side in range(2):
                        rows = slice(HD * side, HD * side + HD)
                        src = bank[2 + w % 2][HD * group:HD * group + HD, 2 * BLOCK * side:2 * BLOCK * side + 2 * BLOCK]
                        ins = nc.scalar.copy(Q[rows, tile:tile + 2, BLOCK * blk:BLOCK * blk + BLOCK],
                                             src.rearrange("p (a b) -> p a b", a=2))
                    ins.then_inc(o_read, 1)
                if 3 <= u < 35:
                    w = u - 3
                    lo = 1 if (w % 16) // 2 == 0 else 0
                    act.wait_ge(turned, w + 1)
                    if w:
                        act.wait_ge(mixed, w)
                    nc.scalar.copy(PT[0][:, lo:2, :], psum[:, lo:2, :]).then_inc(turned_hi, 1)
                if u < 32:
                    lo = BLOCK if (u % 16) // 2 == 0 else 0
                    act.wait_ge(gap_done, u + 1)
                    for pos in range(4):
                        nc.scalar.activation(PB[u % 4][:, pos, lo:], PB[u % 4][:, pos, lo:], ACT.Exp,
                                             bias=neg_top[:, u % 4, pos:pos + 1],
                                             accum_out=total[:, u % 4, pos:pos + 1])
                    nc.scalar.activation(sink_exp[:, u % 4, :], sink_gap[:, u % 4, :], ACT.Exp).then_inc(exp_done, 1)
                if u == 15:
                    act.wait_ge(biased, 16)
                    act.dma_start(BIAS[:, :, :], bass.AP(skew_scratch.tensor,
                                                         skew_scratch.offset + 8 * RLEN * P + BLOCK - 1,
                                                         [[RLEN - 1, P], [RLEN * P, 8], [1, 2 * BLOCK]])
                                  ).then_inc(bias_ready, 16)

            act.wait_ge(o_read, 32)
            t, ends = Z_TILE, []
            for n in range(4):
                for e in range(2):
                    if n:
                        act.wait_ge(az_done, 2 * n - 1 + e)
                    for half in range(2):
                        read_tile(t + 2 * e + half, AZ[:, e, hs(half)], ACT.Silu)
                if n:
                    act.wait_ge(tiles, Z_TILE + 8 + 16 + 20 * (n - 1))
                for e in range(2):
                    act.wait_ge(az_done, 2 * n + e + 1)
                    nc.scalar.copy(AYH[:, e, :], Q[:, 2 * n + e, :]).then_inc(ay_hi, 1)
                t += 4 if n == 0 else 20
            act.wait_ge(az_done, 8)
            for m in range(16):
                act.wait_ge(dve_read, 448 + m + 1)
                square(FIN2, m)
                if m == 2:
                    load_roots()
                if m == 9:
                    mean_root(FIN2, 0)
            mean_root(FIN2, 1)

        @block.vector
        def _(dve):
            steps = [0]

            def step(ins):
                steps[0] += 1
                ins.then_inc(dve_step, 1)
                dve.wait_ge(dve_step, steps[0])

            def rstd(n, half):
                dve.wait_ge(root_done, 2 * STATS_BEFORE[n] + half + 1)
                dst = sum_place(n, half)
                nc.vector.reciprocal(dst, dst).then_inc(rstd_done, 1)

            def scaled(n, m):
                half, k = divmod(m, 8)
                if k == 0:
                    dve.wait_ge(rstd_done, 2 * STATS_BEFORE[KV if n == ATT else n] + half + 1)
                if n == ATT or m >= 10:
                    dve.wait_ge(lo_done, APPLIED_BEFORE[n] + m - 3)
                elif 2 <= m < 8:
                    dve.wait_ge(lo_done, APPLIED_BEFORE[n] + m - 1)
                nc.vector.scalar_tensor_tensor(piece(n, m), X[:, k, hs(half)], gain(n, k), body(T[2], half),
                                               ALU.mult, ALU.mult).then_inc(norm_done, 1)

            def low(n, m):
                half, k = divmod(m, 8)
                dve.wait_ge(hi_done, APPLIED_BEFORE[n] + m + 1)
                src = piece(n, m)
                if shift(n, k) is None:
                    ins = nc.vector.tensor_tensor(HL[:, k, hs(half)], src, HH[:, k, hs(half)].bitcast(f32), ALU.subtract)
                else:
                    ins = nc.vector.scalar_tensor_tensor(HL[:, k, hs(half)], src, shift(n, k),
                                                         HH[:, k, hs(half)].bitcast(f32), ALU.add, ALU.subtract)
                ins.then_inc(lo_done, 1)

            def apply(n, first=0):
                for m in range(first, 16):
                    if m == 8 and n != ATT:
                        rstd(n, 1)
                    scaled(n, m)
                    if m:
                        low(n, m - 1)
                low(n, 15)

            def apply_early(n, j):
                if j == 10:
                    rstd(n, 0)
                if j >= 11:
                    scaled(n, j - 11)
                if j >= 12:
                    low(n, j - 12)

            def norm_stream(n, m):
                half, k = divmod(m, 8)
                if k == 0:
                    dve.wait_ge(rstd_done, 2 * STATS_BEFORE[n] + half + 1)
                part = X[:, k, hs(half)]
                r = sum_place(n, half)
                nc.vector.scalar_tensor_tensor(part, part, gain(n, k), r, ALU.mult, ALU.mult).then_inc(stream_normed, 1)

            def add_down(t, b0, d, gate=None, behind=None):
                dve.wait_ge(dve_read, d)
                for j in range(16):
                    half, e = divmod(j, 8)
                    dve.wait_ge(tiles, t + j + 1)
                    part = X[:, e, hs(half)]
                    src = bank[(b0 + j) % 4]
                    if gate is None:
                        ins = nc.vector.tensor_tensor(part, src, part, ALU.add)
                    else:
                        ins = nc.vector.scalar_tensor_tensor(part, src, mods[:, gate + e:gate + e + 1], part,
                                                             ALU.mult, ALU.add)
                    ins.then_inc(dve_read, 1)
                    if behind:
                        behind(j)

            dve.sem_inc(ada_read, 1)
            dve.sem_inc(p_done, 1)
            step(nc.vector.memset(zero[:, :], 0.0))
            nc.vector.memset(ones[:, :], 1.0)
            nc.vector.memset(eps[:, 0:1], 1e-6)
            nc.vector.memset(eps[:, 2:3], 1e-12)
            nc.vector.memset(eps[:, 1:2], 1e-5).then_inc(setup_done, 1)
            for n in range(15):
                nc.vector.memset(inv_count[:, n:n + 1], 1.0 / (n + 1))
            for buf in T:
                nc.vector.memset(buf[:, 0:16], 0.0)
                nc.vector.memset(buf[:, 16 + S:], 0.0)
            for buf in UB:
                nc.vector.memset(buf[:, 0:16], 0.0)
                nc.vector.memset(buf[:, 16 + S:], 0.0)
            step(nc.vector.memset(by_distance[:, :], NEG))
            dve.wait_ge(rel_ready, 16)
            first = 0
            for n in range(1, BLOCK + 1):
                if n == BLOCK or bucket_of(n) != bucket_of(first):
                    b = bucket_of(first)
                    last = nc.vector.tensor_copy(by_distance[:, 2 * BLOCK - n:2 * BLOCK - first],
                                                 rel[:, b:b + 1].to_broadcast([HEADS, n - first]))
                    first = n
            last.then_inc(distance_done, 1)

            for k in range(1, KT):
                dve.wait_ge(square_done, k + 1)
                if k > 1:
                    dve.wait_ge(sum_done, k - 1)
                nc.vector.tensor_tensor(body(T[2], 0), squares(MIX, 0) if k == 1 else body(T[2], 0), squares(MIX, k),
                                        ALU.add).then_inc(sum_done, 1)
            rstd(MIX, 0)
            dve.wait_ge(vec_ready, 16)
            apply(MIX)

            def conv_taps(first, last):
                for n in range(first, last):
                    j, tap = divmod(n, TAPS)
                    u, c = UB[j], body(UB[(j + 4) % 5])
                    w = v("conv_b", TAPS * j + tap)
                    window = u[:, 1 + tap:1 + tap + S]
                    if tap == 0:
                        dve.wait_ge(glu_done, 2 * j + 2)
                        if j:
                            dve.wait_ge(conv_done, j)
                        step(nc.vector.tensor_scalar(c, window, w, v("conv_b_b", j), ALU.mult, ALU.add))
                    else:
                        ins = nc.vector.scalar_tensor_tensor(c, window, w, c, ALU.mult, ALU.add)
                        if tap == TAPS - 1:
                            ins.then_inc(conv_done, 1)
                        else:
                            step(ins)

            UNIT_TAPS = 15
            for j in range(MT):
                for half in range(2):
                    dve.wait_ge(act_read, 4 * j + 2 * half + 2)
                    nc.vector.tensor_tensor(body(UB[j], half), body(T[1], half), body(T[0], half), ALU.mult
                                            ).then_inc(glu_done, 1)
                conv_taps(UNIT_TAPS * j, UNIT_TAPS * j + UNIT_TAPS)
            rest = MT * TAPS - MT * UNIT_TAPS
            turns = [MT * UNIT_TAPS + rest * n // (3 * MT) for n in range(3 * MT + 1)]
            for j in range(MT):
                conv_taps(*turns[3 * j:3 * j + 2])
                conv_taps(*turns[3 * j + 1:3 * j + 3])
                dve.wait_ge(prod_done, 2 * j + 2)
                step(nc.vector.tensor_scalar(body(T[0]), T[2][:, 15:15 + S], v("conv_a", 3 * j), None, ALU.mult))
                step(nc.vector.scalar_tensor_tensor(body(T[0]), T[2][:, 16:16 + S], v("conv_a", 3 * j + 1), body(T[0]),
                                                    ALU.mult, ALU.add))
                step(nc.vector.scalar_tensor_tensor(body(T[0]), T[2][:, 17:17 + S], v("conv_a", 3 * j + 2), body(T[0]),
                                                    ALU.mult, ALU.add))
                for half in range(2):
                    dve.wait_ge(act_read, 16 + 6 * j + 5 + half)
                    y = body(T[0], half)
                    nc.vector.tensor_tensor(y, y, body(T[1], half), ALU.mult).then_inc(my_done, 1)
                conv_taps(*turns[3 * j + 2:3 * j + 4])
            for n in range(8):
                dve.wait_ge(x_ready[n], 16)

            def add_out(n, behind=None):
                if n:
                    dve.wait_ge(dve_read, 16 * n)
                for m in range(16):
                    half, e = divmod(m, 8)
                    dve.wait_ge(tiles, OUT_TILE + 16 * n + m + 1)
                    part = X[:, e, hs(half)]
                    nc.vector.tensor_tensor(part, bank[(OUT_TILE + m) % 4], part, ALU.add).then_inc(dve_read, 1)
                    if behind:
                        behind(m)

            def centre(m):
                half, j = divmod(m, MT)
                dve.wait_ge(ln_sum, half + 1)
                c = body(UB[(j + 4) % 5], half)
                nc.vector.scalar_tensor_tensor(c, bank[4 + half], -1.0 / DM, c, ALU.mult, ALU.add).then_inc(ln_centred, 1)

            def ln_rstds(half):
                dve.wait_ge(ln_root, half + 1)
                nc.vector.reciprocal(body(T[2], half), body(T[2], half)).then_inc(ln_rstd, 1)

            def ln_scale(m):
                half, j = LN_ORDER[m]
                dve.wait_ge(ln_rstd, half + 1)
                dve.wait_ge(ln_centred, 2 * MT)
                c = body(UB[(j + 4) % 5], half)
                nc.vector.tensor_tensor(c, c, body(T[2], half), ALU.mult).then_inc(ln_scaled, 1)

            def ln_low(m):
                half, j = LN_ORDER[m]
                dve.wait_ge(my_hi, 8 + m + 1)
                nc.vector.tensor_tensor(MYL[j // 2][:, j % 2, hs(half)], body(UB[(j + 4) % 5], half),
                                        MYH[j // 2][:, j % 2, hs(half)].bitcast(f32), ALU.subtract).then_inc(my_lo, 1)

            def behind_first(m):
                if 4 <= m < 12:
                    centre(m - 4)

            def behind_second(m):
                if m == 1:
                    ln_rstds(0)
                elif m == 2:
                    ln_scale(0)
                    ln_scale(1)
                elif m == 4:
                    ln_rstds(1)
                elif m in (6, 7):
                    ln_low(m - 6)
                elif m in (8, 9):
                    ln_scale(m - 6)
                elif m in (11, 12):
                    ln_low(m - 9)
                elif m > 12:
                    ln_scale(m - 9)

            add_out(0, behind_first)
            add_out(1, behind_second)
            ln_scale(7)
            for m in range(4, 8):
                ln_low(m)
            add_out(2)
            add_out(3, lambda m: apply_early(FFN, m))

            apply(FFN, 5)

            def ffn_conv(f, a, first_step, taps, free=True, last=False):
                if free:
                    dve.wait_ge(f_lo, f)
                dve.wait_ge(act_read, a + (2 if last else 3))
                ins = nc.vector.tensor_scalar(body(T[2]), T[0][:, 15:15 + S], taps(0), None, ALU.mult)
                ins.then_inc(dve_step, 1)
                dve.wait_ge(dve_step, first_step + 1)
                ins = nc.vector.scalar_tensor_tensor(body(T[2]), T[0][:, 16:16 + S], taps(1), body(T[2]), ALU.mult, ALU.add)
                ins.then_inc(dve_step, 1)
                dve.wait_ge(dve_step, first_step + 2)
                nc.vector.scalar_tensor_tensor(body(T[2]), T[0][:, 17:17 + S], taps(2), body(T[2]), ALU.mult, ALU.add
                                               ).then_inc(f_conv, 1)
                dve.wait_ge(f_silu, f + 1)
                if last:
                    return
                dve.wait_ge(act_read, a + 4)
                nc.vector.tensor_tensor(body(T[2]), body(T[2]), body(T[1]), ALU.mult).then_inc(f_mul, 1)

            def ffn_lo(f, place):
                dve.wait_ge(f_hi, f + 1)
                nc.vector.tensor_tensor(FYL[:, place, :], body(T[2]), FYH[:, place, :].bitcast(f32), ALU.subtract
                                        ).then_inc(f_lo, 1)

            def ffn_w(f):
                return lambda n: v("conv_ffn", 3 * f + n)

            def ada_products(turn, at, count):
                dve.wait_ge(ada_loaded, 16 * turn + 16)
                dve.wait_ge(ada_read, turn + 1)
                for n in range(count):
                    ins = nc.vector.tensor_tensor_reduce(out=ADA[:, n, :], in0=ADA[:, n, :], in1=c_act[:, :], scale=1.0,
                                                         scalar=0.0, op0=ALU.mult, op1=ALU.add,
                                                         accum_out=ada_sum[:, n:n + 1])
                ins.then_inc(ada_summed, 1)
                dve.wait_ge(ada_summed, turn + 1)
                nc.vector.tensor_tensor(mods[:, bass.ds(at, count)], ada_sum[:, 0:count],
                                        vec[:, bass.ds(VEC["ada_b"] + at, count)], ALU.add).then_inc(ada_read, 1)

            ffn_conv(0, 40, steps[0], ffn_w(0), False)
            ffn_lo(0, 0)
            dve.wait_ge(c_ready, 1)
            ada_products(0, 0, ADA_FIRST)
            base = steps[0] + 2
            with dve.Fori(0, FFN_LOOPS) as i:
                a = 44 + 8 * i

                def loop_w(odd):
                    return lambda n: vec[:, bass.ds(VEC["conv_ffn"] + 3 + 3 * odd + n + 6 * i, 1)]

                ffn_conv(2 * i + 1, a, base + 4 * i, loop_w(0))
                ffn_lo(2 * i + 1, 1)
                ffn_conv(2 * i + 2, a + 4, base + 4 * i + 2, loop_w(1))
                add_down(FFN_TILE + 12 + 24 * i, FFN_TILE, 64 + 16 * i)
                ffn_lo(2 * i + 2, 0)
                ada_products(i + 1, 6 * i + ADA_FIRST, 6)
            steps[0] = base + 4 * FFN_LOOPS
            dve.wait_ge(ada_read, FFN_LOOPS + 2)
            for at, scale, base_col in ((0, SCALE0, VEC["norm2_g"]), (KT, SCALEKV, VEC["kv_g"]),
                                        (2 * KT, SCALE1, VEC["norm2_g"] + KT)):
                nc.vector.scalar_tensor_tensor(gains[:, at:at + KT], mods[:, scale:scale + KT], 1.0,
                                               vec[:, base_col:base_col + KT], ALU.add, ALU.mult).then_inc(gains_done, 1)
            dve.wait_ge(gains_done, 3)
            nc.vector.tensor_tensor(gains[:, 0:KT], gains[:, 0:KT], vec[:, VEC["fin1_g"]:VEC["fin1_g"] + KT], ALU.mult
                                    ).then_inc(gains_done, 1)
            ffn_conv(FT - 1, 124, steps[0], ffn_w(FT - 1), last=True)
            steps[0] += 2
            for half in range(2):
                y = body(T[2], half)
                dve.wait_ge(act_read, 126 + half + 1)
                nc.vector.tensor_tensor(y, y, body(T[1], half), ALU.mult).then_inc(f_mul, 1)
                dve.wait_ge(f_hi, FT + half)
                nc.vector.tensor_tensor(FYL[:, 1, hs(half)], y, FYH[:, 1, hs(half)].bitcast(f32), ALU.subtract
                                        ).then_inc(f_lo, 1)
            dve.wait_ge(f_lo, FT + 1)

            def add_gained(m):
                half, k = divmod(m, 8)
                dst = body(T[2], half)
                if k:
                    dve.wait_ge(gained_square, m + 1)
                    if k > 1:
                        dve.wait_ge(gained_sum, 7 * half + k - 1)
                    nc.vector.tensor_tensor(dst, SQ_GAINED[:, hs(0)] if k == 1 else dst, SQ_GAINED[:, hs(m % 2)], ALU.add
                                            ).then_inc(gained_sum, 1)

            def join_sums(half):
                dve.wait_ge(gained_sum, 7 * half + 7)
                dve.wait_ge(sum_done, 14 * SUMS_BEFORE[FIN1] + 7 * half + 7)
                nc.vector.scalar_tensor_tensor(body(T[2], half), SUM_PLAIN[:, hs(half)], 1e-6, body(T[2], half),
                                               ALU.mult, ALU.add).then_inc(sums_joined, 1)

            def behind_last(j):
                if j >= 2:
                    add_gained(j - 2)
                if j == 11:
                    join_sums(0)

            add_down(POOL_TILE - 16, POOL_TILE, 224, behind=behind_last)

            rstd(POOL, 0)
            add_gained(14)
            add_gained(15)
            join_sums(1)
            dve.wait_ge(gains_done, 4)
            apply(POOL)
            for g in range(GROUPS):
                w = POOL_WINDOWS[g]
                t, a, d = POOL_TILE + 56 * g, 128 + 16 * g, 240 + 40 * g
                for n in range(4):
                    dve.wait_ge(act_read, a + 2 * n + 2)
                    if n:
                        dve.wait_ge(p_lo, 4 * g + n)
                    elif g:
                        dve.wait_ge(gy_lo, 8 * g)
                    order = [1, 2, 1, 2] if g % 2 else [2, 1, 2]
                    src, width = 0, 1
                    for m in range(g + 1):
                        dst = order[m]
                        step(nc.vector.tensor_tensor(body(T[dst]), body(T[src]), T[src][:, 16 - width:16 - width + S],
                                                     ALU.add))
                        src, width = dst, 2 * width
                    edge = w - 1
                    step(nc.vector.scalar_tensor_tensor(T[1][:, 16:16 + S], T[src][:, 16:16 + S], 1.0 / w,
                                                        T[0][:, 16:16 + S], ALU.mult, ALU.subtract))
                    step(nc.vector.tensor_tensor(T[1][:, 16:16 + edge], T[src][:, 16:16 + edge], inv_count[:, 0:edge],
                                                 ALU.mult))
                    nc.vector.tensor_tensor(T[1][:, 16:16 + edge], T[1][:, 16:16 + edge], T[0][:, 16:16 + edge],
                                            ALU.subtract).then_inc(p_done, 1)
                    dve.wait_ge(p_hi, 4 * g + n + 1)
                    nc.vector.tensor_tensor(PL[:, n, :], body(T[1]), PH[:, n, :].bitcast(f32), ALU.subtract
                                            ).then_inc(p_lo, 1)
                    if g == 0 and n < 2:
                        rstd(FIN1, n)
                    elif g == 0:
                        for m in range(8 * (n - 2), 8 * (n - 2) + 8):
                            norm_stream(FIN1, m)

                def group_y(first, t0, gates_read, d0):
                    for half in range(2):
                        for e in range(2):
                            m = 2 * half + e
                            dve.wait_ge(tiles, t0 + m + 1)
                            dve.wait_ge(act_read, gates_read)
                            nc.vector.scalar_tensor_tensor(body(T[1 + e], half), bank[m], v("a_scale", 4 * g + first + e),
                                                           SZ[:, e, hs(half)], ALU.mult, ALU.mult).then_inc(dve_read, 1)
                        for e in range(2):
                            m = 2 * half + e
                            dve.wait_ge(gy_hi, 8 * g + 2 * first + m + 1)
                            nc.vector.tensor_tensor(GYL[:, e, hs(half)], body(T[1 + e], half),
                                                    GYH[:, e, hs(half)].bitcast(f32), ALU.subtract).then_inc(gy_lo, 1)

                group_y(0, t + 12, a + 12, d)
                if g == 0:
                    dve.wait_ge(stream_normed, 16)
                add_down(t + 20, 0, d + 4, GATE0)
                group_y(2, t + 36, a + 16, d + 20)
                add_down(t + 40, 0, d + 24, GATE0,
                         behind=(lambda j: apply_early(KV, j)) if g == GROUPS - 1 else None)

            apply(KV, 5)
            apply(ATT)

            for n in range(2):
                dve.wait_ge(v_hi, n + 1)
                cols = slice(512 * n, 512 * n + 512)
                nc.vector.tensor_tensor(WL[2][:, cols], bank[4 + n], WH[2][:, cols].bitcast(f32), ALU.subtract
                                        ).then_inc(v_split, 1)
            dve.wait_ge(sink_ready, 16)

            def soften(u):
                group, rest = divmod(u, 16)
                blk, quarter = divmod(rest, 2)
                r, lo = u % 4, BLOCK if blk == 0 else 0
                if rest == 0:
                    dve.wait_ge(bias_ready, 16 * group + 16)
                dve.wait_ge(scored, u + 1)
                if u >= 4:
                    dve.wait_ge(turned, u - 3)
                scores = psum[:, 4 + 2 * (u % 2):6 + 2 * (u % 2), :].rearrange("p a (b c) -> p (a b) c", b=2)
                nc.vector.tensor_tensor(PB[r][:, :, lo:], scores[:, :, lo:], BIAS[:, 4 * quarter:4 * quarter + 4, lo:],
                                        ALU.add).then_inc(biased, 1)
                dve.wait_ge(biased, u + 1)
                step(nc.vector.tensor_reduce(top[:, r, :], PB[r][:, :, lo:], AX.X, ALU.max))
                sink = sinks[:, 8 * group + 4 * quarter:8 * group + 4 * quarter + 4]
                step(nc.vector.tensor_tensor(top[:, r, :], top[:, r, :], sink, ALU.max))
                nc.vector.tensor_scalar(neg_top[:, r, :], top[:, r, :], -1.0, None, ALU.mult)
                nc.vector.tensor_tensor(sink_gap[:, r, :], sink, top[:, r, :], ALU.subtract).then_inc(gap_done, 1)

            for u in range(32 + 3):
                if u < 32:
                    soften(u)
                if 1 <= u < 33:
                    r = (u - 1) % 4
                    dve.wait_ge(exp_done, u)
                    step(nc.vector.tensor_tensor(total[:, r, :], total[:, r, :], sink_exp[:, r, :], ALU.add))
                    nc.vector.reciprocal(total[:, r, :], total[:, r, :]).then_inc(inv_done, 1)
                if u >= 3:
                    w = u - 3
                    lo = 1 if (w % 16) // 2 == 0 else 0
                    dve.wait_ge(turned_hi, w + 1)
                    nc.vector.tensor_tensor(PT[1][:, lo:2, :], psum[:, lo:2, :], PT[0][:, lo:2, :].bitcast(f32),
                                            ALU.subtract).then_inc(turned_split, 1)

            dve.wait_ge(o_read, 32)
            t, d = Z_TILE, 400

            def gated(n):
                for e in range(2):
                    dve.wait_ge(act_read, 214 + 4 * n + 2 * e + 2)
                    nc.vector.tensor_tensor(Q[:, 2 * n + e, :], Q[:, 2 * n + e, :], AZ[:, e, :], ALU.mult).then_inc(az_done, 1)

            def gated_lo(n):
                for e in range(2):
                    dve.wait_ge(ay_hi, 2 * n + e + 1)
                    nc.vector.tensor_tensor(AYL[:, e, :], Q[:, 2 * n + e, :], AYH[:, e, :].bitcast(f32), ALU.subtract
                                            ).then_inc(ay_lo, 1)

            gated(0)
            gated_lo(0)
            for n in range(1, 4):
                gated(n)
                first = Z_TILE + 8 + 20 * (n - 1)
                add_down(first, first, 400 + 16 * (n - 1), GATE1)
                gated_lo(n)

            def final_early(j):
                if j == 10:
                    rstd(FIN2, 0)
                if j >= 11:
                    norm_stream(FIN2, j - 11)

            add_down(Z_TILE + 64, Z_TILE + 64, 448, GATE1, behind=final_early)
            for m in range(5, 8):
                norm_stream(FIN2, m)
            rstd(FIN2, 1)
            for m in range(8, 16):
                norm_stream(FIN2, m)


def kernel(x, norm_mix_g, w_in, conv_a_w, conv_b_w, conv_b_b, ln_b_g, ln_b_b, w_out, norm_ffn_g, w_gate, w_up,
           conv_ffn_w, w_down, norm_final_g, c_2, norm_g_2, ada_w_2, ada_b_2, a_w_in_2, a_w_group_2, a_scale_2,
           a_w_out_2, kv_norm_g_2, kv_ada_w_2, kv_ada_b_2, w_kv_2, b_w_in_2, b_sinks_2, b_w_out_2, rel_bias_2,
           final_g_2):
    import numpy as np
    import concourse.bacc as bacc
    from concourse.bass_utils import run_bass_kernel_spmd as run

    def columns(a):
        return np.asarray(a).reshape(-1, P).T

    def taps(w):
        w = np.asarray(w)
        return w.reshape(w.shape[0], -1, P).transpose(2, 1, 0).reshape(P, -1)

    def column_slab(w, e):
        return w[:, P * e:P * e + P].reshape(KT, P, P).transpose(1, 0, 2).reshape(P, 1024)

    def row_slab(w, r):
        return w[P * r:P * r + P, :]

    x = np.asarray(x)
    w_in, w_out, w_gate, w_up, w_down = (np.asarray(a)[0] for a in (w_in, w_out, w_gate, w_up, w_down))
    a_in, a_group, a_out = np.asarray(a_w_in_2)[0], np.asarray(a_w_group_2)[0], np.asarray(a_w_out_2)[0]
    w_kv, b_in, b_out = np.asarray(w_kv_2), np.asarray(b_w_in_2)[0], np.asarray(b_w_out_2)[0]
    slabs = []
    for j in range(MT):
        slabs += [column_slab(w_in, 12 + j), column_slab(w_in, 16 + j)]
    for j in range(MT):
        slabs += [column_slab(w_in, 8 + j), column_slab(w_in, j), column_slab(w_in, 4 + j)]
    slabs += [row_slab(w_out, r) for r in range(KT)]
    for f in range(FT):
        slabs += [column_slab(w_gate, f), column_slab(w_up, f)]
        if f and f % 2 == 0:
            slabs += [row_slab(w_down, f - 2), row_slab(w_down, f - 1)]
    slabs += [row_slab(w_down, FT - 2), row_slab(w_down, FT - 1)]
    for g in range(GROUPS):
        slabs += [column_slab(a_in, 4 * g + n) for n in range(4)]
        slabs += [column_slab(a_in, 16 + 4 * g + n) for n in range(2)]
        slabs += [a_group[g][:, 256 * n:256 * n + 256].reshape(4, P, 256).transpose(1, 0, 2).reshape(P, 1024)
                  for n in range(2)]
        slabs += [column_slab(a_in, 16 + 4 * g + n) for n in range(2, 4)]
        slabs += [row_slab(a_out, 4 * g + n) for n in range(4)]
    for g in range(2):
        k = w_kv[:, HD * g:HD * g + HD]
        slabs.append(column_slab(np.concatenate([k, k], axis=1), 0))
    slabs.append(column_slab(w_kv, 1))
    slabs += [column_slab(b_in, n) for n in range(KT)]
    z = [[column_slab(b_in, 8 + 2 * n), column_slab(b_in, 9 + 2 * n)] for n in range(4)]
    o = [[row_slab(b_out, 2 * n), row_slab(b_out, 2 * n + 1)] for n in range(4)]
    slabs += z[0] + z[1] + o[0] + z[2] + o[1] + z[3] + o[2] + o[3]
    slabs = np.stack(slabs)
    assert len(slabs) == NSLAB

    ada_w, kv_ada = np.asarray(ada_w_2), np.asarray(kv_ada_w_2)
    ada = np.stack([w[:, P * e:P * e + P].T for w in (ada_w[0], ada_w[1], kv_ada) for e in range(w.shape[1] // P)])
    vec = np.concatenate([columns(norm_mix_g), taps(np.asarray(conv_a_w)[0]), taps(np.asarray(conv_b_w)[0]),
                          columns(conv_b_b), columns(ln_b_g), columns(ln_b_b), columns(norm_ffn_g),
                          taps(np.asarray(conv_ffn_w)[0]), columns(norm_final_g), columns(norm_g_2),
                          columns(ada_b_2), columns(kv_ada_b_2), columns(a_scale_2), columns(kv_norm_g_2),
                          columns(final_g_2)], axis=1)
    assert vec.shape[1] == NVEC
    arrays = {
        "x": x[0].T.reshape(KT, P, S).transpose(1, 0, 2),
        "vec": vec,
        "slabs": slabs,
        "ada": ada,
        "c": np.broadcast_to(np.asarray(c_2)[0], (P, D)),
        "rel": np.asarray(rel_bias_2).T[HEAD_ORDER],
        "sinks": np.broadcast_to(np.asarray(b_sinks_2)[0][HEAD_ORDER], (P, HEADS)),
    }
    arrays = {n: np.ascontiguousarray(a) for n, a in arrays.items()}
    nc = bacc.Bacc("TRN2", target_bir_lowering=False, num_devices=1, dynamic_dma_scratch_size=16)
    f32 = mybir.dt.float32
    arrays = {f"in_{n}": a for n, a in arrays.items()}
    aps = [nc.dram_tensor(n, a.shape, f32, kind="ExternalInput").ap() for n, a in arrays.items()]
    row_scratch = nc.dram_tensor("row_scratch", (HEADS, RLEN), f32, kind="Internal").ap()
    skew_scratch = nc.dram_tensor("skew_scratch", (HEADS, P, RLEN), f32, kind="Internal").ap()
    out = nc.dram_tensor("out", (P, KT, S), f32, kind="ExternalOutput").ap()
    build(nc, *aps, row_scratch, skew_scratch, out)
    r = run(nc, [arrays], core_ids=[0])
    return r.results[0]["out"].transpose(1, 0, 2).reshape(D, S).T[None]
```

```python
import math
from contextlib import ExitStack

import concourse.bass as bass
from concourse import mybir

P = 128
D = 1024
S = 1024
HALF = S // 2
KT = D // P
DM = 512
MT = DM // P
DFF = 2816
FT = DFF // P
TAPS = 31
POOL_WINDOWS = (2, 4, 8, 16)
GROUPS = len(POOL_WINDOWS)
HEADS, HD = 16, 64
BLOCK = 128
NB = S // BLOCK
BUCKETS, MAX_DISTANCE = 32, 128
NEG = -1e30
RLEN = 384

VEC = {}
_at = 0
for _name, _n in (("mix_g", KT), ("conv_a", 3 * MT), ("conv_b", TAPS * MT), ("conv_b_b", MT), ("ln_g", MT),
                  ("ln_b", MT), ("ffn_g", KT), ("conv_ffn", 3 * FT), ("fin1_g", KT), ("norm2_g", 2 * KT),
                  ("ada_b", 64), ("a_scale", 16), ("kv_g", KT), ("fin2_g", KT)):
    VEC[_name] = _at
    _at += _n
NVEC = _at
NADA = 64
SHIFT0, SCALE0, GATE0, SHIFT1, SCALE1, GATE1, SHIFTKV, SCALEKV = 0, 8, 16, 24, 32, 40, 48, 56

HEAD_ORDER = [4 * q + o for q in range(HEADS // 4) for o in (0, 2, 1, 3)]

PAIR_PLACES = ([n % 3 for n in range(14)]
               + [2] + [0, 1, 2] * 10 + [0, 1]
               + [0, 1, 2, 0, 1, 2, 1] * GROUPS)
SLAB_PLACE = [2 * p + h for p in PAIR_PLACES for h in (0, 1)]
SLAB_PLACE += [0, 1] + [4]
SLAB_PLACE += [2 * p + h for p in (1, 0, 2, 0, 2, 0, 1, 2, 0, 1, 2, 0) for h in (0, 1)]
NSLAB = len(SLAB_PLACE)
FFN_SLAB, POOL_SLAB, ATT_SLAB = 28, 94, 150
FFN_LOOPS = 10
ADA_FIRST = NADA - 6 * FFN_LOOPS

OUT_TILE = 16 + 24
FFN_TILE = OUT_TILE + 4 * 16
POOL_TILE = FFN_TILE + 4 + 24 * FFN_LOOPS + 20
ATT_TILE = POOL_TILE + 56 * GROUPS
Q_TILE = ATT_TILE + 6
Z_TILE = Q_TILE + 16


def slab_ends():
    ends, t = [], 0

    def products(slabs, crossed=True):
        nonlocal t
        for n in range(slabs):
            ends.append(t + ((3 + n) if crossed else 2 * (n + 1)))
        t += 2 * slabs

    def down():
        nonlocal t
        t += 16
        ends.extend([t, t])

    for _ in range(4):
        products(2)
    products(12, False)
    for _ in range(4):
        down()
    products(2)
    for _ in range(FFN_LOOPS):
        products(2), products(2), down()
    products(2, False), down()
    for _ in range(GROUPS):
        products(2), products(2, False), products(2, False)
        ends.extend([t + 4, t + 4 + 4 + 16 + 4])
        t += 4
        products(2, False)
        t += 16
        downs = [t, t]
        t += 4
        t += 16
        ends.extend(downs + [t, t])
    products(2), products(1, False), products(2)
    products(6, False)
    for n in (0, 0, 1, 0, 1, 0):
        down() if n else products(2, False)
    ends.extend([t + 24, t + 24, t + 32, t + 32])
    return ends


SLAB_END = slab_ends()


def refill_after(g, per=0, times=1):
    need = []
    for i in range(times):
        at = g + (per[0] * i if per else 0)
        older = [o for o in range(at) if SLAB_PLACE[o] == SLAB_PLACE[at]]
        need.append((SLAB_END[older[-1]] if older else 0) - (per[1] * i if per else 0))
    return max(need)


def bucket_of(n):
    exact = BUCKETS // 2
    if n < exact:
        return n
    return min(exact + int(math.log(n / exact) / math.log(MAX_DISTANCE / exact) * (BUCKETS - exact)), BUCKETS - 1)


def build(nc, x_in, vec_in, slab_in, ada_in, c_in, rel_in, sink_in, row_scratch, skew_scratch, out):
    f32, f32r = mybir.dt.float32, mybir.dt.float32r
    ACT, ALU, AX = mybir.ActivationFunctionType, mybir.AluOpType, mybir.AxisListType
    root = ExitStack()
    with root:
        def sb(scope, name, shape, dt=f32):
            return scope.enter_context(nc.sbuf_tensor(name, shape, dt))

        def sem(name):
            return root.enter_context(nc.semaphore(name))

        X = sb(root, "stream", [P, KT, S])
        HH = sb(root, "norm_hi", [P, KT, S], f32r)
        HL = sb(root, "norm_lo", [P, KT, S], f32r)
        WH = [sb(root, f"w_hi{n}", [P, 1024], f32r) for n in range(6)]
        WL = [sb(root, f"w_lo{n}", [P, 1024], f32r) for n in range(6)]
        RAW = [sb(root, f"w_raw{n}", [P, 1024]) for n in range(2)]
        vec = sb(root, "vec", [P, NVEC])
        ones = sb(root, "ones", [P, P])
        mods = sb(root, "mods", [P, NADA])
        gains = sb(root, "gains", [P, 3 * KT])
        ada_sum = sb(root, "ada_sum", [P, 6])
        inv_count = sb(root, "inv_count", [P, 16])
        eps = sb(root, "eps", [P, 3])
        zero = sb(root, "zero", [P, 1])
        scrap = sb(root, "scrap", [P, 1])
        sinks = sb(root, "sinks", [P, HEADS])
        top = sb(root, "top", [P, 4, 4])
        neg_top = sb(root, "neg_top", [P, 4, 4])
        sink_gap = sb(root, "sink_gap", [P, 4, 4])
        sink_exp = sb(root, "sink_exp", [P, 4, 4])
        total = sb(root, "total", [P, 4, 4])

        with ExitStack() as s:
            MYH = [sb(s, f"mix_y_hi{n}", [P, 2, S], f32r) for n in range(2)]
            MYL = [sb(s, f"mix_y_lo{n}", [P, 2, S], f32r) for n in range(2)]
            UB = [sb(s, f"glu{n}", [P, 1056]) for n in range(5)]
            rel = sb(s, "rel", [HEADS, BUCKETS])
            by_distance = sb(s, "by_distance", [HEADS, RLEN])
        with ExitStack() as s:
            FYH = sb(s, "ffn_y_hi", [P, 2, S], f32r)
            FYL = sb(s, "ffn_y_lo", [P, 2, S], f32r)
            ADA = sb(s, "ada_raw", [P, 6, 1024])
            c_act = sb(s, "c_act", [P, D])
            SQ_GAINED = sb(s, "squares_gained", [P, S])
            SUM_PLAIN = sb(s, "sum_plain", [P, S])
        with ExitStack() as s:
            PH = sb(s, "pooled_hi", [P, 4, S], f32r)
            PL = sb(s, "pooled_lo", [P, 4, S], f32r)
            SZ = sb(s, "pool_gate", [P, 2, S])
            GYH = sb(s, "pool_y_hi", [P, 2, S], f32r)
            GYL = sb(s, "pool_y_lo", [P, 2, S], f32r)
            T = [sb(s, f"temp{n}", [P, 1044]) for n in range(3)]
        with ExitStack() as s:
            Q = sb(s, "q_then_o", [P, KT, S])
            KD = [sb(s, f"keys{n}", [P, S]) for n in range(2)]
            with ExitStack() as s2:
                BIAS = sb(s2, "bias", [P, 8, 2 * BLOCK])
                PB = [sb(s2, f"probs{n}", [P, 4, 2 * BLOCK]) for n in range(4)]
                ident = sb(s2, "ident", [P, P])
            AYH = sb(s, "att_y_hi", [P, 2, S], f32r)
            AYL = sb(s, "att_y_lo", [P, 2, S], f32r)
            AZ = sb(s, "att_gate", [P, 2, S])
        V = [w[:, :].rearrange("p (b c) -> p b c", b=NB) for w in (WH[2], WL[2])]
        PT = [w[:, :].rearrange("p (k h q) -> p k (h q)", k=2, h=4) for w in (WH[3], WL[3])]
        VT = PB[0][:, :, :].rearrange("p a b -> p (a b)")

        psum = root.enter_context(nc.psum_tensor("psum", [P, 8, 512], f32))
        bank = [psum[:, n, :] for n in range(8)]

        vec_ready = sem("vec_ready")
        x_ready = [sem(f"x_ready{n}") for n in range(8)]
        rel_ready, sink_ready = sem("rel_ready"), sem("sink_ready")
        setup_done = sem("setup_done")
        distance_done, rows_out, skew_out = (sem(n) for n in ("distance_done", "rows_out", "skew_out"))
        bias_ready = [sem(f"bias_ready{n}") for n in range(4)]
        raw_ready = [sem(f"raw_ready{n}") for n in range(2)]
        w_hi_done, slab_ready = sem("w_hi_done"), sem("slab_ready")
        tiles = sem("tiles")
        act_read, dve_read = sem("act_read"), sem("dve_read")
        dve_step = sem("dve_step")
        square_done, sum_done, stat_done, root_done, rstd_done = (
            sem(n) for n in ("square_done", "sum_done", "stat_done", "root_done", "rstd_done"))
        table_loaded = sem("table_loaded")
        gained_square, gained_sum, sums_joined = (sem(n) for n in ("gained_square", "gained_sum", "sums_joined"))
        norm_done, hi_done, lo_done = sem("norm_done"), sem("hi_done"), sem("lo_done")
        stream_normed, pool_normed, stream_gained = sem("stream_normed"), sem("pool_normed"), sem("stream_gained")
        glu_done, conv_done, first_tap = sem("glu_done"), sem("conv_done"), sem("first_tap")
        prod_done, my_done, my_hi, my_lo = sem("prod_done"), sem("my_done"), sem("my_hi"), sem("my_lo")
        ln_sum, ln_centred, ln_square, ln_added, ln_var, ln_root, ln_rstd, ln_scaled, ln_silu = (
            sem(n) for n in ("ln_sum", "ln_centred", "ln_square", "ln_added", "ln_var", "ln_root", "ln_rstd",
                             "ln_scaled", "ln_silu"))
        f_conv, f_silu, f_mul, f_hi, f_lo = (sem(n) for n in ("f_conv", "f_silu", "f_mul", "f_hi", "f_lo"))
        c_loaded, c_ready, ada_loaded, ada_summed, ada_read = (
            sem(n) for n in ("c_loaded", "c_ready", "ada_loaded", "ada_summed", "ada_read"))
        gains_done = sem("gains_done")
        p_done, p_hi, p_lo, gy_hi, gy_lo = (sem(n) for n in ("p_done", "p_hi", "p_lo", "gy_hi", "gy_lo"))
        v_turned, v_hi, v_split, ident_zero, ident_done = (
            sem(n) for n in ("v_turned", "v_hi", "v_split", "ident_zero", "ident_done"))
        scored, biased, gap_done, exp_done, inv_done, normed, turned, turned_hi, turned_split, mixed, o_read = (
            sem(n) for n in ("scored", "biased", "gap_done", "exp_done", "inv_done", "normed", "turned",
                             "turned_hi", "turned_split", "mixed", "o_read"))
        az_done, ay_hi, ay_lo, out_done = sem("az_done"), sem("ay_hi"), sem("ay_lo"), sem("out_done")

        def hs(half):
            return slice(HALF * half, HALF * half + HALF)

        def body(t, half=None):
            return t[:, 16:16 + S] if half is None else t[:, 16 + HALF * half:16 + HALF * half + HALF]

        def slot(n):
            return body(T[(n % 4) // 2], n % 2)

        def v(name, n=0):
            return vec[:, VEC[name] + n:VEC[name] + n + 1]

        MIX, FFN, FIN1, POOL, KV, ATT, FIN2 = range(7)
        SUMS_BEFORE = {MIX: 0, FFN: 1, FIN1: 2, KV: 3, FIN2: 4}
        STATS_BEFORE = {MIX: 0, FFN: 1, POOL: 2, FIN1: 3, KV: 4, FIN2: 5}
        APPLIED_BEFORE = {MIX: 0, FFN: 16, FIN1: 32, POOL: 32, KV: 48, ATT: 64, FIN2: 80}

        def squares(n, m):
            return body(T[0], m % 2)

        POOL_FROM = 13

        LN_ORDER = [(half, 2 * pair + e) for pair in range(MT // 2) for half in range(2) for e in range(2)]

        def first_chunk(u):
            return 1 if (u % 16) // 2 == 0 else 0

        def chunks(u, chunk=0):
            return sum(2 - first_chunk(w) for w in range(u)) + max(0, chunk - first_chunk(u))

        def sum_place(n, half):
            return SUM_PLAIN[:, hs(half)] if n == FIN1 else body(T[2], half)

        def piece(n, m):
            return body(T[1], m % 2) if n != ATT and m < 8 else slot(m)

        def gain(n, k):
            if n == MIX:
                return v("mix_g", k)
            if n == FFN:
                return v("ffn_g", k)
            if n == FIN1:
                return v("fin1_g", k)
            if n == FIN2:
                return v("fin2_g", k)
            at = KT * {POOL: 0, KV: 1, ATT: 2}[n] + k
            return gains[:, at:at + 1]

        def shift(n, k):
            if n not in (POOL, KV, ATT):
                return None
            at = {POOL: SHIFT0, KV: SHIFTKV, ATT: SHIFT1}[n] + k
            return mods[:, at:at + 1]

        block = root.enter_context(nc.Block())

        @block.sync
        def _(sp):
            sp.dma_start(vec[:, :], vec_in).then_inc(vec_ready, 16)
            for half in range(2):
                for k in range(0, KT, 2):
                    sp.dma_start(X[:, k:k + 2, hs(half)], x_in[:, k:k + 2, hs(half)]
                                 ).then_inc(x_ready[(8 * half + k) // 2], 16)
                if half == 0:
                    for n in range(2):
                        sp.dma_start(RAW[n][:, :], slab_in[n, :, :]).then_inc(raw_ready[n], 16)
            with sp.Fori(1, NSLAB // 2) as i:
                for n in range(2):
                    sp.wait_ge(slab_ready, 2 * i + n - 1)
                    sp.dma_start(RAW[n][:, :], slab_in[2 * i + n, :, :]).then_inc(raw_ready[n], 16)
            if NSLAB % 2:
                sp.wait_ge(slab_ready, NSLAB - 2)
                sp.dma_start(RAW[0][:, :], slab_in[NSLAB - 1, :, :]).then_inc(raw_ready[0], 16)
            for half in range(2):
                for k in range(0, KT, 2):
                    sp.wait_ge(stream_normed, 16 + min(8 * half + k + 2, POOL_FROM))
                    if 8 * half + k + 2 > POOL_FROM:
                        sp.wait_ge(pool_normed, 8 * half + k + 2 - POOL_FROM)
                    sp.dma_start(out[:, k:k + 2, hs(half)], X[:, k:k + 2, hs(half)]).then_inc(out_done, 16)
            sp.wait_ge(out_done, 128)

        @block.gpsimd
        def _(gp):
            gp.wait_ge(setup_done, 1)

            def split(g, at, place, refill):
                if at >= 6:
                    gp.wait_ge(tiles, refill)
                gp.wait_ge(raw_ready[at % 2], 8 * (g - at % 2) + 16)
                nc.gpsimd.tensor_tensor(WH[place][:, :], RAW[at % 2][:, :], zero[:, :].to_broadcast([P, 1024]),
                                        ALU.add).then_inc(w_hi_done, 1)
                gp.wait_ge(w_hi_done, g + 1)
                nc.gpsimd.tensor_tensor(WL[place][:, :], RAW[at % 2][:, :], WH[place][:, :].bitcast(f32),
                                        ALU.subtract).then_inc(slab_ready, 1)

            def straight(first, last):
                for g in range(first, last):
                    split(g, g, SLAB_PLACE[g], refill_after(g))

            def sums(n, free=None, first=0, last=16):
                if free:
                    gp.wait_ge(*free)
                base = SUMS_BEFORE[n]
                for m in range(first, last):
                    half, k = divmod(m, 8)
                    dst = sum_place(n, half)
                    if k == 0:
                        continue
                    gp.wait_ge(square_done, 16 * base + m + 1)
                    if k > 1:
                        gp.wait_ge(sum_done, 14 * base + 7 * half + k - 1)
                    nc.gpsimd.tensor_tensor(dst, squares(n, m - 1) if k == 1 else dst, squares(n, m), ALU.add
                                            ).then_inc(sum_done, 1)

            straight(0, 2)
            sums(MIX, first=8)
            straight(2, 15)
            for j in range(MT):
                if j:
                    gp.wait_ge(my_done, 2 * j)
                else:
                    gp.wait_ge(norm_done, 16)
                for half in range(2):
                    gp.wait_ge(act_read, 16 + 6 * j + 3 + half)
                    nc.gpsimd.tensor_tensor(body(T[2], half), body(T[0], half), body(T[1], half), ALU.mult
                                            ).then_inc(prod_done, 1)
                split(15 + 3 * j, 15 + 3 * j, SLAB_PLACE[15 + 3 * j], refill_after(15 + 3 * j))
                for half in range(2):
                    gp.wait_ge(my_hi, 2 * j + half + 1)
                    nc.gpsimd.tensor_tensor(MYL[j // 2][:, j % 2, hs(half)], body(T[0], half),
                                            MYH[j // 2][:, j % 2, hs(half)].bitcast(f32), ALU.subtract).then_inc(my_lo, 1)
                straight(16 + 3 * j, (18 if j < MT - 1 else 17) + 3 * j)
            for half in range(2):
                dst = body(T[2], half)
                for j in range(1, MT):
                    gp.wait_ge(ln_square, MT * half + j + 1)
                    if j > 1:
                        gp.wait_ge(ln_added, 3 * half + j - 1)
                    nc.gpsimd.tensor_tensor(dst, slot(0) if j == 1 else dst, slot(j), ALU.add).then_inc(ln_added, 1)
            straight(26, FFN_SLAB + 2)
            sums(FFN, first=8)
            with gp.Fori(0, FFN_LOOPS) as i:
                for n in range(FFN_SLAB + 2, FFN_SLAB + 8):
                    split(n + 6 * i, n, SLAB_PLACE[n], refill_after(n, (6, 24), FFN_LOOPS) + 24 * i)
            straight(POOL_SLAB - 4, POOL_SLAB + 1)
            sums(FIN1, (f_lo, FT + 1))
            with gp.Fori(0, GROUPS - 1) as i:
                for n in range(POOL_SLAB + 1, POOL_SLAB + 15):
                    split(n + 14 * i, n, SLAB_PLACE[n], refill_after(n, (14, 56), GROUPS - 1) + 56 * i)
            straight(ATT_SLAB - 13, ATT_SLAB + 2)
            sums(KV, first=8)
            straight(ATT_SLAB + 2, ATT_SLAB + 9)
            gp.wait_ge(lo_done, APPLIED_BEFORE[ATT] + 16)
            nc.gpsimd.memset(ident[:, :], 1.0).then_inc(ident_zero, 1)
            gp.wait_ge(ident_zero, 1)
            nc.gpsimd.affine_select(out=ident[:, :], in_=ident[:, :], compare_op=ALU.is_equal, fill=0.0, base=0,
                                    pattern=[[-1, P]], channel_multiplier=1).then_inc(ident_done, 1)
            straight(ATT_SLAB + 9, ATT_SLAB + 13)
            for u in range(32):
                lo = BLOCK if (u % 16) // 2 == 0 else 0
                gp.wait_ge(inv_done, u + 1)
                nc.gpsimd.tensor_tensor(PB[u % 4][:, :, lo:], PB[u % 4][:, :, lo:],
                                        total[:, u % 4, :].unsqueeze(2).to_broadcast([P, 4, 2 * BLOCK - lo]),
                                        ALU.mult).then_inc(normed, 1)
                if u in (8, 16):
                    g = ATT_SLAB + 12 + u // 8
                    straight(g, g + 1)
            gp.wait_ge(mixed, 32)
            straight(ATT_SLAB + 15, NSLAB)
            sums(FIN2, (az_done, 8), last=8)
            for m in range(POOL_FROM, 16):
                gp.wait_ge(stream_gained, m - POOL_FROM + 1)
                gp.wait_ge(rstd_done, 2 * STATS_BEFORE[FIN2] + 2)
                part = X[:, m - 8, hs(1)]
                nc.gpsimd.tensor_tensor(part, part, body(T[2], 1), ALU.mult).then_inc(pool_normed, 1)

        @block.tensor
        def _(pe):
            def products(dst, terms):
                for n, (wh, wl, xh, xl) in enumerate(terms):
                    nc.tensor.matmul(dst, wh, xh, start=n == 0, stop=False)
                    nc.tensor.matmul(dst, wh, xl, start=False, stop=False)
                    last = nc.tensor.matmul(dst, wl, xh, start=False, stop=n == len(terms) - 1)
                return last

            def stat(n, half):
                if n == POOL:
                    pe.wait_ge(sums_joined, half + 1)
                else:
                    pe.wait_ge(sum_done, 14 * SUMS_BEFORE[n] + 7 * half + 7)
                nc.tensor.matmul(bank[(6 if n == FIN1 else 4) + half], ones[:, :], sum_place(n, half), start=True, stop=True
                                 ).then_inc(stat_done, 1)

            def slab_tile(t, place, half, at=None):
                terms = []
                for k in range(KT):
                    cols = slice(P * k, P * k + P)
                    terms.append((WH[place][:, cols], WL[place][:, cols], HH[:, k, hs(half)], HL[:, k, hs(half)]))
                products(bank[t % 4] if at is None else at, terms).then_inc(tiles, 1)

            def freed(j, own, own_base, before):
                if j >= 4:
                    pe.wait_ge(own, own_base + j - 3)
                else:
                    for reader, count in before:
                        pe.wait_ge(reader, count - 3 + j)

            def gated_pair(t, g, norm, before=()):
                pe.wait_ge(slab_ready, g + 2)
                place = SLAB_PLACE[g]
                for half in range(2):
                    for reader, count in before:
                        pe.wait_ge(reader, count - 2 + 2 * half)
                    for k in range(KT):
                        if half == 0 and k == (6 if norm == MIX else 3) and norm != ATT:
                            stat(norm, 1)
                        if half == 0 and norm == POOL and k in (5, 6):
                            stat(FIN1, k - 5)
                        pe.wait_ge(lo_done, APPLIED_BEFORE[norm] + 8 * half + k + 1)
                        cols = slice(P * k, P * k + P)
                        xh, xl = HH[:, k, hs(half)], HL[:, k, hs(half)]
                        for n in range(2):
                            dst, wh, wl = bank[(t + 2 * half + n) % 4], WH[place + n][:, cols], WL[place + n][:, cols]
                            nc.tensor.matmul(dst, wh, xh, start=k == 0, stop=False)
                            nc.tensor.matmul(dst, wh, xl, start=False, stop=False)
                            last = nc.tensor.matmul(dst, wl, xh, start=False, stop=k == KT - 1)
                            if k == KT - 1:
                                last.then_inc(tiles, 1)

            def pair_job(t, g, place, own_base, before, crossed=True, part=range(4)):
                order = [(0, 0), (1, 0), (0, 1), (1, 1)] if crossed else [(0, 0), (0, 1), (1, 0), (1, 1)]
                for j in part:
                    n, half = order[j]
                    if j == 0:
                        pe.wait_ge(slab_ready, g + 1)
                    if n == 1 and order[j - 1][0] == 0 and j < 3:
                        pe.wait_ge(slab_ready, g + 2)
                    freed(j, act_read, own_base, before)
                    slab_tile(t + j, place + n, half)

            def down_job(t, g, place, own_base, before, yh, yl, norm=None, between=None):
                pe.wait_ge(slab_ready, g + 2)
                for j in range(16):
                    half, e = divmod(j, 8)
                    if between:
                        between(j)
                    if norm is not None and j == (13 if norm == POOL else 10):
                        stat(norm, 0)
                    freed(j, dve_read, own_base, before)
                    cols = slice(P * e, P * e + P)
                    products(bank[(t + j) % 4], [(WH[place + r][:, cols], WL[place + r][:, cols],
                                                  yh[:, r, hs(half)], yl[:, r, hs(half)]) for r in range(2)]
                             ).then_inc(tiles, 1)

            pe.wait_ge(setup_done, 1)

            stat(MIX, 0)
            gated_pair(0, 0, MIX)
            for n in range(1, 4):
                pair_job(4 * n, 2 * n, SLAB_PLACE[2 * n], 4 * n, [(act_read, 4 * n)])
            for n in range(6):
                pair_job(16 + 4 * n, 8 + 2 * n, SLAB_PLACE[8 + 2 * n], 16 + 4 * n, [(act_read, 16 + 4 * n)],
                         crossed=False)
            def ln_sums(n, m):
                if (n, m) == (0, 4):
                    pe.wait_ge(conv_done, MT)
                    for half in range(2):
                        for j in range(MT):
                            last = nc.tensor.matmul(bank[4 + half], ones[:, :], body(UB[(j + 4) % 5], half),
                                                    start=j == 0, stop=j == MT - 1)
                        last.then_inc(ln_sum, 1)
                if (n, m) in ((0, 12), (1, 2)):
                    half = n
                    pe.wait_ge(ln_added, 3 * half + 3)
                    nc.tensor.matmul(bank[4 + half], ones[:, :], body(T[2], half), start=True, stop=True
                                     ).then_inc(ln_var, 1)

            def out_between(n, m):
                ln_sums(n, m)
                if m % 8 == 0:
                    pe.wait_ge(my_lo, 4 * n + (4 if n < 2 else 2 + 2 * (m // 8)))

            for n in range(4):
                down_job(OUT_TILE + 16 * n, 20 + 2 * n, SLAB_PLACE[20 + 2 * n], 16 * n,
                         [(dve_read, 16 * n)] if n else [(act_read, 40)], MYH[n % 2], MYL[n % 2],
                         norm=FFN if n == 3 else None, between=lambda m, n=n: out_between(n, m))

            gated_pair(FFN_TILE, FFN_SLAB, FFN, [(dve_read, 64)])

            with pe.Fori(0, FFN_LOOPS) as i:
                t, g, a, d = FFN_TILE + 4 + 24 * i, FFN_SLAB + 2 + 6 * i, 44 + 8 * i, 64 + 16 * i
                at = FFN_SLAB + 2
                pair_job_t = FFN_TILE + 4
                for m in range(2):
                    before = [(act_read, 44), (dve_read, d)] if m == 0 else [(act_read, a + 4)]
                    order = [(0, 0), (1, 0), (0, 1), (1, 1)]
                    for j, (n, half) in enumerate(order):
                        if half == 0:
                            pe.wait_ge(slab_ready, g + 2 * m + n + 1)
                        freed(j, act_read, a + 4 * m, before)
                        slab_tile(pair_job_t + 4 * m + j, SLAB_PLACE[at + 2 * m] + n, half)
                pe.wait_ge(f_lo, 2 * i + 2)
                pe.wait_ge(slab_ready, g + 6)
                for j in range(16):
                    half, e = divmod(j, 8)
                    freed(j, dve_read, d, [(act_read, a + 8)])
                    cols = slice(P * e, P * e + P)
                    place = SLAB_PLACE[at + 4]
                    products(bank[(pair_job_t + j) % 4], [(WH[place + r][:, cols], WL[place + r][:, cols],
                                                           FYH[:, r, hs(half)], FYL[:, r, hs(half)])
                                                          for r in range(2)]).then_inc(tiles, 1)
            t, g = POOL_TILE - 20, POOL_SLAB - 4
            pair_job(t, g, SLAB_PLACE[g], 124, [(dve_read, 224)], crossed=False)

            def last_y(m):
                if m % 8 == 0:
                    pe.wait_ge(f_lo, FT + m // 8)

            down_job(t + 4, g + 2, SLAB_PLACE[g + 2], 224, [(act_read, 128)], FYH, FYL, norm=POOL, between=last_y)

            def pool_turn(i, first_turn=False, last_turn=False):
                g, a, d = POOL_SLAB + 14 * i, 128 + 16 * i, 240 + 40 * i

                def input_slab(n, j, reader, count):
                    pe.wait_ge(slab_ready, g + n + 1)
                    for half in range(2):
                        pe.wait_ge(reader, count + half)
                        slab_tile(j + half, SLAB_PLACE[POOL_SLAB + n], half)

                if first_turn:
                    gated_pair(0, g, POOL, [(dve_read, d)])
                    pe.wait_ge(slab_ready, g + 3)
                    for half in range(2):
                        pe.wait_ge(act_read, a + 1 + 2 * half)
                        slab_tile(4 + half, SLAB_PLACE[POOL_SLAB + 2], half)
                    input_slab(3, 6, act_read, a + 3)
                else:
                    for n in range(4):
                        if n < 2:
                            input_slab(n, 2 * n, dve_read, d - 3 + 2 * n)
                        else:
                            input_slab(n, 2 * n, act_read, a + 2 * n - 3)
                for n in range(2):
                    input_slab(4 + n, 8 + 2 * n, act_read, a + 8 + 2 * n - 3)

                def group_product(j, first, before):
                    place = SLAB_PLACE[POOL_SLAB + 6 + first // 2]
                    for m, (e, half) in enumerate([(0, 0), (1, 0), (0, 1), (1, 1)]):
                        pe.wait_ge(before[0], before[1] - 3 + m)
                        terms = []
                        for k in range(4):
                            cols = slice(256 * k + P * e, 256 * k + P * e + P)
                            terms.append((WH[place][:, cols], WL[place][:, cols], PH[:, k, hs(half)], PL[:, k, hs(half)]))
                        products(bank[(j + m) % 4], terms).then_inc(tiles, 1)

                pe.wait_ge(slab_ready, g + 8)
                pe.wait_ge(p_lo, 4 * i + 4)
                group_product(12, 0, (act_read, a + 12))
                for n in range(2):
                    input_slab(8 + n, 16 + 2 * n, dve_read, d + 4 - 3 + 2 * n)

                def down(n, j, first):
                    pe.wait_ge(slab_ready, g + n + 2)
                    place = SLAB_PLACE[POOL_SLAB + n]
                    for m in range(16):
                        half, e = divmod(m, 8)
                        if e == 0:
                            pe.wait_ge(gy_lo, 8 * i + (0 if first else 4) + 2 * half + 2)
                        if last_turn and not first and m == 10:
                            stat(KV, 0)
                        if first and m < 4:
                            pe.wait_ge(act_read, a + 16 - 3 + m)
                        else:
                            pe.wait_ge(dve_read, d + (4 if first else 24) + m - 3)
                        cols = slice(P * e, P * e + P)
                        products(bank[(j + m) % 4], [(WH[place + r][:, cols], WL[place + r][:, cols],
                                                      GYH[:, r, hs(half)], GYL[:, r, hs(half)])
                                                     for r in range(2)]).then_inc(tiles, 1)

                down(10, 20, True)
                group_product(36, 2, (dve_read, d + 20))
                down(12, 40, False)

            pool_turn(0, first_turn=True)
            with pe.Fori(1, GROUPS - 1) as i:
                pool_turn(i)
            pool_turn(GROUPS - 1, last_turn=True)

            t, g = ATT_TILE, ATT_SLAB
            gated_pair(t, g, KV, [(dve_read, 400)])
            pe.wait_ge(slab_ready, g + 3)
            for half in range(2):
                pe.wait_ge(act_read, 192 + 4 + half - 3)
                slab_tile(t + 4 + half, SLAB_PLACE[g + 2], half)
            def query_pair(n, part=range(4)):
                g = ATT_SLAB + 3 + 2 * n
                pair_job(Q_TILE + 4 * n, g, SLAB_PLACE[g], 198 + 4 * n, [(act_read, 198 + 4 * n)],
                         crossed=False, part=part)

            gated_pair(Q_TILE, ATT_SLAB + 3, ATT, [(act_read, 198)])
            for n in range(1, 3):
                query_pair(n)
            pe.wait_ge(ident_done, 1)
            for b in range(NB):
                last = nc.tensor.transpose(bank[4 + b // 4][:, P * (b % 4):P * (b % 4) + P],
                                           VT[:, P * b:P * b + P], ident[:, :])
                if b % 4 == 3:
                    last.then_inc(v_turned, 1)
            query_pair(3, (0,))
            pe.wait_ge(v_split, 2)

            def first_gate(j):
                pe.wait_ge(slab_ready, ATT_SLAB + 11 + j // 2 + 1)
                pe.wait_ge(biased, 31 + j // 2)
                slab_tile(Z_TILE + j, SLAB_PLACE[ATT_SLAB + 11] + j // 2, j % 2, at=bank[4 + j])

            def quad(u):
                group, rest = divmod(u, 16)
                blk, quarter = divmod(rest, 2)
                return group, blk, 4 * group + 2 * quarter

            def scores(u):
                group, blk, q_tile = quad(u)
                if u >= 2:
                    pe.wait_ge(biased, u - 1)
                lo = BLOCK if blk == 0 else 0
                keys = slice(BLOCK * blk - BLOCK + lo, BLOCK * blk + BLOCK)
                for pos in range(4):
                    rows = slice(HD * (pos // 2), HD * (pos // 2) + HD)
                    dst = bank[4 + 2 * (u % 2) + pos // 2]
                    last = nc.tensor.matmul(dst[:, 256 * (pos % 2) + lo:256 * (pos % 2) + 256],
                                            Q[rows, q_tile + pos % 2, BLOCK * blk:BLOCK * blk + BLOCK],
                                            KD[group][rows, keys], start=True, stop=True)
                last.then_inc(scored, 1)

            def turn(u):
                pe.wait_ge(normed, u + 1)
                for chunk in range(first_chunk(u), 2):
                    if u:
                        pe.wait_ge(turned_split, chunks(u - 1, chunk + 1))
                    for pos in range(4):
                        last = nc.tensor.transpose(bank[chunk][:, P * pos:P * pos + P],
                                                   PB[u % 4][:, pos, BLOCK * chunk:BLOCK * chunk + BLOCK], ident[:, :])
                    last.then_inc(turned, 1)

            def mix_values(u):
                _, blk, _ = quad(u)
                pe.wait_ge(turned_split, chunks(u + 1))
                if u >= 2:
                    pe.wait_ge(o_read, u - 1)
                terms = []
                for chunk in range(1 if blk == 0 else 0, 2):
                    b = blk - 1 + chunk
                    terms.append((V[0][:, b, :], V[1][:, b, :], PT[0][:, chunk, :], PT[1][:, chunk, :]))
                products(bank[2 + u % 2], terms).then_inc(mixed, 1)

            for u in range(32 + 4):
                if u < 32:
                    scores(u)
                else:
                    first_gate(u - 32)
                if u < 3:
                    query_pair(3, (u + 1,))
                if u >= 4:
                    mix_values(u - 4)
                if 3 <= u < 35:
                    if u == 3:
                        pe.wait_ge(act_read, 214)
                    turn(u - 3)

            pe.wait_ge(o_read, 32)
            pe.wait_ge(turned_split, chunks(32))
            t, g, a, d, done = Z_TILE + 4, ATT_SLAB + 13, 218, 400, 0
            before = []
            for is_down in (0, 1, 0, 1, 0):
                if is_down:
                    pe.wait_ge(ay_lo, 2 * done + 2)
                    down_job(t, g, SLAB_PLACE[g], d, before, AYH, AYL)
                    t, d, done, before = t + 16, d + 16, done + 1, [(dve_read, d + 16)]
                else:
                    pair_job(t, g, SLAB_PLACE[g], a, before, crossed=False)
                    t, a, before = t + 4, a + 4, [(act_read, a + 4)]
                g += 2
            for j in range(32):
                half, n, e = j // 16, j // 8 % 2, j % 8
                if j in (0, 8):
                    pe.wait_ge(ay_lo, 6 + 2 * n)
                    pe.wait_ge(slab_ready, g + 2 * n + 2)
                if j == 19:
                    stat(FIN2, 0)
                freed(j, dve_read, d, before)
                place, cols = SLAB_PLACE[g + 2 * n], slice(P * e, P * e + P)
                yh, yl = ((AYH, AYL), (HH, HL))[n]
                products(bank[(t + j) % 4], [(WH[place + r][:, cols], WL[place + r][:, cols],
                                              yh[:, r, hs(half)], yl[:, r, hs(half)]) for r in range(2)]
                         ).then_inc(tiles, 1)
            stat(FIN2, 1)

        @block.scalar
        def _(act):
            loads = [0]

            def square(n, m):
                half, k = divmod(m, 8)
                at = 14 * SUMS_BEFORE[n] + 7 * half
                if k >= 2:
                    act.wait_ge(sum_done, at + k - 2 + (1 if k == 2 else 0))
                elif half == 1:
                    act.wait_ge(sum_done, at + k - 1)
                nc.scalar.activation(squares(n, m), X[:, k, hs(half)], ACT.Square).then_inc(square_done, 1)

            def square_gained(m):
                half, k = divmod(m, 8)
                if k >= 2:
                    act.wait_ge(gained_sum, 7 * half + k - 2 + (1 if k == 2 else 0))
                elif half == 1:
                    act.wait_ge(gained_sum, k + 6)
                nc.scalar.activation(SQ_GAINED[:, hs(m % 2)], X[:, k, hs(half)], ACT.Square, scale=gain(FIN1, k)
                                     ).then_inc(gained_square, 1)

            def load_roots():
                act.wait_ge(setup_done, 1)
                nc.scalar.activation(scrap[:, :], eps[:, 0:1], ACT.Sqrt).then_inc(table_loaded, 1)
                loads[0] += 1
                act.wait_ge(table_loaded, loads[0])

            def mean_root(n, half):
                act.wait_ge(stat_done, 2 * STATS_BEFORE[n] + half + 1)
                dst = sum_place(n, half)
                bias = eps[:, 2:3] if n == POOL else eps[:, 0:1]
                nc.scalar.activation(dst, bank[(6 if n == FIN1 else 4) + half], ACT.Sqrt, bias=bias, scale=1.0 / D
                                     ).then_inc(root_done, 1)

            def hi(n, m):
                half, k = divmod(m, 8)
                act.wait_ge(norm_done, APPLIED_BEFORE[n] + m + 1)
                if shift(n, k) is None:
                    nc.scalar.copy(HH[:, k, hs(half)], piece(n, m)).then_inc(hi_done, 1)
                else:
                    nc.scalar.activation(HH[:, k, hs(half)], piece(n, m), ACT.Identity, bias=shift(n, k)
                                         ).then_inc(hi_done, 1)

            def norm_after_down(n, reads):
                for m in range(16):
                    act.wait_ge(dve_read, reads + m + 1)
                    square(n, m)
                    if m == 2:
                        load_roots()
                    if m == 9:
                        mean_root(n, 0)
                    if m >= 11:
                        hi(n, m - 11)
                hi(n, 5)
                mean_root(n, 1)
                for m in range(6, 16):
                    hi(n, m)

            def read_tile(t, dst, func=ACT.Copy, scale=1.0):
                count, b = t if isinstance(t, tuple) else (t, t % 4)
                act.wait_ge(tiles, count + 1)
                nc.scalar.activation(dst, bank[b], func, scale=scale).then_inc(act_read, 1)

            act.dma_start(rel[:, :], rel_in).then_inc(rel_ready, 16)
            act.dma_start(sinks[:, :], sink_in).then_inc(sink_ready, 16)

            load_roots()
            for m in range(16):
                if m % 2 == 0:
                    act.wait_ge(x_ready[m // 2], 16)
                square(MIX, m)
                if m == 8:
                    mean_root(MIX, 0)
                if m >= 12:
                    hi(MIX, m - 12)
            for m in range(4, 16):
                hi(MIX, m)
                if m == 7:
                    mean_root(MIX, 1)
            act.wait_ge(distance_done, 1)
            act.dma_start(row_scratch, by_distance[:, :]).then_inc(rows_out, 16)
            act.wait_ge(lo_done, 16)
            for j in range(MT):
                for half in range(2):
                    if j:
                        act.wait_ge(glu_done, 2 * (j - 1) + half + 1)
                    read_tile(4 * j + 2 * half, body(T[1], half))
                    read_tile(4 * j + 2 * half + 1, body(T[0], half), ACT.Sigmoid)
            act.wait_ge(rows_out, 16)
            act.dma_start(skew_scratch, row_scratch.unsqueeze(1).to_broadcast([HEADS, P, RLEN])).then_inc(skew_out, 16)
            act.wait_ge(glu_done, 2 * MT)
            for j in range(MT):
                t = 16 + 6 * j
                for half in range(2):
                    if j:
                        act.wait_ge(my_lo, 2 * j)
                    read_tile(t + half, body(T[0], half))
                for half in range(2):
                    if j:
                        act.wait_ge(my_done, 2 * j)
                    read_tile(t + 2 + half, body(T[1], half))
                act.wait_ge(prod_done, 2 * j + 2)
                nc.scalar.activation(body(T[0]), T[2][:, 15:15 + S], ACT.Identity, bias=zero[:, :],
                                     scale=v("conv_a", 3 * j)).then_inc(first_tap, 1)
                for half in range(2):
                    read_tile(t + 4 + half, body(T[1], half))
                for half in range(2):
                    act.wait_ge(my_done, 2 * j + half + 1)
                    nc.scalar.copy(MYH[j // 2][:, j % 2, hs(half)], body(T[0], half)).then_inc(my_hi, 1)
            for half in range(2):
                for j in range(MT):
                    act.wait_ge(ln_centred, MT * half + j + 1)
                    if half == 0:
                        act.wait_ge(my_lo, 8)
                    else:
                        act.wait_ge(ln_added, max(j, 1))
                    nc.scalar.activation(slot(j), body(UB[(j + 4) % 5], half), ACT.Square).then_inc(ln_square, 1)
            for half in range(2):
                act.wait_ge(ln_var, half + 1)
                nc.scalar.activation(body(T[2], half), bank[4 + half], ACT.Sqrt, bias=eps[:, 1:2], scale=1.0 / DM
                                     ).then_inc(ln_root, 1)
            for m, (half, j) in enumerate(LN_ORDER):
                if m % 4 == 0:
                    act.wait_ge(tiles, OUT_TILE + 16 * (1 + j // 2))
                c = body(UB[(j + 4) % 5], half)
                act.wait_ge(ln_scaled, m + 1)
                nc.scalar.activation(c, c, ACT.Silu, bias=v("ln_b", j), scale=v("ln_g", j)).then_inc(ln_silu, 1)
                act.wait_ge(ln_silu, m + 1)
                nc.scalar.copy(MYH[j // 2][:, j % 2, hs(half)], c).then_inc(my_hi, 1)

            norm_after_down(FFN, 48)
            act.wait_ge(tiles, FFN_TILE)
            act.dma_start(ADA[:, 0:ADA_FIRST, :], ada_in[0:ADA_FIRST, :, :].rearrange("s p n -> p s n")
                          ).then_inc(ada_loaded, 16)
            act.dma_start(c_act[:, :], c_in).then_inc(c_loaded, 16)

            def ffn_tile(f, t, b0, free_slot, place, y_free):
                for n, (T_n, half) in enumerate(((0, 0), (1, 0), (0, 1), (1, 1))):
                    if free_slot:
                        act.wait_ge(f_conv if T_n == 0 else f_mul, f)
                    read_tile((t + n, (b0 + n) % 4), body(T[T_n], half))
                act.wait_ge(f_conv, f + 1)
                nc.scalar.activation(body(T[2]), body(T[2]), ACT.Silu).then_inc(f_silu, 1)
                act.wait_ge(tiles, y_free)
                act.wait_ge(f_mul, f + 1)
                nc.scalar.copy(FYH[:, place, :], body(T[2])).then_inc(f_hi, 1)

            act.wait_ge(lo_done, APPLIED_BEFORE[FFN] + 16)
            ffn_tile(0, FFN_TILE, FFN_TILE, False, 0, FFN_TILE)
            act.wait_ge(c_loaded, 16)
            nc.scalar.activation(c_act[:, :], c_act[:, :], ACT.Silu).then_inc(c_ready, 1)
            with act.Fori(0, FFN_LOOPS) as i:
                t = FFN_TILE + 4 + 24 * i
                ffn_tile(2 * i + 1, t, FFN_TILE + 4, True, 1, t)
                act.wait_ge(ada_summed, i + 1)
                act.dma_start(ADA[:, :, :], ada_in[bass.ds(6 * i + ADA_FIRST, 6), :, :].rearrange("s p n -> p s n")
                              ).then_inc(ada_loaded, 16)
                ffn_tile(2 * i + 2, t + 4, FFN_TILE + 8, True, 0, t + 24)
            t = POOL_TILE - 20
            for half in range(2):
                act.wait_ge(f_conv, FT - 1)
                read_tile(t + half, body(T[0], half))
            act.wait_ge(f_conv, FT)
            nc.scalar.activation(body(T[2]), body(T[2]), ACT.Silu).then_inc(f_silu, 1)
            for half in range(2):
                act.wait_ge(f_mul, FT - 1)
                read_tile(t + 2 + half, body(T[1], half))
                act.wait_ge(f_mul, FT + half)
                nc.scalar.copy(FYH[:, 1, hs(half)], body(T[2], half)).then_inc(f_hi, 1)

            for m in range(16):
                act.wait_ge(dve_read, 224 + m + 1)
                square(FIN1, m)
                square_gained(m)
                if m == 2:
                    load_roots()
                if m == 11:
                    mean_root(POOL, 0)
            for m in range(16):
                hi(POOL, m)
                if m == 5:
                    mean_root(POOL, 1)
            for half in range(2):
                mean_root(FIN1, half)
            act.wait_ge(lo_done, APPLIED_BEFORE[POOL] + 16)

            def pool_turn(g, crossed=False):
                t, d = POOL_TILE + 56 * g, 240 + 40 * g
                for n in range(4):
                    for half in range(2):
                        act.wait_ge(p_done, 4 * g + n + 1)
                        at = n + 2 * half if crossed and n < 2 else 2 * n + half
                        read_tile((t + at, at % 4), body(T[0], half))
                    act.wait_ge(tiles, t - 16)
                    act.wait_ge(p_done, 4 * g + n + 2)
                    src = T[1]
                    nc.scalar.copy(PH[:, n, :], body(src)).then_inc(p_hi, 1)
                for n in range(2):
                    act.wait_ge(dve_read, d - 16)
                    for half in range(2):
                        read_tile((t + 8 + 2 * n + half, (2 * n + half) % 4), SZ[:, n, hs(half)], ACT.Silu)

                def y_his(first, base, free):
                    act.wait_ge(tiles, free)
                    for m, (e, half) in enumerate(((0, 0), (1, 0), (0, 1), (1, 1))):
                        act.wait_ge(dve_read, base + m + 1)
                        nc.scalar.copy(GYH[:, e, hs(half)], body(T[1 + e], half)).then_inc(gy_hi, 1)

                y_his(0, d, t)
                for n in range(2):
                    act.wait_ge(dve_read, d + 4)
                    for half in range(2):
                        read_tile((t + 16 + 2 * n + half, (2 * n + half) % 4), SZ[:, n, hs(half)], ACT.Silu)
                y_his(2, d + 20, t + 36)

            pool_turn(0, crossed=True)
            with act.Fori(1, GROUPS) as g:
                pool_turn(g)

            norm_after_down(KV, 384)
            act.wait_ge(tiles, ATT_TILE)
            act.wait_ge(skew_out, 16)

            def load_bias(n):
                act.dma_start(BIAS[:, 4 * (n % 2):4 * (n % 2) + 4, :],
                              bass.AP(skew_scratch.tensor, skew_scratch.offset + 4 * n * RLEN * P + BLOCK - 1,
                                      [[RLEN - 1, P], [RLEN * P, 4], [1, 2 * BLOCK]])).then_inc(bias_ready[n], 16)

            load_bias(0)
            load_bias(1)
            t = ATT_TILE
            for half in range(2):
                for n in range(2):
                    read_tile(t + 2 * half + n, KD[n][:, hs(half)])
            for half in range(2):
                read_tile(t + 4 + half, VT[:, hs(half)])
            for m in range(16):
                if m % 8 == 0:
                    act.wait_ge(tiles, ATT_TILE + 5 + m // 8)
                hi(ATT, m)
            t = Q_TILE
            for n in range(4):
                for j, (e, half) in enumerate([(0, 0), (1, 0), (0, 1), (1, 1)] if n == 0 else
                                              [(0, 0), (0, 1), (1, 0), (1, 1)]):
                    if n < 3:
                        read_tile(t + 4 * n + j, Q[:, 2 * n + e, hs(half)], scale=HD ** -0.5)
            for n in range(2):
                act.wait_ge(v_turned, n + 1)
                nc.scalar.copy(WH[2][:, 512 * n:512 * n + 512], bank[4 + n]).then_inc(v_hi, 1)

            for u in range(32 + 4):
                if u < 4:
                    read_tile(Q_TILE + 12 + u, Q[:, 6 + u // 2, hs(u % 2)], scale=HD ** -0.5)
                if u >= 4:
                    w = u - 4
                    group, rest = divmod(w, 16)
                    blk, quarter = divmod(rest, 2)
                    tile = 4 * group + 2 * quarter
                    act.wait_ge(mixed, w + 1)
                    for side in range(2):
                        rows = slice(HD * side, HD * side + HD)
                        src = bank[2 + w % 2][HD * group:HD * group + HD, 2 * BLOCK * side:2 * BLOCK * side + 2 * BLOCK]
                        ins = nc.scalar.copy(Q[rows, tile:tile + 2, BLOCK * blk:BLOCK * blk + BLOCK],
                                             src.rearrange("p (a b) -> p a b", a=2))
                    ins.then_inc(o_read, 1)
                if 3 <= u < 35:
                    w = u - 3
                    for chunk in range(first_chunk(w), 2):
                        act.wait_ge(turned, chunks(w, chunk + 1))
                        if w:
                            act.wait_ge(mixed, w)
                        nc.scalar.copy(PT[0][:, chunk, :], bank[chunk]).then_inc(turned_hi, 1)
                if u < 32:
                    lo = BLOCK if (u % 16) // 2 == 0 else 0
                    act.wait_ge(gap_done, u + 1)
                    for pos in range(4):
                        nc.scalar.activation(PB[u % 4][:, pos, lo:], PB[u % 4][:, pos, lo:], ACT.Exp,
                                             bias=neg_top[:, u % 4, pos:pos + 1],
                                             accum_out=total[:, u % 4, pos:pos + 1])
                    nc.scalar.activation(sink_exp[:, u % 4, :], sink_gap[:, u % 4, :], ACT.Exp).then_inc(exp_done, 1)
                if u in (14, 15):
                    act.wait_ge(biased, u + 1)
                    load_bias(u - 12)

            act.wait_ge(o_read, 32)
            t, ends = Z_TILE, []
            for n in range(4):
                for e in range(2):
                    if n:
                        act.wait_ge(az_done, 2 * n - 1 + e)
                    for half in range(2):
                        m = 2 * e + half
                        read_tile((t + m, 4 + m if n == 0 else (t + m) % 4), AZ[:, e, hs(half)], ACT.Silu)
                if n:
                    act.wait_ge(tiles, Z_TILE + (48 if n == 3 else 8 + 16 + 20 * (n - 1)))
                for e in range(2):
                    act.wait_ge(az_done, 2 * n + e + 1)
                    nc.scalar.copy((HH if n == 3 else AYH)[:, e, :], Q[:, 2 * n + e, :]).then_inc(ay_hi, 1)
                t += 4 if n == 0 else 20
            act.wait_ge(az_done, 8)
            for m in range(16):
                act.wait_ge(dve_read, 432 + 16 * (m // 8) + 8 + m % 8 + 1)
                square(FIN2, m)
                if m == 2:
                    load_roots()
                if m == 7:
                    mean_root(FIN2, 0)
            act.wait_ge(square_done, 16 * SUMS_BEFORE[FIN2] + 16)
            for m in range(POOL_FROM, 16):
                part = X[:, m - 8, hs(1)]
                nc.scalar.activation(part, part, ACT.Identity, bias=zero[:, :], scale=gain(FIN2, m - 8)
                                     ).then_inc(stream_gained, 1)
            mean_root(FIN2, 1)

        @block.vector
        def _(dve):
            steps = [0]

            def step(ins):
                steps[0] += 1
                ins.then_inc(dve_step, 1)
                dve.wait_ge(dve_step, steps[0])

            def rstd(n, half):
                dve.wait_ge(root_done, 2 * STATS_BEFORE[n] + half + 1)
                dst = sum_place(n, half)
                nc.vector.reciprocal(dst, dst).then_inc(rstd_done, 1)

            def add_square(n, m):
                half, k = divmod(m, 8)
                if k == 0:
                    return
                dst = body(T[2], half)
                dve.wait_ge(square_done, 16 * SUMS_BEFORE[n] + m + 1)
                if k > 1:
                    dve.wait_ge(sum_done, 14 * SUMS_BEFORE[n] + 7 * half + k - 1)
                nc.vector.tensor_tensor(dst, squares(n, m - 1) if k == 1 else dst, squares(n, m), ALU.add
                                        ).then_inc(sum_done, 1)

            def scaled(n, m):
                half, k = divmod(m, 8)
                if k == 0:
                    dve.wait_ge(rstd_done, 2 * STATS_BEFORE[KV if n == ATT else n] + half + 1)
                if n == ATT or m >= 10:
                    dve.wait_ge(lo_done, APPLIED_BEFORE[n] + m - 3)
                elif 2 <= m < 8:
                    dve.wait_ge(lo_done, APPLIED_BEFORE[n] + m - 1)
                nc.vector.scalar_tensor_tensor(piece(n, m), X[:, k, hs(half)], gain(n, k), body(T[2], half),
                                               ALU.mult, ALU.mult).then_inc(norm_done, 1)

            def low(n, m):
                half, k = divmod(m, 8)
                dve.wait_ge(hi_done, APPLIED_BEFORE[n] + m + 1)
                src = piece(n, m)
                if shift(n, k) is None:
                    ins = nc.vector.tensor_tensor(HL[:, k, hs(half)], src, HH[:, k, hs(half)].bitcast(f32), ALU.subtract)
                else:
                    ins = nc.vector.scalar_tensor_tensor(HL[:, k, hs(half)], src, shift(n, k),
                                                         HH[:, k, hs(half)].bitcast(f32), ALU.add, ALU.subtract)
                ins.then_inc(lo_done, 1)

            def apply(n, first=0):
                for m in range(first, 16):
                    if m == 8 and n != ATT:
                        low(n, 7)
                        rstd(n, 1)
                        scaled(n, 8)
                        continue
                    scaled(n, m)
                    if m:
                        low(n, m - 1)
                low(n, 15)

            def apply_early(n, j):
                if 2 <= j <= 8:
                    add_square(n, j - 1)
                if j == 10:
                    rstd(n, 0)
                if j >= 11:
                    scaled(n, j - 11)
                if j >= 12:
                    low(n, j - 12)

            def norm_stream(n, m):
                half, k = divmod(m, 8)
                if k == 0:
                    dve.wait_ge(rstd_done, 2 * STATS_BEFORE[n] + half + 1)
                part = X[:, k, hs(half)]
                r = sum_place(n, half)
                nc.vector.scalar_tensor_tensor(part, part, gain(n, k), r, ALU.mult, ALU.mult).then_inc(stream_normed, 1)

            def add_down(t, b0, d, gate=None, behind=None):
                dve.wait_ge(dve_read, d)
                for j in range(16):
                    half, e = divmod(j, 8)
                    dve.wait_ge(tiles, t + j + 1)
                    part = X[:, e, hs(half)]
                    src = bank[(b0 + j) % 4]
                    if gate is None:
                        ins = nc.vector.tensor_tensor(part, src, part, ALU.add)
                    else:
                        ins = nc.vector.scalar_tensor_tensor(part, src, mods[:, gate + e:gate + e + 1], part,
                                                             ALU.mult, ALU.add)
                    ins.then_inc(dve_read, 1)
                    if behind:
                        behind(j)

            dve.sem_inc(ada_read, 1)
            dve.sem_inc(p_done, 1)
            step(nc.vector.memset(zero[:, :], 0.0))
            nc.vector.memset(ones[:, :], 1.0)
            nc.vector.memset(eps[:, 0:1], 1e-6)
            nc.vector.memset(eps[:, 2:3], 1e-12)
            nc.vector.memset(eps[:, 1:2], 1e-5).then_inc(setup_done, 1)
            for n in range(15):
                nc.vector.memset(inv_count[:, n:n + 1], 1.0 / (n + 1))
            for buf in T:
                nc.vector.memset(buf[:, 0:16], 0.0)
                nc.vector.memset(buf[:, 16 + S:], 0.0)
            for buf in UB:
                nc.vector.memset(buf[:, 0:16], 0.0)
                nc.vector.memset(buf[:, 16 + S:], 0.0)
            step(nc.vector.memset(by_distance[:, :], NEG))
            dve.wait_ge(rel_ready, 16)
            first = 0
            for n in range(1, BLOCK + 1):
                if n == BLOCK or bucket_of(n) != bucket_of(first):
                    b = bucket_of(first)
                    last = nc.vector.tensor_copy(by_distance[:, 2 * BLOCK - n:2 * BLOCK - first],
                                                 rel[:, b:b + 1].to_broadcast([HEADS, n - first]))
                    first = n
            last.then_inc(distance_done, 1)

            for k in range(1, KT):
                add_square(MIX, k)
            rstd(MIX, 0)
            dve.wait_ge(vec_ready, 16)
            apply(MIX)

            def conv_taps(first, last):
                for n in range(first, last):
                    j, tap = divmod(n, TAPS)
                    u, c = UB[j], body(UB[(j + 4) % 5])
                    w = v("conv_b", TAPS * j + tap)
                    window = u[:, 1 + tap:1 + tap + S]
                    if tap == 0:
                        dve.wait_ge(glu_done, 2 * j + 2)
                        if j:
                            dve.wait_ge(conv_done, j)
                        step(nc.vector.tensor_scalar(c, window, w, v("conv_b_b", j), ALU.mult, ALU.add))
                    else:
                        ins = nc.vector.scalar_tensor_tensor(c, window, w, c, ALU.mult, ALU.add)
                        if tap == TAPS - 1:
                            ins.then_inc(conv_done, 1)
                        else:
                            step(ins)

            UNIT_TAPS = 15
            for j in range(MT):
                for half in range(2):
                    dve.wait_ge(act_read, 4 * j + 2 * half + 2)
                    nc.vector.tensor_tensor(body(UB[j], half), body(T[1], half), body(T[0], half), ALU.mult
                                            ).then_inc(glu_done, 1)
                conv_taps(UNIT_TAPS * j, UNIT_TAPS * j + UNIT_TAPS)
            rest = MT * TAPS - MT * UNIT_TAPS
            turns = [MT * UNIT_TAPS + rest * n // (3 * MT) for n in range(3 * MT + 1)]
            for j in range(MT):
                conv_taps(*turns[3 * j:3 * j + 2])
                conv_taps(*turns[3 * j + 1:3 * j + 3])
                dve.wait_ge(first_tap, j + 1)
                step(nc.vector.scalar_tensor_tensor(body(T[0]), T[2][:, 16:16 + S], v("conv_a", 3 * j + 1), body(T[0]),
                                                    ALU.mult, ALU.add))
                step(nc.vector.scalar_tensor_tensor(body(T[0]), T[2][:, 17:17 + S], v("conv_a", 3 * j + 2), body(T[0]),
                                                    ALU.mult, ALU.add))
                if j == MT - 1:
                    conv_taps(*turns[3 * j + 2:3 * j + 4])
                for half in range(2):
                    dve.wait_ge(act_read, 16 + 6 * j + 5 + half)
                    y = body(T[0], half)
                    nc.vector.tensor_tensor(y, y, body(T[1], half), ALU.mult).then_inc(my_done, 1)
                if j < MT - 1:
                    conv_taps(*turns[3 * j + 2:3 * j + 4])
            for n in range(8):
                dve.wait_ge(x_ready[n], 16)

            def add_out(n, behind=None):
                if n:
                    dve.wait_ge(dve_read, 16 * n)
                for m in range(16):
                    half, e = divmod(m, 8)
                    dve.wait_ge(tiles, OUT_TILE + 16 * n + m + 1)
                    part = X[:, e, hs(half)]
                    nc.vector.tensor_tensor(part, bank[(OUT_TILE + m) % 4], part, ALU.add).then_inc(dve_read, 1)
                    if behind:
                        behind(m)

            def centre(m):
                half, j = divmod(m, MT)
                dve.wait_ge(ln_sum, half + 1)
                c = body(UB[(j + 4) % 5], half)
                nc.vector.scalar_tensor_tensor(c, bank[4 + half], -1.0 / DM, c, ALU.mult, ALU.add).then_inc(ln_centred, 1)

            def ln_rstds(half):
                dve.wait_ge(ln_root, half + 1)
                nc.vector.reciprocal(body(T[2], half), body(T[2], half)).then_inc(ln_rstd, 1)

            def ln_scale(m):
                half, j = LN_ORDER[m]
                dve.wait_ge(ln_rstd, half + 1)
                dve.wait_ge(ln_centred, 2 * MT)
                c = body(UB[(j + 4) % 5], half)
                nc.vector.tensor_tensor(c, c, body(T[2], half), ALU.mult).then_inc(ln_scaled, 1)

            def ln_low(m):
                half, j = LN_ORDER[m]
                dve.wait_ge(my_hi, 8 + m + 1)
                nc.vector.tensor_tensor(MYL[j // 2][:, j % 2, hs(half)], body(UB[(j + 4) % 5], half),
                                        MYH[j // 2][:, j % 2, hs(half)].bitcast(f32), ALU.subtract).then_inc(my_lo, 1)

            def behind_first(m):
                if 4 <= m < 12:
                    centre(m - 4)

            def behind_second(m):
                if m == 1:
                    ln_rstds(0)
                elif m == 2:
                    ln_scale(0)
                    ln_scale(1)
                elif m == 4:
                    ln_rstds(1)
                elif m in (6, 7):
                    ln_low(m - 6)
                elif m in (8, 9):
                    ln_scale(m - 6)
                elif m in (11, 12):
                    ln_low(m - 9)
                elif m > 12:
                    ln_scale(m - 9)

            add_out(0, behind_first)
            add_out(1, behind_second)
            ln_scale(7)
            for m in range(4, 8):
                ln_low(m)
            add_out(2)
            dve.wait_ge(ln_scaled, 2 * MT)
            add_out(3, lambda m: apply_early(FFN, m))

            apply(FFN, 5)

            def ffn_conv(f, a, first_step, taps, free=True, last=False):
                if free:
                    dve.wait_ge(f_lo, f)
                dve.wait_ge(act_read, a + (2 if last else 3))
                ins = nc.vector.tensor_scalar(body(T[2]), T[0][:, 15:15 + S], taps(0), None, ALU.mult)
                ins.then_inc(dve_step, 1)
                dve.wait_ge(dve_step, first_step + 1)
                ins = nc.vector.scalar_tensor_tensor(body(T[2]), T[0][:, 16:16 + S], taps(1), body(T[2]), ALU.mult, ALU.add)
                ins.then_inc(dve_step, 1)
                dve.wait_ge(dve_step, first_step + 2)
                nc.vector.scalar_tensor_tensor(body(T[2]), T[0][:, 17:17 + S], taps(2), body(T[2]), ALU.mult, ALU.add
                                               ).then_inc(f_conv, 1)
                dve.wait_ge(f_silu, f + 1)
                if last:
                    return
                dve.wait_ge(act_read, a + 4)
                nc.vector.tensor_tensor(body(T[2]), body(T[2]), body(T[1]), ALU.mult).then_inc(f_mul, 1)

            def ffn_lo(f, place):
                dve.wait_ge(f_hi, f + 1)
                nc.vector.tensor_tensor(FYL[:, place, :], body(T[2]), FYH[:, place, :].bitcast(f32), ALU.subtract
                                        ).then_inc(f_lo, 1)

            def ffn_w(f):
                return lambda n: v("conv_ffn", 3 * f + n)

            def ada_products(turn, at, count):
                dve.wait_ge(ada_loaded, 16 * turn + 16)
                dve.wait_ge(ada_read, turn + 1)
                for n in range(count):
                    ins = nc.vector.tensor_tensor_reduce(out=ADA[:, n, :], in0=ADA[:, n, :], in1=c_act[:, :], scale=1.0,
                                                         scalar=0.0, op0=ALU.mult, op1=ALU.add,
                                                         accum_out=ada_sum[:, n:n + 1])
                ins.then_inc(ada_summed, 1)
                dve.wait_ge(ada_summed, turn + 1)
                nc.vector.tensor_tensor(mods[:, bass.ds(at, count)], ada_sum[:, 0:count],
                                        vec[:, bass.ds(VEC["ada_b"] + at, count)], ALU.add).then_inc(ada_read, 1)

            ffn_conv(0, 40, steps[0], ffn_w(0), False)
            ffn_lo(0, 0)
            dve.wait_ge(c_ready, 1)
            ada_products(0, 0, ADA_FIRST)
            base = steps[0] + 2
            with dve.Fori(0, FFN_LOOPS) as i:
                a = 44 + 8 * i

                def loop_w(odd):
                    return lambda n: vec[:, bass.ds(VEC["conv_ffn"] + 3 + 3 * odd + n + 6 * i, 1)]

                ffn_conv(2 * i + 1, a, base + 4 * i, loop_w(0))
                ffn_lo(2 * i + 1, 1)
                ffn_conv(2 * i + 2, a + 4, base + 4 * i + 2, loop_w(1))
                add_down(FFN_TILE + 12 + 24 * i, FFN_TILE, 64 + 16 * i)
                ffn_lo(2 * i + 2, 0)
                ada_products(i + 1, 6 * i + ADA_FIRST, 6)
            steps[0] = base + 4 * FFN_LOOPS
            dve.wait_ge(ada_read, FFN_LOOPS + 2)
            for at, scale, base_col in ((0, SCALE0, VEC["norm2_g"]), (KT, SCALEKV, VEC["kv_g"]),
                                        (2 * KT, SCALE1, VEC["norm2_g"] + KT)):
                nc.vector.scalar_tensor_tensor(gains[:, at:at + KT], mods[:, scale:scale + KT], 1.0,
                                               vec[:, base_col:base_col + KT], ALU.add, ALU.mult).then_inc(gains_done, 1)
            dve.wait_ge(gains_done, 3)
            nc.vector.tensor_tensor(gains[:, 0:KT], gains[:, 0:KT], vec[:, VEC["fin1_g"]:VEC["fin1_g"] + KT], ALU.mult
                                    ).then_inc(gains_done, 1)
            dve.wait_ge(gains_done, 4)
            ffn_conv(FT - 1, 124, steps[0], ffn_w(FT - 1), last=True)
            steps[0] += 2
            for half in range(2):
                y = body(T[2], half)
                dve.wait_ge(act_read, 126 + half + 1)
                nc.vector.tensor_tensor(y, y, body(T[1], half), ALU.mult).then_inc(f_mul, 1)
                dve.wait_ge(f_hi, FT + half)
                nc.vector.tensor_tensor(FYL[:, 1, hs(half)], y, FYH[:, 1, hs(half)].bitcast(f32), ALU.subtract
                                        ).then_inc(f_lo, 1)
            dve.wait_ge(f_lo, FT + 1)

            def add_gained(m):
                half, k = divmod(m, 8)
                dst = body(T[2], half)
                if k:
                    dve.wait_ge(gained_square, m + 1)
                    if k > 1:
                        dve.wait_ge(gained_sum, 7 * half + k - 1)
                    nc.vector.tensor_tensor(dst, SQ_GAINED[:, hs(0)] if k == 1 else dst, SQ_GAINED[:, hs(m % 2)], ALU.add
                                            ).then_inc(gained_sum, 1)

            def join_sums(half):
                dve.wait_ge(gained_sum, 7 * half + 7)
                dve.wait_ge(sum_done, 14 * SUMS_BEFORE[FIN1] + 7 * half + 7)
                nc.vector.scalar_tensor_tensor(body(T[2], half), SUM_PLAIN[:, hs(half)], 1e-6, body(T[2], half),
                                               ALU.mult, ALU.add).then_inc(sums_joined, 1)

            def behind_last(j):
                if j >= 2:
                    add_gained(j - 2)
                if j == 10:
                    join_sums(0)
                if j == 14:
                    rstd(POOL, 0)

            add_down(POOL_TILE - 16, POOL_TILE, 224, behind=behind_last)

            scaled(POOL, 0)
            add_gained(14)
            scaled(POOL, 1)
            low(POOL, 0)
            add_gained(15)
            join_sums(1)
            apply(POOL, 2)
            for g in range(GROUPS):
                w = POOL_WINDOWS[g]
                t, a, d = POOL_TILE + 56 * g, 128 + 16 * g, 240 + 40 * g
                for n in range(4):
                    dve.wait_ge(act_read, a + 2 * n + 2)
                    if n:
                        dve.wait_ge(p_lo, 4 * g + n)
                    elif g:
                        dve.wait_ge(gy_lo, 8 * g)
                    order = [1, 2, 1, 2] if g % 2 else [2, 1, 2]
                    src, width = 0, 1
                    for m in range(g + 1):
                        dst = order[m]
                        step(nc.vector.tensor_tensor(body(T[dst]), body(T[src]), T[src][:, 16 - width:16 - width + S],
                                                     ALU.add))
                        src, width = dst, 2 * width
                    edge = w - 1
                    step(nc.vector.scalar_tensor_tensor(T[1][:, 16:16 + S], T[src][:, 16:16 + S], 1.0 / w,
                                                        T[0][:, 16:16 + S], ALU.mult, ALU.subtract))
                    step(nc.vector.tensor_tensor(T[1][:, 16:16 + edge], T[src][:, 16:16 + edge], inv_count[:, 0:edge],
                                                 ALU.mult))
                    nc.vector.tensor_tensor(T[1][:, 16:16 + edge], T[1][:, 16:16 + edge], T[0][:, 16:16 + edge],
                                            ALU.subtract).then_inc(p_done, 1)
                    dve.wait_ge(p_hi, 4 * g + n + 1)
                    nc.vector.tensor_tensor(PL[:, n, :], body(T[1]), PH[:, n, :].bitcast(f32), ALU.subtract
                                            ).then_inc(p_lo, 1)
                    if g == 0 and n < 2:
                        rstd(FIN1, n)
                    elif g == 0:
                        for m in range(8 * (n - 2), 8 * (n - 2) + 8):
                            norm_stream(FIN1, m)

                def group_y(first, t0, gates_read, d0):
                    for half in range(2):
                        for e in range(2):
                            m = 2 * half + e
                            dve.wait_ge(tiles, t0 + m + 1)
                            dve.wait_ge(act_read, gates_read)
                            nc.vector.scalar_tensor_tensor(body(T[1 + e], half), bank[m], v("a_scale", 4 * g + first + e),
                                                           SZ[:, e, hs(half)], ALU.mult, ALU.mult).then_inc(dve_read, 1)
                        for e in range(2):
                            m = 2 * half + e
                            dve.wait_ge(gy_hi, 8 * g + 2 * first + m + 1)
                            nc.vector.tensor_tensor(GYL[:, e, hs(half)], body(T[1 + e], half),
                                                    GYH[:, e, hs(half)].bitcast(f32), ALU.subtract).then_inc(gy_lo, 1)

                group_y(0, t + 12, a + 12, d)
                if g == 0:
                    dve.wait_ge(stream_normed, 16)
                add_down(t + 20, 0, d + 4, GATE0)
                group_y(2, t + 36, a + 16, d + 20)
                if g == GROUPS - 1:
                    dve.wait_ge(gy_lo, 8 * GROUPS)
                add_down(t + 40, 0, d + 24, GATE0,
                         behind=(lambda j: apply_early(KV, j)) if g == GROUPS - 1 else None)

            apply(KV, 5)
            apply(ATT)

            for n in range(2):
                dve.wait_ge(v_hi, n + 1)
                cols = slice(512 * n, 512 * n + 512)
                nc.vector.tensor_tensor(WL[2][:, cols], bank[4 + n], WH[2][:, cols].bitcast(f32), ALU.subtract
                                        ).then_inc(v_split, 1)
            dve.wait_ge(sink_ready, 16)

            def soften(u):
                group, rest = divmod(u, 16)
                blk, quarter = divmod(rest, 2)
                r, lo = u % 4, BLOCK if blk == 0 else 0
                if rest < 2:
                    dve.wait_ge(bias_ready[2 * group + quarter], 16)
                dve.wait_ge(scored, u + 1)
                if u >= 4:
                    dve.wait_ge(turned, chunks(u - 3))
                scores = psum[:, 4 + 2 * (u % 2):6 + 2 * (u % 2), :].rearrange("p a (b c) -> p (a b) c", b=2)
                nc.vector.tensor_tensor(PB[r][:, :, lo:], scores[:, :, lo:], BIAS[:, 4 * quarter:4 * quarter + 4, lo:],
                                        ALU.add).then_inc(biased, 1)
                dve.wait_ge(biased, u + 1)
                step(nc.vector.tensor_reduce(top[:, r, :], PB[r][:, :, lo:], AX.X, ALU.max))
                sink = sinks[:, 8 * group + 4 * quarter:8 * group + 4 * quarter + 4]
                step(nc.vector.tensor_tensor(top[:, r, :], top[:, r, :], sink, ALU.max))
                nc.vector.tensor_scalar(neg_top[:, r, :], top[:, r, :], -1.0, None, ALU.mult)
                nc.vector.tensor_tensor(sink_gap[:, r, :], sink, top[:, r, :], ALU.subtract).then_inc(gap_done, 1)

            for u in range(32 + 3):
                if u < 32:
                    soften(u)
                if 1 <= u < 33:
                    r = (u - 1) % 4
                    dve.wait_ge(exp_done, u)
                    step(nc.vector.tensor_tensor(total[:, r, :], total[:, r, :], sink_exp[:, r, :], ALU.add))
                    nc.vector.reciprocal(total[:, r, :], total[:, r, :]).then_inc(inv_done, 1)
                if u >= 3:
                    w = u - 3
                    for chunk in range(first_chunk(w), 2):
                        dve.wait_ge(turned_hi, chunks(w, chunk + 1))
                        nc.vector.tensor_tensor(PT[1][:, chunk, :], bank[chunk], PT[0][:, chunk, :].bitcast(f32),
                                                ALU.subtract).then_inc(turned_split, 1)

            dve.wait_ge(o_read, 32)
            t, d = Z_TILE, 400

            def gated(n):
                for e in range(2):
                    dve.wait_ge(act_read, 214 + 4 * n + 2 * e + 2)
                    nc.vector.tensor_tensor(Q[:, 2 * n + e, :], Q[:, 2 * n + e, :], AZ[:, e, :], ALU.mult).then_inc(az_done, 1)

            def gated_lo(n):
                for e in range(2):
                    dve.wait_ge(ay_hi, 2 * n + e + 1)
                    yh, yl = (HH, HL) if n == 3 else (AYH, AYL)
                    nc.vector.tensor_tensor(yl[:, e, :], Q[:, 2 * n + e, :], yh[:, e, :].bitcast(f32), ALU.subtract
                                            ).then_inc(ay_lo, 1)

            gated(0)
            gated_lo(0)
            for n in range(1, 3):
                gated(n)
                first = Z_TILE + 8 + 20 * (n - 1)
                add_down(first, first, 400 + 16 * (n - 1), GATE1)
                gated_lo(n)
            gated(3)
            gated_lo(3)
            first = Z_TILE + 48
            for j in range(32):
                half, e = j // 16, j % 8
                if j % 8 == 0:
                    dve.wait_ge(dve_read, 432 + j)
                dve.wait_ge(tiles, first + j + 1)
                part = X[:, e, hs(half)]
                nc.vector.scalar_tensor_tensor(part, bank[(first + j) % 4], mods[:, GATE1 + e:GATE1 + e + 1], part,
                                               ALU.mult, ALU.add).then_inc(dve_read, 1)
                if j == 19:
                    rstd(FIN2, 0)
                if 20 <= j < 24:
                    norm_stream(FIN2, j - 20)
                if j > 24:
                    add_square(FIN2, j - 17)
            add_square(FIN2, 15)
            for m in range(4, 8):
                norm_stream(FIN2, m)
            rstd(FIN2, 1)
            for m in range(8, POOL_FROM):
                norm_stream(FIN2, m)


def kernel(x, norm_mix_g, w_in, conv_a_w, conv_b_w, conv_b_b, ln_b_g, ln_b_b, w_out, norm_ffn_g, w_gate, w_up,
           conv_ffn_w, w_down, norm_final_g, c_2, norm_g_2, ada_w_2, ada_b_2, a_w_in_2, a_w_group_2, a_scale_2,
           a_w_out_2, kv_norm_g_2, kv_ada_w_2, kv_ada_b_2, w_kv_2, b_w_in_2, b_sinks_2, b_w_out_2, rel_bias_2,
           final_g_2):
    import numpy as np
    import concourse.bacc as bacc
    from concourse.bass_utils import run_bass_kernel_spmd as run

    def columns(a):
        return np.asarray(a).reshape(-1, P).T

    def taps(w):
        w = np.asarray(w)
        return w.reshape(w.shape[0], -1, P).transpose(2, 1, 0).reshape(P, -1)

    def column_slab(w, e):
        return w[:, P * e:P * e + P].reshape(KT, P, P).transpose(1, 0, 2).reshape(P, 1024)

    def row_slab(w, r):
        return w[P * r:P * r + P, :]

    x = np.asarray(x)
    w_in, w_out, w_gate, w_up, w_down = (np.asarray(a)[0] for a in (w_in, w_out, w_gate, w_up, w_down))
    a_in, a_group, a_out = np.asarray(a_w_in_2)[0], np.asarray(a_w_group_2)[0], np.asarray(a_w_out_2)[0]
    w_kv, b_in, b_out = np.asarray(w_kv_2), np.asarray(b_w_in_2)[0], np.asarray(b_w_out_2)[0]
    slabs = []
    for j in range(MT):
        slabs += [column_slab(w_in, 12 + j), column_slab(w_in, 16 + j)]
    for j in range(MT):
        slabs += [column_slab(w_in, 8 + j), column_slab(w_in, j), column_slab(w_in, 4 + j)]
    slabs += [row_slab(w_out, r) for r in range(KT)]
    for f in range(FT):
        slabs += [column_slab(w_gate, f), column_slab(w_up, f)]
        if f and f % 2 == 0:
            slabs += [row_slab(w_down, f - 2), row_slab(w_down, f - 1)]
    slabs += [row_slab(w_down, FT - 2), row_slab(w_down, FT - 1)]
    for g in range(GROUPS):
        slabs += [column_slab(a_in, 4 * g + n) for n in range(4)]
        slabs += [column_slab(a_in, 16 + 4 * g + n) for n in range(2)]
        slabs += [a_group[g][:, 256 * n:256 * n + 256].reshape(4, P, 256).transpose(1, 0, 2).reshape(P, 1024)
                  for n in range(2)]
        slabs += [column_slab(a_in, 16 + 4 * g + n) for n in range(2, 4)]
        slabs += [row_slab(a_out, 4 * g + n) for n in range(4)]
    for g in range(2):
        k = w_kv[:, HD * g:HD * g + HD]
        slabs.append(column_slab(np.concatenate([k, k], axis=1), 0))
    slabs.append(column_slab(w_kv, 1))
    slabs += [column_slab(b_in, n) for n in range(KT)]
    z = [[column_slab(b_in, 8 + 2 * n), column_slab(b_in, 9 + 2 * n)] for n in range(4)]
    o = [[row_slab(b_out, 2 * n), row_slab(b_out, 2 * n + 1)] for n in range(4)]
    slabs += z[0] + z[1] + o[0] + z[2] + o[1] + z[3] + o[2] + o[3]
    slabs = np.stack(slabs)
    assert len(slabs) == NSLAB

    ada_w, kv_ada = np.asarray(ada_w_2), np.asarray(kv_ada_w_2)
    ada = np.stack([w[:, P * e:P * e + P].T for w in (ada_w[0], ada_w[1], kv_ada) for e in range(w.shape[1] // P)])
    vec = np.concatenate([columns(norm_mix_g), taps(np.asarray(conv_a_w)[0]), taps(np.asarray(conv_b_w)[0]),
                          columns(conv_b_b), columns(ln_b_g), columns(ln_b_b), columns(norm_ffn_g),
                          taps(np.asarray(conv_ffn_w)[0]), columns(norm_final_g), columns(norm_g_2),
                          columns(ada_b_2), columns(kv_ada_b_2), columns(a_scale_2), columns(kv_norm_g_2),
                          columns(final_g_2)], axis=1)
    assert vec.shape[1] == NVEC
    arrays = {
        "x": x[0].T.reshape(KT, P, S).transpose(1, 0, 2),
        "vec": vec,
        "slabs": slabs,
        "ada": ada,
        "c": np.broadcast_to(np.asarray(c_2)[0], (P, D)),
        "rel": np.asarray(rel_bias_2).T[HEAD_ORDER],
        "sinks": np.broadcast_to(np.asarray(b_sinks_2)[0][HEAD_ORDER], (P, HEADS)),
    }
    arrays = {n: np.ascontiguousarray(a) for n, a in arrays.items()}
    nc = bacc.Bacc("TRN2", target_bir_lowering=False, num_devices=1, dynamic_dma_scratch_size=16)
    f32 = mybir.dt.float32
    arrays = {f"in_{n}": a for n, a in arrays.items()}
    aps = [nc.dram_tensor(n, a.shape, f32, kind="ExternalInput").ap() for n, a in arrays.items()]
    row_scratch = nc.dram_tensor("row_scratch", (HEADS, RLEN), f32, kind="Internal").ap()
    skew_scratch = nc.dram_tensor("skew_scratch", (HEADS, P, RLEN), f32, kind="Internal").ap()
    out = nc.dram_tensor("out", (P, KT, S), f32, kind="ExternalOutput").ap()
    build(nc, *aps, row_scratch, skew_scratch, out)
    r = run(nc, [arrays], core_ids=[0])
    return r.results[0]["out"].transpose(1, 0, 2).reshape(D, S).T[None]
```
